# Optimizing a Trainium2 kernel written in Bass

```python
import jax, jax.numpy as jnp
from jax import lax
import numpy as np

D_MODEL = 2048
BATCH = 1
SEQ = 256
DEPTH = 2
DEC_BATCH = 8
DEC_SEQ = 4
PAST_LEN = 1024
PAGE_SIZE = 128

HEAD_DIM = 128
ROPE_DIMS = HEAD_DIM // 4
ROPE_THETA = 500000.0
NORM_EPS = 1e-6
Q_BLOCK = 128
H_RET = 8
RET_CHUNK = 128
RET_THETA = 10000.0
H_DIL = 8
DIL_PATTERNS = ((128, 1), (512, 4), (2048, 16))
DIL_WMAX = 2048
H_NSA = 8
G_NSA = 2
NSA_BLOCK = 64
NSA_TOPK = 16
NSA_WINDOW = 512
D_RNN = 1024
RNN_BLOCKS = 8
CONV_W = 4
LRU_C = 8.0
N_MEM = 256
H_MEM = 4
D_FF = 4 * D_MODEL
N_EVEN = (DEPTH + 1) // 2
N_ODD = DEPTH // 2

kernel_name = "hybrid_retention_dilated_nsa_rglru_step"

def _offsets(sizes):
    return [int(v) for v in np.cumsum(sizes)[:-1]]

def rmsnorm(x, g):
    xf = x.astype(jnp.float32)
    y = xf * lax.rsqrt(jnp.mean(xf * xf, axis=-1, keepdims=True) + NORM_EPS)
    return (y * g.astype(jnp.float32)).astype(x.dtype)

def rope(x, pos, n_rot, theta):
    half = n_rot // 2
    inv = 1.0 / (theta ** (jnp.arange(half, dtype=jnp.float32) * (2.0 / n_rot)))
    ang = pos.astype(jnp.float32)[:, None] * inv[None, :]
    cos = jnp.cos(ang)[:, None, :]
    sin = jnp.sin(ang)[:, None, :]
    xr = x[..., :n_rot].astype(jnp.float32)
    x1, x2 = xr[..., :half], xr[..., half:]
    rot = jnp.concatenate([x1 * cos - x2 * sin, x2 * cos + x1 * sin], axis=-1)
    return jnp.concatenate([rot.astype(x.dtype), x[..., n_rot:]], axis=-1)

def masked_softmax(s, mask):
    s = jnp.where(mask, s, -jnp.inf)
    m = jnp.max(s, axis=-1, keepdims=True)
    m = jnp.where(jnp.isfinite(m), m, 0.0)
    p = jnp.exp(s - m)
    l = jnp.sum(p, axis=-1, keepdims=True)
    return p / jnp.maximum(l, 1e-30), m, l

def ret_log_decay():
    return jnp.log1p(-jnp.exp2(-5.0 - jnp.arange(H_RET, dtype=jnp.float32)))

def retention_chunk(s_prev, q, k, v, log_g):
    c = q.shape[2]
    i = jnp.arange(c, dtype=jnp.float32)
    diff = i[:, None] - i[None, :]
    decay = jnp.where(diff >= 0, jnp.exp(jnp.maximum(diff, 0.0)[None] * log_g[:, None, None]), 0.0)
    inner = jnp.einsum('nhid,nhjd->nhij', q, k) * decay
    q_decay = jnp.exp((i[None, :] + 1.0) * log_g[:, None])[None, :, :, None]
    k_decay = jnp.exp((c - 1.0 - i[None, :]) * log_g[:, None])[None, :, :, None]
    o = jnp.einsum('nhij,nhjv->nhiv', inner, v) + jnp.einsum('nhid,nhdv->nhiv', q, s_prev) * q_decay
    s_new = jnp.exp(c * log_g)[None, :, None, None] * s_prev + jnp.einsum('nhjd,nhjv->nhdv', k * k_decay, v)
    return s_new, o

def dilated_attention(q, kx, vx, q_idx):
    outs, lses = [], []
    for window, dil in DIL_PATTERNS:
        offs = jnp.arange(window // dil + 1, dtype=jnp.int32) * dil
        idx = q_idx[:, None] - offs[None, :]
        valid = idx >= 0
        idx = jnp.maximum(idx, 0)
        kg = kx[:, idx]
        vg = vx[:, idx]
        s = jnp.einsum('nthd,ntkhd->nthk', q, kg).astype(jnp.float32)
        p, m, l = masked_softmax(s, valid[None, :, None, :])
        outs.append(jnp.einsum('nthk,ntkhd->nthd', p, vg).astype(jnp.float32))
        lses.append((m + jnp.log(l))[..., 0])
    w = jax.nn.softmax(jnp.stack(lses), axis=0)
    return jnp.einsum('pnth,pnthd->nthd', w, jnp.stack(outs))

def even_project(xn, pos, w_in, dq_g, dk_g):
    n, t, _ = xn.shape
    sizes = [H_RET * HEAD_DIM] * 4 + [H_DIL * HEAD_DIM] * 3
    rq, rk, rv, rg, dq, dk, dv = jnp.split(xn @ w_in, _offsets(sizes), axis=-1)
    heads = lambda a, h: a.reshape(n, t, h, HEAD_DIM)
    scale = HEAD_DIM ** -0.5
    rq = rope(heads(rq, H_RET), pos, HEAD_DIM, RET_THETA) * scale
    rk = rope(heads(rk, H_RET), pos, HEAD_DIM, RET_THETA)
    dq = rope(rmsnorm(heads(dq, H_DIL), dq_g), pos, ROPE_DIMS, ROPE_THETA) * scale
    dk = rope(rmsnorm(heads(dk, H_DIL), dk_g), pos, ROPE_DIMS, ROPE_THETA)
    return rq, rk, heads(rv, H_RET), rg, dq, dk, heads(dv, H_DIL)

def even_output(ret_o, rg, dil_o, gn_g, w_out):
    n, t = rg.shape[:2]
    mu = jnp.mean(ret_o, axis=-1, keepdims=True)
    var = jnp.mean(jnp.square(ret_o - mu), axis=-1, keepdims=True)
    y = (ret_o - mu) * lax.rsqrt(var + NORM_EPS) * gn_g.astype(jnp.float32)
    y = y.reshape(n, t, -1) * jax.nn.silu(rg.astype(jnp.float32))
    cat = jnp.concatenate([y, dil_o.reshape(n, t, -1).astype(jnp.float32)], axis=-1)
    return cat.astype(w_out.dtype) @ w_out

def even_mixer_prompt(xn, pos, w_in, gn_g, dq_g, dk_g, w_out):
    n, t, _ = xn.shape
    rq, rk, rv, rg, dq, dk, dv = even_project(xn, pos, w_in, dq_g, dk_g)
    nc = t // RET_CHUNK
    def to_chunks(a):
        return a.astype(jnp.float32).reshape(n, nc, RET_CHUNK, H_RET, HEAD_DIM).transpose(1, 0, 3, 2, 4)
    log_g = ret_log_decay()
    s0 = jnp.zeros((n, H_RET, HEAD_DIM, HEAD_DIM), jnp.float32)
    s_fin, oc = lax.scan(lambda s, c: retention_chunk(s, c[0], c[1], c[2], log_g), s0,
                         (to_chunks(rq), to_chunks(rk), to_chunks(rv)))
    ret_o = oc.transpose(1, 0, 3, 2, 4).reshape(n, t, H_RET, HEAD_DIM)
    nqb = t // Q_BLOCK
    qb = dq.reshape(n, nqb, Q_BLOCK, H_DIL, HEAD_DIM).swapaxes(0, 1)
    ib = jnp.arange(t, dtype=jnp.int32).reshape(nqb, Q_BLOCK)
    ob = lax.map(lambda a: dilated_attention(a[0], dk, dv, a[1]), (qb, ib))
    dil_o = ob.swapaxes(0, 1).reshape(n, t, H_DIL, HEAD_DIM)
    y = even_output(ret_o, rg, dil_o, gn_g, w_out)
    keep = min(DIL_WMAX, t)
    return y, s_fin, dk[:, t - keep:], dv[:, t - keep:]

def even_mixer_sample(xn, pos, s_past, buf_k, buf_v, w_in, gn_g, dq_g, dk_g, w_out):
    n, t, _ = xn.shape
    rq, rk, rv, rg, dq, dk, dv = even_project(xn, pos, w_in, dq_g, dk_g)
    hf = lambda a: a.astype(jnp.float32).transpose(0, 2, 1, 3)
    s_new, o = retention_chunk(s_past.astype(jnp.float32), hf(rq), hf(rk), hf(rv), ret_log_decay())
    ret_o = o.transpose(0, 2, 1, 3)
    kx = jnp.concatenate([buf_k.astype(dk.dtype), dk], axis=1)
    vx = jnp.concatenate([buf_v.astype(dv.dtype), dv], axis=1)
    q_idx = buf_k.shape[1] + jnp.arange(t, dtype=jnp.int32)
    dil_o = dilated_attention(dq, kx, vx, q_idx)
    y = even_output(ret_o, rg, dil_o, gn_g, w_out)
    return y, s_new, dk, dv

def compress(rows, pw):
    n, l = rows.shape[:2]
    nb = l // NSA_BLOCK
    blocks = rows[:, :nb * NSA_BLOCK].reshape(n, nb, NSA_BLOCK, G_NSA, HEAD_DIM)
    return jnp.einsum('nbrgd,rd->nbgd', blocks, pw)

def nsa_attention(q, qpos, kc, vc, fetch_sel, kw, vw, kwpos, gates):
    n, t, h, d = q.shape
    nb = kc.shape[1]
    qg = q.reshape(n, t, G_NSA, h // G_NSA, d)
    blk = jnp.arange(nb, dtype=jnp.int32)
    s_c = jnp.einsum('ntghd,nbgd->ntghb', qg, kc).astype(jnp.float32)
    cmask = ((blk[None, :] + 1) * NSA_BLOCK - 1) <= qpos[:, None]
    p_c, _, _ = masked_softmax(s_c, cmask[None, :, None, None, :])
    o_c = jnp.einsum('ntghb,nbgd->ntghd', p_c, vc)
    cur = qpos // NSA_BLOCK
    cand = blk[None, :] < cur[:, None]
    imp = jnp.where(cand[None, :, None, :], jnp.sum(p_c, axis=3), -jnp.inf)
    top_v, top_i = lax.top_k(imp, min(NSA_TOPK, nb))
    blocks = jnp.concatenate([top_i, jnp.broadcast_to(cur[None, :, None, None], (n, t, G_NSA, 1))], axis=-1)
    bvalid = jnp.concatenate([jnp.isfinite(top_v), jnp.ones((n, t, G_NSA, 1), bool)], axis=-1)
    ks, vs = fetch_sel(blocks)
    nsel = blocks.shape[-1]
    kpos = blocks[..., None] * NSA_BLOCK + jnp.arange(NSA_BLOCK, dtype=jnp.int32)
    smask = bvalid[..., None] & (kpos <= qpos[None, :, None, None, None])
    ks = ks.reshape(n, t, G_NSA, nsel * NSA_BLOCK, d)
    vs = vs.reshape(n, t, G_NSA, nsel * NSA_BLOCK, d)
    smask = smask.reshape(n, t, G_NSA, 1, nsel * NSA_BLOCK)
    s_s = jnp.einsum('ntghd,ntgkd->ntghk', qg, ks).astype(jnp.float32)
    p_s, _, _ = masked_softmax(s_s, smask)
    o_s = jnp.einsum('ntghk,ntgkd->ntghd', p_s, vs)
    s_w = jnp.einsum('ntghd,nsgd->ntghs', qg, kw).astype(jnp.float32)
    dist = qpos[:, None] - kwpos[None, :]
    wmask = (dist >= 0) & (dist < NSA_WINDOW) & (kwpos[None, :] >= 0)
    p_w, _, _ = masked_softmax(s_w, wmask[None, :, None, None, :])
    o_w = jnp.einsum('ntghs,nsgd->ntghd', p_w, vw)
    g = gates.reshape(n, t, G_NSA, h // G_NSA, 3)
    o = g[..., 0:1] * o_c + g[..., 1:2] * o_s + g[..., 2:3] * o_w
    return o.reshape(n, t, h, d)

def odd_project(xn, pos, w_in, q_g, k_g):
    n, t, _ = xn.shape
    sizes = [H_NSA * HEAD_DIM] + [G_NSA * HEAD_DIM] * 6 + [3 * H_NSA, D_RNN, D_RNN]
    cq, kcm, vcm, ksl, vsl, kwn, vwn, gt, lx, ly = jnp.split(xn @ w_in, _offsets(sizes), axis=-1)
    q = rope(rmsnorm(cq.reshape(n, t, H_NSA, HEAD_DIM), q_g), pos, ROPE_DIMS, ROPE_THETA) * HEAD_DIM ** -0.5
    kv = lambda a: a.reshape(n, t, G_NSA, HEAD_DIM)
    key = lambda a, g: rope(rmsnorm(kv(a), g), pos, ROPE_DIMS, ROPE_THETA)
    gates = jax.nn.sigmoid(gt.reshape(n, t, H_NSA, 3).astype(jnp.float32))
    return (q, key(kcm, k_g[0]), kv(vcm), key(ksl, k_g[1]), kv(vsl), key(kwn, k_g[2]), kv(vwn),
            gates, lx, ly)

def rglru(xb, h0, conv_buf, conv_w, conv_b, w_a, b_a, w_i, b_i, lam):
    n, t, d = xb.shape
    xin = jnp.concatenate([conv_buf.astype(jnp.float32), xb.astype(jnp.float32)], axis=1)
    xc = conv_b.astype(jnp.float32) + sum(xin[:, j:j + t] * conv_w[j].astype(jnp.float32) for j in range(CONV_W))
    xr = xc.reshape(n, t, RNN_BLOCKS, d // RNN_BLOCKS)
    r = jax.nn.sigmoid(jnp.einsum('ntbi,bij->ntbj', xr, w_a.astype(jnp.float32)).reshape(n, t, d) + b_a)
    i = jax.nn.sigmoid(jnp.einsum('ntbi,bij->ntbj', xr, w_i.astype(jnp.float32)).reshape(n, t, d) + b_i)
    log_a = -LRU_C * r * jax.nn.softplus(-lam.astype(jnp.float32))
    a = jnp.exp(log_a)
    b = jnp.sqrt(-jnp.expm1(2.0 * log_a)) * (i * xc)
    b = b.at[:, 0].add(a[:, 0] * h0.astype(jnp.float32))
    def combine(lhs, rhs):
        return rhs[0] * lhs[0], rhs[0] * lhs[1] + rhs[1]
    _, h = lax.associative_scan(combine, (a, b), axis=1)
    return h, h[:, -1], xin[:, -(CONV_W - 1):]

def odd_output(o_nsa, h, ly, w_out):
    n, t = ly.shape[:2]
    y_rnn = jax.nn.gelu(ly.astype(jnp.float32)) * h
    cat = jnp.concatenate([o_nsa.reshape(n, t, -1).astype(jnp.float32), y_rnn], axis=-1)
    return cat.astype(w_out.dtype) @ w_out

def odd_mixer_prompt(xn, pos, w_in, q_g, k_g, pw_k, pw_v, conv_w, conv_b, w_a, b_a, w_i, b_i, lam, w_out):
    n, t, _ = xn.shape
    q, kcm, vcm, ksl, vsl, kwn, vwn, gates, lx, ly = odd_project(xn, pos, w_in, q_g, k_g)
    kc, vc = compress(kcm, pw_k), compress(vcm, pw_v)
    nb = t // NSA_BLOCK
    kb = ksl.reshape(n, nb, NSA_BLOCK, G_NSA, HEAD_DIM)
    vb = vsl.reshape(n, nb, NSA_BLOCK, G_NSA, HEAD_DIM)
    n_idx = jnp.arange(n)[:, None, None, None]
    g_idx = jnp.arange(G_NSA)[None, None, :, None]
    def fetch(blocks):
        return kb[n_idx, blocks, :, g_idx], vb[n_idx, blocks, :, g_idx]
    pad = ((0, 0), (NSA_WINDOW, 0), (0, 0), (0, 0))
    kw_pad, vw_pad = jnp.pad(kwn, pad), jnp.pad(vwn, pad)
    nqb = t // Q_BLOCK
    def blocks_of(a):
        return a.reshape((n, nqb, Q_BLOCK) + a.shape[2:]).swapaxes(0, 1)
    def one_block(args):
        qb, gb, s0 = args
        pb = s0 + jnp.arange(Q_BLOCK, dtype=jnp.int32)
        kw = lax.dynamic_slice_in_dim(kw_pad, s0, NSA_WINDOW + Q_BLOCK, axis=1)
        vw = lax.dynamic_slice_in_dim(vw_pad, s0, NSA_WINDOW + Q_BLOCK, axis=1)
        kwpos = s0 - NSA_WINDOW + jnp.arange(NSA_WINDOW + Q_BLOCK, dtype=jnp.int32)
        return nsa_attention(qb, pb, kc, vc, fetch, kw, vw, kwpos, gb)
    starts = jnp.arange(nqb, dtype=jnp.int32) * Q_BLOCK
    ob = lax.map(one_block, (blocks_of(q), blocks_of(gates), starts))
    o = ob.swapaxes(0, 1).reshape(n, t, H_NSA, HEAD_DIM)
    h, h_last, conv_new = rglru(lx, jnp.zeros((n, D_RNN), jnp.float32), jnp.zeros((n, CONV_W - 1, D_RNN), jnp.float32),
                               conv_w, conv_b, w_a, b_a, w_i, b_i, lam)
    y = odd_output(o, h, ly, w_out)
    keep = min(NSA_WINDOW, t)
    return y, kcm, vcm, ksl, vsl, kwn[:, t - keep:], vwn[:, t - keep:], h_last, conv_new

def odd_mixer_sample(xn, pos, pool_ck, pool_cv, pool_sk, pool_sv, win_k, win_v, h0, conv_buf, page_table,
                     w_in, q_g, k_g, pw_k, pw_v, conv_w, conv_b, w_a, b_a, w_i, b_i, lam, w_out):
    n, t, _ = xn.shape
    n_pages = page_table.shape[1]
    past = n_pages * PAGE_SIZE
    q, kcm, vcm, ksl, vsl, kwn, vwn, gates, lx, ly = odd_project(xn, pos, w_in, q_g, k_g)
    def past_rows(pool):
        return pool[page_table].reshape(n, past, G_NSA, HEAD_DIM)
    kc = compress(jnp.concatenate([past_rows(pool_ck).astype(kcm.dtype), kcm], axis=1), pw_k)
    vc = compress(jnp.concatenate([past_rows(pool_cv).astype(vcm.dtype), vcm], axis=1), pw_v)
    bpp = PAGE_SIZE // NSA_BLOCK
    npb = past // NSA_BLOCK
    nbn = -(-t // NSA_BLOCK)
    def new_blocks(a):
        a = jnp.pad(a, ((0, 0), (0, nbn * NSA_BLOCK - t), (0, 0), (0, 0)))
        return a.reshape(n, nbn, NSA_BLOCK, G_NSA, HEAD_DIM)
    kb_new, vb_new = new_blocks(ksl), new_blocks(vsl)
    kb_pool = pool_sk.reshape(-1, NSA_BLOCK, G_NSA, HEAD_DIM)
    vb_pool = pool_sv.reshape(-1, NSA_BLOCK, G_NSA, HEAD_DIM)
    n_idx = jnp.arange(n)[:, None, None, None]
    g_idx = jnp.arange(G_NSA)[None, None, :, None]
    def fetch(blocks):
        is_past = (blocks < npb)[..., None, None]
        phys = page_table[n_idx, jnp.minimum(blocks // bpp, n_pages - 1)] * bpp + blocks % bpp
        nb_i = jnp.clip(blocks - npb, 0, nbn - 1)
        ks = jnp.where(is_past, kb_pool[phys, :, g_idx].astype(ksl.dtype), kb_new[n_idx, nb_i, :, g_idx])
        vs = jnp.where(is_past, vb_pool[phys, :, g_idx].astype(vsl.dtype), vb_new[n_idx, nb_i, :, g_idx])
        return ks, vs
    kw = jnp.concatenate([win_k.astype(kwn.dtype), kwn], axis=1)
    vw = jnp.concatenate([win_v.astype(vwn.dtype), vwn], axis=1)
    kwpos = past - win_k.shape[1] + jnp.arange(win_k.shape[1] + t, dtype=jnp.int32)
    o = nsa_attention(q, pos, kc, vc, fetch, kw, vw, kwpos, gates)
    h, h_last, conv_new = rglru(lx, h0, conv_buf, conv_w, conv_b, w_a, b_a, w_i, b_i, lam)
    y = odd_output(o, h, ly, w_out)
    return y, kcm, vcm, ksl, vsl, kwn, vwn, h_last, conv_new

def mem_kv(mem, norm_g, w_k, w_v, k_g):
    mn = rmsnorm(mem, norm_g)
    n, m, _ = mn.shape
    k = rmsnorm((mn @ w_k).reshape(n, m, H_MEM, HEAD_DIM), k_g)
    v = (mn @ w_v).reshape(n, m, H_MEM, HEAD_DIM)
    return k, v

def mem_attend(xn, k, v, w_q, q_g, w_o):
    n, t, _ = xn.shape
    q = rmsnorm((xn @ w_q).reshape(n, t, H_MEM, HEAD_DIM), q_g) * HEAD_DIM ** -0.5
    s = jnp.einsum('nthd,nmhd->nhtm', q, k.astype(q.dtype)).astype(jnp.float32)
    p = jax.nn.softmax(s, axis=-1)
    o = jnp.einsum('nhtm,nmhd->nthd', p, v).reshape(n, t, -1)
    return o.astype(w_o.dtype) @ w_o

def sq_relu_mlp(xn, w1, w2):
    hid = jax.nn.relu(xn @ w1)
    return (hid * hid) @ w2

def setup_inputs(seed: int = 0) -> dict:
    key = jax.random.key(seed)
    ks = jax.random.split(key, 96)
    counter = [0]
    def nk():
        k = ks[counter[0]]
        counter[0] += 1
        return k
    def nrm(shape, scale=1.0):
        return scale * jax.random.normal(nk(), shape, jnp.float32)
    def gain(shape):
        return 1.0 + 0.02 * nrm(shape)
    hd = HEAD_DIM
    n_pages = PAST_LEN // PAGE_SIZE
    n_used = DEC_BATCH * n_pages
    n_phys = n_used + max(1, n_used // 4)
    dil_keep = min(DIL_WMAX, PAST_LEN)
    win_keep = min(NSA_WINDOW, PAST_LEN)
    ev_in = 4 * H_RET * hd + 3 * H_DIL * hd
    od_in = H_NSA * hd + 6 * G_NSA * hd + 3 * H_NSA + 2 * D_RNN
    ev_mix = (H_RET + H_DIL) * hd
    od_mix = H_NSA * hd + D_RNN
    bw = D_RNN // RNN_BLOCKS
    d = D_MODEL
    x_prompt = nrm((BATCH, SEQ, d))
    x_sample = nrm((DEC_BATCH, DEC_SEQ, d))
    mem_prompt = nrm((BATCH, N_MEM, d))
    state_ret = nrm((N_EVEN, DEC_BATCH, H_RET, hd, hd), 0.5)
    cache_dil_k = nrm((N_EVEN, DEC_BATCH, dil_keep, H_DIL, hd))
    cache_dil_v = nrm((N_EVEN, DEC_BATCH, dil_keep, H_DIL, hd))
    cache_nsa_cmp_k = nrm((N_ODD, n_phys, PAGE_SIZE, G_NSA, hd))
    cache_nsa_cmp_v = nrm((N_ODD, n_phys, PAGE_SIZE, G_NSA, hd))
    cache_nsa_slc_k = nrm((N_ODD, n_phys, PAGE_SIZE, G_NSA, hd))
    cache_nsa_slc_v = nrm((N_ODD, n_phys, PAGE_SIZE, G_NSA, hd))
    cache_nsa_win_k = nrm((N_ODD, DEC_BATCH, win_keep, G_NSA, hd))
    cache_nsa_win_v = nrm((N_ODD, DEC_BATCH, win_keep, G_NSA, hd))
    state_lru_h = nrm((N_ODD, DEC_BATCH, D_RNN), 0.5)
    state_lru_conv = nrm((N_ODD, DEC_BATCH, CONV_W - 1, D_RNN))
    cache_mem_k = nrm((DEPTH, DEC_BATCH, N_MEM, H_MEM, hd))
    cache_mem_v = nrm((DEPTH, DEC_BATCH, N_MEM, H_MEM, hd))
    page_table = jax.random.permutation(nk(), n_phys)[:n_used].reshape(DEC_BATCH, n_pages).astype(jnp.int32)
    u = jax.random.uniform(nk(), (N_ODD, D_RNN), jnp.float32, 0.9, 0.999)
    s = u ** (1.0 / LRU_C)
    lru_lambda = jnp.log(s) - jnp.log1p(-s)
    pw_scale = NSA_BLOCK ** -0.5
    return {
        "x_prompt": x_prompt, "x_sample": x_sample, "mem_prompt": mem_prompt,
        "state_ret": state_ret, "cache_dil_k": cache_dil_k, "cache_dil_v": cache_dil_v,
        "cache_nsa_cmp_k": cache_nsa_cmp_k, "cache_nsa_cmp_v": cache_nsa_cmp_v,
        "cache_nsa_slc_k": cache_nsa_slc_k, "cache_nsa_slc_v": cache_nsa_slc_v,
        "cache_nsa_win_k": cache_nsa_win_k, "cache_nsa_win_v": cache_nsa_win_v,
        "state_lru_h": state_lru_h, "state_lru_conv": state_lru_conv,
        "cache_mem_k": cache_mem_k, "cache_mem_v": cache_mem_v, "page_table": page_table,
        "ev_w_in": nrm((N_EVEN, d, ev_in), d ** -0.5),
        "ret_gn_g": gain((N_EVEN, H_RET, hd)),
        "dil_q_norm_g": gain((N_EVEN, hd)),
        "dil_k_norm_g": gain((N_EVEN, hd)),
        "ev_w_out": nrm((N_EVEN, ev_mix, d), ev_mix ** -0.5),
        "od_w_in": nrm((N_ODD, d, od_in), d ** -0.5),
        "nsa_q_norm_g": gain((N_ODD, hd)),
        "nsa_k_norm_g": gain((N_ODD, 3, hd)),
        "nsa_pw_k": pw_scale * (1.0 + nrm((N_ODD, NSA_BLOCK, hd), 0.5)),
        "nsa_pw_v": pw_scale * (1.0 + nrm((N_ODD, NSA_BLOCK, hd), 0.5)),
        "lru_conv_w": nrm((N_ODD, CONV_W, D_RNN), CONV_W ** -0.5),
        "lru_conv_b": nrm((N_ODD, D_RNN), 0.01),
        "lru_w_a": nrm((N_ODD, RNN_BLOCKS, bw, bw), bw ** -0.5),
        "lru_b_a": nrm((N_ODD, D_RNN), 0.01),
        "lru_w_i": nrm((N_ODD, RNN_BLOCKS, bw, bw), bw ** -0.5),
        "lru_b_i": nrm((N_ODD, D_RNN), 0.01),
        "lru_lambda": lru_lambda,
        "od_w_out": nrm((N_ODD, od_mix, d), od_mix ** -0.5),
        "norm_mix_g": gain((DEPTH, d)),
        "norm_mem_g": gain((DEPTH, d)),
        "norm_mlp_g": gain((DEPTH, d)),
        "mem_norm_g": gain((DEPTH, d)),
        "mem_w_q": nrm((DEPTH, d, H_MEM * hd), d ** -0.5),
        "mem_w_k": nrm((DEPTH, d, H_MEM * hd), d ** -0.5),
        "mem_w_v": nrm((DEPTH, d, H_MEM * hd), d ** -0.5),
        "mem_q_norm_g": gain((DEPTH, hd)),
        "mem_k_norm_g": gain((DEPTH, hd)),
        "mem_w_o": nrm((DEPTH, H_MEM * hd, d), (H_MEM * hd) ** -0.5),
        "mlp_w1": nrm((DEPTH, d, D_FF), d ** -0.5),
        "mlp_w2": nrm((DEPTH, D_FF, d), 0.5 * D_FF ** -0.5),
    }

def reference(x_prompt, x_sample, mem_prompt, state_ret, cache_dil_k, cache_dil_v,
              cache_nsa_cmp_k, cache_nsa_cmp_v, cache_nsa_slc_k, cache_nsa_slc_v,
              cache_nsa_win_k, cache_nsa_win_v, state_lru_h, state_lru_conv,
              cache_mem_k, cache_mem_v, page_table,
              ev_w_in, ret_gn_g, dil_q_norm_g, dil_k_norm_g, ev_w_out,
              od_w_in, nsa_q_norm_g, nsa_k_norm_g, nsa_pw_k, nsa_pw_v,
              lru_conv_w, lru_conv_b, lru_w_a, lru_b_a, lru_w_i, lru_b_i, lru_lambda, od_w_out,
              norm_mix_g, norm_mem_g, norm_mlp_g, mem_norm_g,
              mem_w_q, mem_w_k, mem_w_v, mem_q_norm_g, mem_k_norm_g, mem_w_o,
              mlp_w1, mlp_w2):
    past = page_table.shape[1] * PAGE_SIZE
    pos_p = jnp.arange(x_prompt.shape[1], dtype=jnp.int32)
    pos_s = past + jnp.arange(x_sample.shape[1], dtype=jnp.int32)
    xp, xs = x_prompt, x_sample
    ret_p, ret_s, dk_p, dv_p, dk_s, dv_s = [], [], [], [], [], []
    ck_p, cv_p, ck_s, cv_s, sk_p, sv_p, sk_s, sv_s = [], [], [], [], [], [], [], []
    wk_p, wv_p, wk_s, wv_s, lh_p, lh_s, lc_p, lc_s = [], [], [], [], [], [], [], []
    mk_p, mv_p = [], []
    for layer in range(DEPTH):
        hp = rmsnorm(xp, norm_mix_g[layer])
        hs = rmsnorm(xs, norm_mix_g[layer])
        if layer % 2 == 0:
            e = layer // 2
            yp, s_p, k_p, v_p = even_mixer_prompt(hp, pos_p, ev_w_in[e], ret_gn_g[e], dil_q_norm_g[e],
                                                  dil_k_norm_g[e], ev_w_out[e])
            ys, s_s, k_s, v_s = even_mixer_sample(hs, pos_s, state_ret[e], cache_dil_k[e], cache_dil_v[e],
                                                  ev_w_in[e], ret_gn_g[e], dil_q_norm_g[e], dil_k_norm_g[e], ev_w_out[e])
            ret_p.append(s_p); ret_s.append(s_s)
            dk_p.append(k_p); dv_p.append(v_p); dk_s.append(k_s); dv_s.append(v_s)
        else:
            o = layer // 2
            odd_w = (od_w_in[o], nsa_q_norm_g[o], nsa_k_norm_g[o], nsa_pw_k[o], nsa_pw_v[o],
                     lru_conv_w[o], lru_conv_b[o], lru_w_a[o], lru_b_a[o], lru_w_i[o], lru_b_i[o],
                     lru_lambda[o], od_w_out[o])
            yp, a1, a2, a3, a4, a5, a6, a7, a8 = odd_mixer_prompt(hp, pos_p, *odd_w)
            ys, b1, b2, b3, b4, b5, b6, b7, b8 = odd_mixer_sample(
                hs, pos_s, cache_nsa_cmp_k[o], cache_nsa_cmp_v[o], cache_nsa_slc_k[o], cache_nsa_slc_v[o],
                cache_nsa_win_k[o], cache_nsa_win_v[o], state_lru_h[o], state_lru_conv[o], page_table, *odd_w)
            ck_p.append(a1); cv_p.append(a2); sk_p.append(a3); sv_p.append(a4)
            wk_p.append(a5); wv_p.append(a6); lh_p.append(a7); lc_p.append(a8)
            ck_s.append(b1); cv_s.append(b2); sk_s.append(b3); sv_s.append(b4)
            wk_s.append(b5); wv_s.append(b6); lh_s.append(b7); lc_s.append(b8)
        xp = xp + yp.astype(xp.dtype)
        xs = xs + ys.astype(xs.dtype)
        mk, mv = mem_kv(mem_prompt, mem_norm_g[layer], mem_w_k[layer], mem_w_v[layer], mem_k_norm_g[layer])
        mk_p.append(mk); mv_p.append(mv)
        xp = xp + mem_attend(rmsnorm(xp, norm_mem_g[layer]), mk, mv, mem_w_q[layer], mem_q_norm_g[layer],
                             mem_w_o[layer]).astype(xp.dtype)
        xs = xs + mem_attend(rmsnorm(xs, norm_mem_g[layer]), cache_mem_k[layer], cache_mem_v[layer],
                             mem_w_q[layer], mem_q_norm_g[layer], mem_w_o[layer]).astype(xs.dtype)
        xp = xp + sq_relu_mlp(rmsnorm(xp, norm_mlp_g[layer]), mlp_w1[layer], mlp_w2[layer]).astype(xp.dtype)
        xs = xs + sq_relu_mlp(rmsnorm(xs, norm_mlp_g[layer]), mlp_w1[layer], mlp_w2[layer]).astype(xs.dtype)
    new_ret_p, new_ret_s = jnp.stack(ret_p), jnp.stack(ret_s)
    new_dil_k_p, new_dil_v_p = jnp.stack(dk_p), jnp.stack(dv_p)
    new_dil_k_s, new_dil_v_s = jnp.stack(dk_s), jnp.stack(dv_s)
    new_cmp_k_p, new_cmp_v_p = jnp.stack(ck_p), jnp.stack(cv_p)
    new_cmp_k_s, new_cmp_v_s = jnp.stack(ck_s), jnp.stack(cv_s)
    new_slc_k_p, new_slc_v_p = jnp.stack(sk_p), jnp.stack(sv_p)
    new_slc_k_s, new_slc_v_s = jnp.stack(sk_s), jnp.stack(sv_s)
    new_win_k_p, new_win_v_p = jnp.stack(wk_p), jnp.stack(wv_p)
    new_win_k_s, new_win_v_s = jnp.stack(wk_s), jnp.stack(wv_s)
    new_lru_h_p, new_lru_h_s = jnp.stack(lh_p), jnp.stack(lh_s)
    new_lru_conv_p, new_lru_conv_s = jnp.stack(lc_p), jnp.stack(lc_s)
    new_mem_k_p, new_mem_v_p = jnp.stack(mk_p), jnp.stack(mv_p)
    return (xp, xs, new_ret_p, new_ret_s,
            new_dil_k_p, new_dil_v_p, new_dil_k_s, new_dil_v_s,
            new_cmp_k_p, new_cmp_v_p, new_cmp_k_s, new_cmp_v_s,
            new_slc_k_p, new_slc_v_p, new_slc_k_s, new_slc_v_s,
            new_win_k_p, new_win_v_p, new_win_k_s, new_win_v_s,
            new_lru_h_p, new_lru_h_s, new_lru_conv_p, new_lru_conv_s,
            new_mem_k_p, new_mem_v_p)


_drawn_inputs = setup_inputs


def setup_inputs(seed=0):
    import zlib

    import numpy as np

    out = dict(_drawn_inputs(seed))
    spreads = {}
    factors = {'cache_nsa_slc_k': 4.438,
     'cache_nsa_slc_v': 3.49,
     'cache_nsa_win_k': 3.106,
     'ret_gn_g': 7.017,
     'dil_q_norm_g': 8.0,
     'dil_k_norm_g': 2.803,
     'nsa_q_norm_g': 8.0,
     'nsa_k_norm_g': 7.453,
     'lru_b_a': 36.552,
     'lru_b_i': 8.0,
     'norm_mem_g': 8.0,
     'norm_mlp_g': 3.673,
     'mem_norm_g': 2.898,
     'mem_q_norm_g': 8.0,
     'mem_k_norm_g': 2.802}
    for name, (base, spread) in spreads.items():
        noise = np.random.default_rng([zlib.crc32(name.encode()), seed]).standard_normal(out[name].shape)
        drawn = base * np.exp(spread * noise) if base else spread * noise
        out[name] = __import__('jax').numpy.asarray(drawn.astype(out[name].dtype))
    for name, factor in factors.items():
        out[name] = (out[name] * factor).astype(out[name].dtype)
    return out
```

```python
from contextlib import ExitStack

import numpy as np
import concourse.bass as bass
from concourse import mybir

F32 = mybir.dt.float32
I32 = mybir.dt.int32
ALU = mybir.AluOpType
ACT = mybir.ActivationFunctionType
AXX = mybir.AxisListType.X

P = 128
D = 2048
KT = D // P
TP, NB, TS = 256, 8, 4
NS = NB * TS
T = TP + NS
HD = 128
H = 8
G = 2
HM = 4
NM = 256
PAST = 1024
PAGE = 128
NPG = PAST // PAGE
BLK = 64
NBP = TP // BLK
NBS = PAST // BLK
WIN = 512
FF = 4 * D
EPS = 1e-6
SCALE = HD ** -0.5
SLOT = 4096
SLOTS = 4
NKD = 640
LW = TP + 7 * NB
NEG = -1e30
PAD = 128

RQ, RK, RV, RG, DQ, DK, DV, EV_TILES = 0, 8, 16, 24, 32, 40, 48, 56
NQ, KCM, VCM, KSL, VSL, KWN, VWN, LX, LY, GT, OD_TILES = 0, 8, 10, 12, 14, 16, 18, 20, 28, 36, 37
MK, MV, MQ = 0, 4, 8
GN_MIX, GN_MEM, GN_MLP, GN_KV = 0, 32, 64, 96
G_EV, G_OD, G_MQ, G_MK, G_RET, G_END = 128, 144, 158, 166, 174, 182
S_EV, S_OD, S_MQ, S_MK, S_END = 0, 16, 30, 38, 46


def log_decay():
    return np.log1p(-np.exp2(-5.0 - np.arange(H))).astype(np.float64)


def positions():
    return np.concatenate([np.arange(TP), np.tile(PAST + np.arange(TS), NB)]).astype(np.float32)


def rope_tables(n_rot, theta):
    half = n_rot // 2
    inv = (1.0 / (np.float32(theta) ** (np.arange(half, dtype=np.float32) * np.float32(2.0 / n_rot)))).astype(np.float32)
    ang = (positions()[:, None] * inv[None, :]).astype(np.float32).astype(np.float64)
    cos, sin = np.ones((HD, T)), np.zeros((HD, T))
    cos[:half] = cos[half:n_rot] = np.cos(ang).T
    sin[:half] = sin[half:n_rot] = np.sin(ang).T
    rot = np.zeros((HD, HD))
    for i in range(half):
        rot[i, i + half] = -1.0
        rot[i + half, i] = 1.0
    return cos, sin, rot.T


def core_table():
    c1, s1, r1 = rope_tables(HD, 10000.0)
    c2, s2, r2 = rope_tables(HD // 4, 500000.0)
    return np.concatenate([np.eye(P), np.ones((P, P)), r1, r2, c1, s1, c2, s2], 1).astype(np.float32)


def scales_table():
    s = np.ones((P, S_END + 1))
    s[:, S_END] = EPS
    s[:, S_EV:S_EV + H] = SCALE
    s[:, S_OD:S_OD + H] = SCALE
    s[:, S_MQ:S_MQ + 2 * HM] = SCALE
    return s.astype(np.float32)


def retention_table():
    lg = log_decay()
    j, i = np.arange(P)[:, None], np.arange(TP)[None, :]
    dec = np.where(i >= j, np.exp(np.maximum(i - j, 0)[None] * lg[:, None, None]), 0.0)
    dec = dec.transpose(1, 0, 2).reshape(P, H * TP)
    n = np.arange(NS)
    same = (n[:, None] // TS == n[None, :] // TS)
    dif = (n[None, :] % TS) - (n[:, None] % TS)
    ds_ = np.where(same & (dif >= 0), np.exp(np.maximum(dif, 0)[None] * lg[:, None, None]), 0.0)
    decs = np.zeros((P, H, NS))
    decs[:NS] = ds_.transpose(1, 0, 2)
    qd = np.broadcast_to(np.exp((n % TS + 1.0)[None, :] * lg[:, None])[None], (P, H, NS))
    kd = np.stack([np.exp((TP - 1.0 - np.arange(P))[:, None] * lg), np.exp((P - 1.0 - np.arange(P))[:, None] * lg)], 2)
    g4 = np.broadcast_to(np.exp(TS * lg)[None], (P, H))
    mb = np.zeros((P, H, NB))
    for r in range(NS):
        mb[r, :, r // TS] = np.exp((TS - 1.0 - r % TS) * lg)
    parts = [dec, kd.reshape(P, -1), g4, mb.reshape(P, -1), decs.reshape(P, -1), qd.reshape(P, -1)]
    return np.concatenate(parts, 1).astype(np.float32)


def dilated_multiplicity(dist):
    n = np.zeros(dist.shape)
    for window, dil in ((128, 1), (512, 4), (2048, 16)):
        n += (dist >= 0) & (dist <= window) & (dist % dil == 0)
    return n


def dilated_rows():
    far = np.arange(512).reshape(32, 16)[:, :TS].ravel()
    return np.concatenate([far, 512 + np.arange(512)])


def log_mult(n):
    return np.where(n > 0, np.log(np.maximum(n, 1)), NEG)


def new_key_bias():
    r, b, k = np.arange(P)[:, None, None], np.arange(NB)[None, :, None], np.arange(NS)[None, None, :]
    return (r % TS) - (k % TS), (k // TS == b)


def dilated_table():
    q, k = np.arange(TP), np.arange(TP)
    bias = log_mult(dilated_multiplicity(q[:, None] - k[None, :])).reshape(2, P, TP).transpose(1, 0, 2).reshape(P, -1)
    qs = PAST + np.arange(P) % TS
    biasd = log_mult(dilated_multiplicity(qs[:, None] - dilated_rows()[None, :]))
    dist, own = new_key_bias()
    biasn = np.where(own, log_mult(dilated_multiplicity(dist)), NEG).reshape(P, -1)
    return np.concatenate([bias, biasd, biasn], 1).astype(np.float32)


def sparse_table():
    q, k = np.arange(TP), np.arange(TP)
    bias = np.where(q[:, None] >= k[None, :], 0.0, NEG).reshape(2, P, TP).transpose(1, 0, 2).reshape(P, -1)
    ok = (np.arange(NBP)[None, :] + 1) * BLK - 1 <= q[:, None]
    cb = np.where(ok, 0.0, NEG).reshape(2, P, NBP).transpose(1, 0, 2).reshape(P, -1)
    cm = ok.astype(float).reshape(2, P, NBP).transpose(1, 0, 2).reshape(P, -1)
    qs = PAST + np.arange(P) % TS
    kw = PAST - WIN + np.arange(WIN)
    wb = np.where(qs[:, None] - kw[None, :] < WIN, 0.0, NEG)
    dist, own = new_key_bias()
    nb = np.where(own & (dist >= 0), 0.0, NEG).reshape(P, -1)
    sel = np.zeros((P, NPG, NBS))
    for p in range(NPG):
        sel[:BLK, p, 2 * p] = 1.0
        sel[BLK:, p, 2 * p + 1] = 1.0
    return np.concatenate([bias, cb, cm, wb, nb, sel.reshape(P, -1)], 1).astype(np.float32)


class Ring:

    def __init__(self):
        self.unit = 0
        self.full = [0] * SLOTS

    def segment(self, units, dmas=(1, 1, 1, 1)):
        seg = Segment(self.unit, tuple(self.full), units, dmas)
        for u in range(units):
            self.full[(self.unit + u) % SLOTS] += 16 * dmas[u % SLOTS]
        self.unit += units
        return seg


class Segment:
    def __init__(self, first, full, units, dmas):
        self.first, self.full, self.units, self.dmas = first, full, units, dmas

    def slot(self, j):
        return (self.first + j) % SLOTS

    def arrived(self, j, it=0):
        return 16 * self.dmas[j % SLOTS] * (it + j // SLOTS + 1) + self.full[self.slot(j)]

    def may_fill(self, j, it=0):
        return it * SLOTS + (self.first + j + 1)

    def used(self, j, it=0):
        return it * SLOTS + (self.first + j + 1 + SLOTS)


class Stage:

    def __init__(self, kind, base, rounds):
        self.kind, self.base, self.rounds = kind, base, rounds

    def at(self, it=0):
        return it + (self.base + 1)

    @property
    def end(self):
        return self.base + self.rounds


class Chain:

    def __init__(self, eng, sem):
        self.eng, self.sem, self.base, self.k, self.it, self.per = eng, sem, 0, 0, 0, 0

    def __call__(self, ins):
        self.k += 1
        ins.then_inc(self.sem, 1)
        self.eng.wait_ge(self.sem, self.it * self.per + (self.base + self.k))

    def enter(self, it, per):
        self.base, self.k, self.it, self.per = self.base + self.k, 0, it, per

    def leave(self, rounds):
        assert self.k == self.per, (self.k, self.per)
        self.base, self.k, self.it, self.per = self.base + rounds * self.per, 0, 0, 0


def build(nc, a, o, scratch):
    ring = Ring()
    rounds = {}

    def stage(kind, n):
        st = Stage(kind, rounds.get(kind, 0), n)
        rounds[kind] = st.end
        return st

    class L:
        pass

    layers = []
    for layer in range(2):
        s = L()
        s.n_mix = stage("norm", 1)
        if layer == 0:
            s.w_in = ring.segment(28)
            s.pairs_in = stage("pair", 28)
            s.ret = stage("ret", H)
            s.prep = [(stage("prep", 16), DQ, G_EV, S_EV)]
            s.att = stage("att", H)
            s.dil = stage("dil", NB)
            s.dil_seg = ring.segment(4 * NB)
        else:
            s.w_in = ring.segment(10)
            s.pairs_in = stage("pair", 10)
            s.w_gt = ring.segment(1)
            s.pair_gt = stage("pair", 1)
            s.w_in2 = ring.segment(8)
            s.pairs_in2 = stage("pair", 8)
            s.lru_seg = ring.segment(1)
            s.lru = stage("lru", H)
            s.prep = [(stage("prep", 10), NQ, G_OD, S_OD), (stage("prep", 2), KSL, G_OD + 10, S_OD + 10),
                      (stage("prep", 2), KWN, G_OD + 12, S_OD + 12)]
            s.gate = stage("gate", 1)
            s.att = stage("nsp", H)
            s.nsd = stage("nsd", NB)
            s.nsd_seg = ring.segment(4 * NB, (16, 8, 8, 2))
        s.w_out = ring.segment(8)
        s.pairs_out = stage("pair", 8)
        s.mem_x = ring.segment(1)
        s.n_kv = stage("norm", 1)
        s.w_kv = ring.segment(4)
        s.pairs_kv = stage("pair", 4)
        s.prep_k = (stage("prep", HM), MK, G_MK + HM * layer, S_MK + HM * layer)
        s.n_mem = stage("norm", 1)
        s.w_q = ring.segment(2)
        s.pairs_q = stage("pair", 2)
        s.prep_q = (stage("prep", HM), MQ, G_MQ + HM * layer, S_MQ + HM * layer)
        s.matt = stage("att", HM)
        s.mdec = stage("mdec", NB)
        s.mdec_seg = ring.segment(NB, (2, 2, 2, 2))
        s.w_o = ring.segment(8)
        s.pairs_o = stage("pair", 8)
        s.n_mlp = stage("norm", 1)
        s.w_1 = ring.segment(32)
        s.pairs_1 = stage("pair", 32)
        s.w_2 = ring.segment(32)
        s.pairs_2 = stage("pair", 8)
        layers.append(s)
    ev, od = layers

    with ExitStack() as ctx:
        def sb(name, shape, dt=F32):
            return ctx.enter_context(nc.sbuf_tensor(name, shape, dt))

        sems = {}

        def sem(name):
            if name not in sems:
                sems[name] = ctx.enter_context(nc.semaphore(name))
            return sems[name]

        RING = sb("ring", [P, SLOTS, SLOT])
        X = sb("x", [P, KT, T])
        HT = sb("ht", [P, KT, T])
        BIG = sb("big", [P, FF // P, T])
        CORE = sb("core", [P, 4 * P + 4 * T])
        GAIN = sb("gain", [P, G_END])
        SCL = sb("scl", [P, S_END + 1])
        PT = sb("pages", [1, NB * NPG], I32)
        GROW = sb("gate_rows", [P, 3, 3 * H])
        GDEC = sb("gate_dec", [NS, NB * 3])
        A = sb("arena", [P, 6500])
        PS = ctx.enter_context(nc.psum_tensor("ps", [P, 8, 512], F32))
        PMEM = sb("stats", [P, 64])

        IDENT, ONES, ROT64, ROT32 = (CORE[:, i * P:(i + 1) * P] for i in range(4))
        COSR, SINR, COSD, SIND = (CORE[:, 4 * P + i * T:4 * P + (i + 1) * T] for i in range(4))
        bigf = BIG[:, :, :].rearrange("p k t -> p (k t)")
        EVT = bigf[:, EV_TILES * T:]
        ODT = bigf[:, OD_TILES * T:]

        def dyn(buf, i, c0=0, c1=T):
            return buf[:, bass.ds(i, 1), c0:c1].rearrange("p o c -> p (o c)")

        def row(buf, i, n):
            return buf[:, bass.ds(i, n)]

        def carve(sizes, start=0):
            out, at = [], start
            for n in sizes:
                out.append(A[:, at:at + n])
                at += n
            assert at <= 6500, at
            return out

        ring_full = [sem(f"ring_full{i}") for i in range(SLOTS)]
        ring_used, pair_free, squared_hid = sem("ring_used"), sem("pair_free"), sem("squared_hid")
        consts_in, tables_in, outs_out = sem("consts_in"), sem("tables_in"), sem("outs_out")
        table_value = {"ret": 32, "dil": 48, "lru": 64, "nsa": 96}
        out_value = {"dil": 16, "mem0": 32, "lx": 48, "lru": 64, "nsa": 80, "mem1": 96}
        EPSC = SCL[:, S_END:S_END + 1]

        def slot(seg, j):
            return RING[:, seg.slot(j), :]

        sqb = carve([T] * 4)
        t_rms = carve([T, T], 4 * T)

        def norm_act(act, st, src, n):
            for i in range(KT):
                if i >= 4:
                    act.wait_ge(sem("norm_summed"), KT * st.base + i - 3)
                act.activation(sqb[i % 4][:, 0:n], src[:, i, 0:n], ACT.Square).then_inc(sem("norm_sq"), 1)
            act.wait_ge(sem("norm_summed"), KT * st.end)
            act.activation(t_rms[0][:, 0:n], PS[:, 4, 0:n], ACT.Ln, scale=1.0 / D, bias=EPSC).then_inc(sem("norm_ln"), 1)
            act.wait_ge(sem("norm_ln"), st.at())
            act.activation(t_rms[1][:, 0:n], t_rms[0][:, 0:n], ACT.Exp, scale=-0.5).then_inc(sem("norm_rms"), 1)

        def norm_pe(pe, st, n):
            for i in range(KT):
                pe.wait_ge(sem("norm_sq"), KT * st.base + i + 1)
                pe.matmul(PS[:, 4, 0:n], ONES, sqb[i % 4][:, 0:n], start=(i == 0), stop=(i == KT - 1)).then_inc(sem("norm_summed"), 1)

        def norm_dve(dve, st, src, gain, n):
            dve.wait_ge(sem("norm_rms"), st.at())
            for i in range(KT):
                dve.scalar_tensor_tensor(out=HT[:, i, 0:n], in0=src[:, i, 0:n], scalar=GAIN[:, gain + i:gain + i + 1],
                                         in1=t_rms[1][:, 0:n], op0=ALU.mult, op1=ALU.mult).then_inc(sem("normed"), 1)

        def after_norm(eng, st):
            eng.wait_ge(sem("normed"), KT * st.end)

        def lin_pe(pe, seg, pairs, src, kt, n, loops, tail=(), width=256):
            def unit(j, it, w):
                pe.wait_ge(ring_full[seg.slot(j)], seg.arrived(j, it))
                pe.wait_ge(pair_free, it * SLOTS + (pairs.base + j + 1))
                W = slot(seg, j)[:, 0:kt * w].rearrange("p (k m) -> p k m", k=kt)
                for m in range(0, w, P):
                    mw = min(P, w - m)
                    for k in range(kt):
                        mm = pe.matmul(PS[0:mw, 2 * ((pairs.base + j) % 2) + m // P, 0:n], W[:, k, m:m + mw], src[:, k, 0:n],
                                       start=(k == 0), stop=(k == kt - 1))
                mm.then_inc(ring_used, 1)
            if loops:
                with pe.Fori(0, loops) as it:
                    for j in range(SLOTS):
                        unit(j, it, 256)
            for j in range(SLOTS * loops, seg.units):
                unit(j, 0, width)

        def lin_act(act, seg, pairs, dst, tile0, n, loops, func=ACT.Copy, width=256):
            def unit(j, it):
                act.wait_ge(ring_used, seg.used(j, it))
                b = 2 * ((pairs.base + j) % 2)
                if width < P:
                    ins = act.activation(dst[0:width, tile0, 0:n], PS[0:width, b, 0:n], func)
                else:
                    ins = act.activation(dst[:, bass.ds(it * 8 + (tile0 + 2 * j), 2), 0:n] if loops and j < 4 * loops
                                         else dst[:, tile0 + 2 * j:tile0 + 2 * j + 2, 0:n], PS[:, b:b + 2, 0:n], func)
                ins.then_inc(pair_free, 1)
            if loops:
                with act.Fori(0, loops) as it:
                    for j in range(SLOTS):
                        unit(j, it)
            for j in range(SLOTS * loops, seg.units):
                unit(j, 0)

        def square_dve(dve, pairs):
            with dve.Fori(0, 8) as it:
                for j in range(SLOTS):
                    dve.wait_ge(pair_free, it * SLOTS + (3 + pairs.base + j))
                    t = BIG[:, bass.ds(it * 8 + 2 * j, 2), :]
                    dve.tensor_tensor(t, t, t, ALU.mult).then_inc(squared_hid, 1)

        def w2_pe(pe, seg, pairs):
            with pe.Fori(0, 4) as it:
                for j in range(2 * SLOTS):
                    q, pair = j % 4, pairs.base + j // 4
                    pe.wait_ge(ring_full[seg.slot(j)], seg.arrived(j, it * 2))
                    if q == 0:
                        pe.wait_ge(pair_free, it * 2 + (pair + 1))
                    W = slot(seg, j).rearrange("p (k m) -> p k m", k=KT)
                    for m in range(2):
                        for k in range(KT):
                            mm = pe.matmul(PS[:, 2 * (pair % 2) + m, 0:T], W[:, k, m * P:(m + 1) * P], BIG[:, KT * q + k, :],
                                           start=(q == 0 and k == 0), stop=(q == 3 and k == KT - 1))
                    mm.then_inc(ring_used, 1)

        def resid_dve(dve, seg, pairs, per, loops):
            with dve.Fori(0, loops) as it:
                step = 2 if per == 4 else 4
                for q in range(step):
                    j = q * per + per - 1
                    dve.wait_ge(ring_used, it * (step * per) + (seg.first + j + 1 + SLOTS))
                    b = 2 * ((pairs.base + q) % 2)
                    x2 = X[:, bass.ds(it * (2 * step) + 2 * q, 2), :]
                    dve.tensor_tensor(x2, x2, PS[:, b:b + 2, 0:T], ALU.add).then_inc(pair_free, 1)

        def after_pairs(eng, pairs):
            eng.wait_ge(pair_free, 2 + pairs.end)

        psq, pxg, pt1, pt2, prr, pln = carve([T] * 6)

        def prep_act(act, st, tile0, n):
            with act.Fori(0, st.rounds) as it:
                act.wait_ge(sem("prep_done"), it + (st.base + 1))
                act.activation(psq[:, 0:n], dyn(BIG, it + tile0, 0, n), ACT.Square).then_inc(sem("prep_sq"), 1)
                act.wait_ge(sem("prep_sum"), st.at(it))
                act.activation(pln[:, 0:n], PS[:, 4, 0:n], ACT.Ln, scale=1.0 / HD, bias=EPSC).then_inc(sem("prep_ln"), 1)
                act.wait_ge(sem("prep_ln"), st.at(it))
                act.activation(prr[:, 0:n], pln[:, 0:n], ACT.Exp, scale=-0.5).then_inc(sem("prep_rms"), 1)

        def prep_pe(pe, st, n, rope):
            with pe.Fori(0, st.rounds) as it:
                if rope:
                    pe.wait_ge(sem("prep_xg"), st.at(it))
                    pe.matmul(PS[:, 5, 0:n], ROT32, pxg[:, 0:n], start=True, stop=True)
                pe.wait_ge(sem("prep_sq"), st.at(it))
                pe.matmul(PS[:, 4, 0:n], ONES, psq[:, 0:n], start=True, stop=True).then_inc(sem("prep_sum"), 1)

        def prep_dve(dve, chain, st, tile0, gain, scl, n, rope):
            with dve.Fori(0, st.rounds) as it:
                chain.enter(it, 2 if rope else 0)
                dve.wait_ge(sem("prep_done"), it + (st.base + 1))
                dve.tensor_scalar(pxg[:, 0:n], dyn(BIG, it + tile0, 0, n), row(GAIN, it + gain, 1), None, ALU.mult).then_inc(sem("prep_xg"), 1)
                dve.wait_ge(sem("prep_xg"), st.at(it))
                dve.wait_ge(sem("prep_sum"), st.at(it))
                if rope:
                    dve.tensor_tensor(pt1[:, 0:n], pxg[:, 0:n], COSD[:, 0:n], ALU.mult)
                    chain(dve.tensor_tensor(pt2[:, 0:n], PS[:, 5, 0:n], SIND[:, 0:n], ALU.mult))
                    chain(dve.tensor_tensor(pt1[:, 0:n], pt1[:, 0:n], pt2[:, 0:n], ALU.add))
                src = pt1 if rope else pxg
                dve.wait_ge(sem("prep_rms"), st.at(it))
                dve.scalar_tensor_tensor(out=dyn(BIG, it + tile0, 0, n), in0=src[:, 0:n], scalar=row(SCL, it + scl, 1), in1=prr[:, 0:n],
                                         op0=ALU.mult, op1=ALU.mult).then_inc(sem("prep_done"), 1)
            chain.leave(st.rounds)

        def after_prep(eng, st):
            eng.wait_ge(sem("prep_done"), 1 + st.end)

        (r_q, r_k, r_v, r_t1, r_t2, r_in, r_vr, r_kr, r_st, r_sn, r_vb, r_sp, r_ins, r_qd) = carve(
            [T, T, T, T, T, 384, 384, 384, 1024, 1024, 1024, P, NS, NS])
        r_o, r_c, r_sq, r_ln = r_q, r_k, r_t1, r_t2
        R_DEC, R_KD, R_G4, R_MB = 0, H * TP, H * TP + 2 * H, H * TP + 3 * H
        R_DS = R_MB + H * NB
        R_QD = R_DS + H * NS
        RTAB1 = R_DS
        r_tab2 = HT[:, 14:16, :].rearrange("p k t -> p (k t)")

        def ret_act(act, st):
            after_pairs(act, ev.pairs_in)
            gate = BIG[:, RG:RG + H, :]
            act.activation(gate, gate, ACT.Silu).then_inc(sem("ret_silu"), 1)
            with act.Fori(0, H) as h:
                act.wait_ge(sem("ret_done"), h + 1)
                act.dma_start(r_st, a["state_ret"][bass.ds(h, 1)].rearrange("o d n -> (o d) n")).then_inc(sem("ret_st"), 16)
                act.activation(r_v, dyn(BIG, h + RV), ACT.Copy).then_inc(sem("ret_v"), 1)
                act.wait_ge(sem("ret_rows"), h + 1)
                act.activation(r_vr[:, 0:256], PS[:, 3, 0:256], ACT.Copy)
                act.activation(r_vr[0:NS, 256:384], PS[0:NS, 3, 256:384], ACT.Copy).then_inc(sem("ret_vr"), 1)
                act.wait_ge(sem("ret_sn"), h + 1)
                act.dma_start(o["ret_s"][bass.ds(h, 1)].rearrange("o d n -> (o d) n"), r_sn).then_inc(sem("ret_saved"), 16)
                act.dma_start(o["ret_p"][bass.ds(h, 1)].rearrange("o d n -> (o d) n"), r_sp).then_inc(sem("ret_saved"), 16)
                act.wait_ge(sem("ret_cen"), h + 1)
                act.activation(r_sq, r_c, ACT.Square).then_inc(sem("ret_sq"), 1)
                act.wait_ge(sem("ret_var"), h + 1)
                act.activation(r_ln, PS[:, 4, 0:T], ACT.Ln, scale=1.0 / HD, bias=EPSC).then_inc(sem("ret_ln"), 1)
                act.wait_ge(sem("ret_ln"), h + 1)
                act.activation(r_ln, r_ln, ACT.Exp, scale=-0.5).then_inc(sem("ret_rstd"), 1)

        def ret_pe(pe, st):
            after_pairs(pe, ev.pairs_in)
            with pe.Fori(0, H) as h:
                pe.wait_ge(sem("ret_done"), h + 1)
                pe.matmul(PS[:, 0, 0:T], ROT64, dyn(BIG, h + RQ), start=True, stop=True)
                pe.matmul(PS[:, 1, 0:T], ROT64, dyn(BIG, h + RK), start=True, stop=True).then_inc(sem("ret_rot"), 1)
                pe.wait_ge(sem("ret_v"), h + 1)
                for i, w in ((0, P), (1, P), (2, NS)):
                    pe.matmul(PS[0:w, 3, i * P:(i + 1) * P], r_v[:, i * P:i * P + w], IDENT, start=True, stop=True)
                pe.wait_ge(sem("ret_qk"), h + 1)
                for i, w in ((0, P), (1, P), (2, NS)):
                    mm = pe.matmul(PS[0:w, 2, i * P:(i + 1) * P], r_k[:, i * P:i * P + w], IDENT, start=True, stop=True)
                mm.then_inc(sem("ret_rows"), 1)
                pe.matmul(PS[:, 4, 0:256], r_k[:, 0:P], r_q[:, 0:256], start=True, stop=True)
                pe.matmul(PS[:, 4, 256:384], r_k[:, P:256], r_q[:, P:256], start=True, stop=True)
                pe.matmul(PS[0:NS, 5, 0:NS], r_k[:, 256:T], r_q[:, 256:T], start=True, stop=True).then_inc(sem("ret_sc"), 1)
                pe.wait_ge(sem("ret_in"), h + 1)
                pe.matmul(PS[:, 6, 0:256], r_vr[:, 0:P], r_in[:, 0:256], start=True, stop=True)
                pe.matmul(PS[:, 6, P:256], r_vr[:, P:256], r_in[:, 256:384], start=False, stop=True, skip_group_check=True)
                pe.wait_ge(sem("ret_st"), 16 * h + 16)
                pe.matmul(PS[:, 7, 0:NS], r_vr[0:NS, 256:384], r_ins[0:NS, :], start=True, stop=True, skip_group_check=True)
                for b in range(NB):
                    mm = pe.matmul(PS[:, 7, b * TS:(b + 1) * TS], r_st[:, b * P:(b + 1) * P], r_qd[:, b * TS:(b + 1) * TS],
                                   start=False, stop=True, skip_group_check=True)
                mm.then_inc(sem("ret_o"), 1)
                pe.matmul(PS[:, 0, 0:P], r_kr[:, 0:P], r_vr[:, 0:P], start=True, stop=False)
                pe.matmul(PS[:, 0, 0:P], r_kr[:, P:256], r_vr[:, P:256], start=False, stop=True)
                for half in range(2):
                    mm = pe.matmul(PS[:, 1 + half, 0:512], r_kr[0:NS, 256:384], r_vb[0:NS, half * 512:(half + 1) * 512], start=True, stop=True)
                mm.then_inc(sem("ret_new"), 1)
                pe.wait_ge(sem("ret_os"), h + 1)
                pe.matmul(PS[:, 3, 0:T], ONES, r_o, start=True, stop=True).then_inc(sem("ret_mean"), 1)
                pe.wait_ge(sem("ret_sq"), h + 1)
                pe.matmul(PS[:, 4, 0:T], ONES, r_sq, start=True, stop=True).then_inc(sem("ret_var"), 1)

        def ret_dve(dve, chain, st):
            tab = EVT
            after_pairs(dve, ev.pairs_in)
            dve.wait_ge(tables_in, table_value["ret"])
            dve.wait_ge(sem("ret_silu"), 1)
            with dve.Fori(0, H) as h:
                chain.enter(h, 4)
                dve.wait_ge(sem("ret_rot"), h + 1)
                for src, bank, dst, s in ((RK, 1, r_k, 1.0), (RQ, 0, r_q, SCALE)):
                    dve.scalar_tensor_tensor(out=r_t1, in0=dyn(BIG, h + src), scalar=s, in1=COSR, op0=ALU.mult, op1=ALU.mult)
                    chain(dve.scalar_tensor_tensor(out=r_t2, in0=PS[:, bank, 0:T], scalar=s, in1=SINR, op0=ALU.mult, op1=ALU.mult))
                    ins = dve.tensor_tensor(dst, r_t1, r_t2, ALU.add)
                    if src == RK:
                        chain(ins)
                ins.then_inc(sem("ret_qk"), 1)
                dve.wait_ge(sem("ret_qk"), h + 1)
                dve.wait_ge(sem("ret_rows"), h + 1)
                kd = tab[:, R_KD:R_KD + 2 * H]
                for i in range(2):
                    dve.tensor_scalar(r_kr[:, i * P:(i + 1) * P], PS[:, 2, i * P:(i + 1) * P], row(kd, h * 2 + i, 1), None, ALU.mult)
                dve.tensor_copy(r_kr[0:NS, 256:384], PS[0:NS, 2, 256:384])
                dve.wait_ge(sem("ret_sc"), h + 1)
                dve.tensor_tensor(r_in[:, 0:256], PS[:, 4, 0:256], row(tab, h * TP, TP), ALU.mult)
                dve.tensor_tensor(r_in[:, 256:384], PS[:, 4, 256:384], row(tab, h * TP, P), ALU.mult)
                dve.tensor_tensor(r_ins[0:NS, :], PS[0:NS, 5, 0:NS], r_tab2[0:NS, bass.ds(h * NS, NS)], ALU.mult)
                dve.tensor_tensor(r_qd, r_q[:, 256:T], row(r_tab2, h * NS + H * NS, NS), ALU.mult)
                dve.wait_ge(sem("ret_vr"), h + 1)
                mb = tab[0:NS, bass.ds(h * NB + R_MB, NB)]
                dve.tensor_tensor(r_vb[0:NS, :].rearrange("p (b v) -> p b v", b=NB),
                                  r_vr[0:NS, 256:384].unsqueeze(1).broadcast_to([NS, NB, P]),
                                  mb.unsqueeze(2).broadcast_to([NS, NB, P]), ALU.mult).then_inc(sem("ret_in"), 1)
                dve.wait_ge(sem("ret_o"), h + 1)
                dve.tensor_copy(r_o[:, 0:256], PS[:, 6, 0:256])
                dve.tensor_copy(r_o[:, 256:T], PS[:, 7, 0:NS]).then_inc(sem("ret_os"), 1)
                dve.wait_ge(sem("ret_os"), h + 1)
                dve.wait_ge(sem("ret_new"), h + 1)
                dve.wait_ge(sem("ret_saved"), h * 32 + 32)
                dve.tensor_copy(r_sp, PS[:, 0, 0:P])
                g4 = row(tab, h + R_G4, 1)
                for half in range(2):
                    c = slice(half * 512, (half + 1) * 512)
                    ins = dve.scalar_tensor_tensor(out=r_sn[:, c], in0=r_st[:, c], scalar=g4, in1=PS[:, 1 + half, 0:512],
                                                   op0=ALU.mult, op1=ALU.add)
                ins.then_inc(sem("ret_sn"), 1)
                dve.wait_ge(sem("ret_mean"), h + 1)
                dve.scalar_tensor_tensor(out=r_c, in0=PS[:, 3, 0:T], scalar=-1.0 / HD, in1=r_o,
                                         op0=ALU.mult, op1=ALU.add).then_inc(sem("ret_cen"), 1)
                dve.wait_ge(sem("ret_cen"), h + 1)
                dve.wait_ge(sem("ret_rstd"), h + 1)
                chain(dve.scalar_tensor_tensor(out=r_c, in0=r_c, scalar=row(GAIN, h + G_RET, 1), in1=r_ln, op0=ALU.mult, op1=ALU.mult))
                dve.tensor_tensor(dyn(HT, h), r_c, dyn(BIG, h + RG), ALU.mult).then_inc(sem("ret_done"), 1)
            chain.leave(H)

        (a_q, a_v, a_sm, a_p, a_pt, a_vr, a_kn) = carve([T, T, 512, 512, 512, 384, 0])
        a_mx, a_nm, a_l, a_r = (PMEM[:, i * 2:i * 2 + 2] for i in range(4))
        VN = bigf[:, 0:H * P]

        def att_act(act, st, tq, tv, rows_out):
            with act.Fori(0, st.rounds) as h:
                act.wait_ge(sem("att_done"), h + (st.base + 1))
                act.activation(a_q, dyn(BIG, h + tq), ACT.Copy)
                act.activation(a_v[:, 0:VW[rows_out]], dyn(BIG, h + tv, 0, VW[rows_out]), ACT.Copy).then_inc(sem("att_qv"), 1)
                act.wait_ge(sem("att_sc"), st.at(h))
                act.activation(a_vr[:, 0:256], PS[:, 5, 0:256], ACT.Copy)
                if rows_out:
                    act.activation(VN[0:NS, bass.ds(h * P, P)], PS[0:NS, 5, 256:384], ACT.Copy)
                act.wait_ge(sem("att_nm"), st.at(h))
                for q in range(2):
                    ins = act.activation(a_p[:, q * TP:(q + 1) * TP], a_sm[:, q * TP:(q + 1) * TP], ACT.Exp, bias=a_nm[:, q:q + 1],
                                         accum_out=a_l[:, q:q + 1])
                ins.then_inc(sem("att_exp"), 1)
                act.wait_ge(sem("att_turned"), st.at(h))
                act.activation(a_pt, PS[:, 6, 0:512], ACT.Copy).then_inc(sem("att_pt"), 1)

        def att_pe(pe, st, tk, rows_out):
            with pe.Fori(0, st.rounds) as h:
                pe.wait_ge(sem("att_qv"), st.at(h))
                for q in range(2):
                    pe.matmul(PS[:, 4, q * TP:(q + 1) * TP], a_q[:, q * P:(q + 1) * P], dyn(BIG, h + tk, 0, TP), start=True, stop=True)
                for i, w in ((0, P), (1, P), (2, NS))[:3 if rows_out else 2]:
                    mm = pe.matmul(PS[0:w, 5, i * P:(i + 1) * P], a_v[:, i * P:i * P + w], IDENT, start=True, stop=True)
                mm.then_inc(sem("att_sc"), 1)
                pe.wait_ge(sem("att_p"), st.at(h))
                for k in range(2):
                    for q in range(2):
                        mm = pe.transpose(PS[:, 6, k * TP + q * P:k * TP + (q + 1) * P], a_p[:, q * TP + k * P:q * TP + (k + 1) * P], IDENT)
                mm.then_inc(sem("att_turned"), 1)
                pe.wait_ge(sem("att_pt"), st.at(h))
                for k in range(2):
                    mm = pe.matmul(PS[:, 7, 0:TP], a_vr[:, k * P:(k + 1) * P], a_pt[:, k * TP:(k + 1) * TP], start=(k == 0), stop=(k == 1))
                mm.then_inc(sem("att_o"), 1)

        def att_dve(dve, chain, st, bias, cat):
            with dve.Fori(0, st.rounds) as h:
                chain.enter(h, 3)
                dve.wait_ge(sem("att_sc"), st.at(h))
                if bias is None:
                    chain(dve.tensor_copy(a_sm, PS[:, 4, 0:512]))
                else:
                    chain(dve.tensor_tensor(a_sm, PS[:, 4, 0:512], bias, ALU.add))
                chain(dve.tensor_reduce(a_mx, a_sm.rearrange("p (q k) -> p q k", q=2), AXX, ALU.max))
                dve.tensor_scalar(a_nm, a_mx, -1.0, None, ALU.mult).then_inc(sem("att_nm"), 1)
                dve.wait_ge(sem("att_exp"), st.at(h))
                chain(dve.reciprocal(a_r, a_l))
                for q in range(2):
                    ins = dve.tensor_scalar(a_p[:, q * TP:(q + 1) * TP], a_p[:, q * TP:(q + 1) * TP], a_r[:, q:q + 1], None, ALU.mult)
                ins.then_inc(sem("att_p"), 1)
                dve.wait_ge(sem("att_o"), st.at(h))
                dve.tensor_copy(dyn(HT, h + cat, 0, TP), PS[:, 7, 0:TP]).then_inc(sem("att_done"), 1)
            chain.leave(st.rounds)

        VW = {True: T, False: TP}

        def after_att(eng, st):
            eng.wait_ge(sem("att_done"), 1 + st.end)

        NKN = NKD + PAD
        (d_qb, d_sm, d_p, d_pt) = carve([H * 36, NKN, NKN, 6 * NS], 0)
        D_B, D_BD, D_BN = 0, 512, 512 + NKD
        s_mx, s_nm, s_l, s_r = (PMEM[0:NS, 8 + i * 4:12 + i * 4] for i in range(4))

        def diag(buf, n, w):
            return buf.rearrange("p (h c) -> p h c", c=n * w + w)[:, :, 0:w]

        def dil_act(act, st):
            with act.Fori(0, NB) as b:
                act.wait_ge(sem("dil_nm"), b + 1)
                act.activation(d_p[0:NS, 0:NKD + NS], d_sm[0:NS, 0:NKD + NS], ACT.Exp, bias=s_nm[:, 0:1], accum_out=s_l[:, 0:1]).then_inc(sem("dil_exp"), 1)

        def dil_pe(pe, st, seg):
            with pe.Fori(0, NB) as b:
                pe.wait_ge(sem("dil_q"), b + 1)
                for h in range(H):
                    j = h // 4
                    if h % 4 == 0:
                        pe.wait_ge(ring_full[seg.slot(j)], seg.arrived(j, b))
                    K = slot(seg, j)[:, 0:4 * NKD].rearrange("p (h k) -> p h k", h=4)[:, h % 4, :]
                    q = d_qb[:, h * NS:(h + 1) * NS]
                    first, last = h == 0, h == H - 1
                    pe.matmul(PS[0:NS, 6, 0:NS], q, BIG[:, DK + h, TP:T], start=first, stop=last)
                    pe.matmul(PS[0:NS, 5, 0:NKD - 512], q, K[:, 512:NKD], start=first, stop=last)
                    mm = pe.matmul(PS[0:NS, 4, 0:512], q, K[:, 0:512], start=first, stop=last)
                    if h == 3:
                        mm.then_inc(ring_used, 1)
                mm.then_inc(ring_used, 1)
                pe.wait_ge(sem("dil_p"), b + 1)
                for i in range(6):
                    mm = pe.matmul(PS[:, 7, i * NS:(i + 1) * NS], d_p[0:NS, i * P:(i + 1) * P], IDENT[0:NS, 0:NS], start=True, stop=True)
                mm.then_inc(sem("dil_turned"), 1)
                pe.wait_ge(sem("dil_pt"), b + 1)
                for h in range(H):
                    j = 2 + h // 4
                    if h % 4 == 0:
                        pe.wait_ge(ring_full[seg.slot(j)], seg.arrived(j, b))
                    V = slot(seg, j)[:, 0:5 * 512].rearrange("p (t h d) -> p t h d", t=5, h=4)
                    out = PS[:, 3, h * TS:(h + 1) * TS]
                    pe.matmul(out, VN[0:NS, h * P:(h + 1) * P], d_pt[0:NS, 5 * NS + h * TS:5 * NS + (h + 1) * TS], start=True, stop=False)
                    for i in range(5):
                        mm = pe.matmul(out, V[:, i, h % 4, :], d_pt[:, i * NS + h * TS:i * NS + (h + 1) * TS], start=False, stop=(i == 4))
                    if h == 3:
                        mm.then_inc(ring_used, 1)
                mm.then_inc(ring_used, 1)

        def dil_dve(dve, chain, st, seg):
            tab = EVT
            chain(dve.memset(d_qb, 0.0))
            dve.memset(d_p[:, 0:NKN], 0.0)
            chain(dve.memset(d_sm[:, 0:NKN], 0.0))
            with dve.Fori(0, NB) as b:
                chain.enter(b, 3)
                dve.tensor_copy(diag(d_qb, H, TS), BIG[:, DQ:DQ + H, bass.ds(b * TS + TP, TS)]).then_inc(sem("dil_q"), 1)
                dve.wait_ge(ring_used, seg.used(1, b))
                dve.tensor_tensor(d_sm[0:NS, 0:512], PS[0:NS, 4, 0:512], tab[0:NS, D_BD:D_BD + 512], ALU.add)
                dve.tensor_tensor(d_sm[0:NS, 512:NKD], PS[0:NS, 5, 0:NKD - 512], tab[0:NS, D_BD + 512:D_BD + NKD], ALU.add)
                chain(dve.tensor_tensor(d_sm[0:NS, NKD:NKD + NS], PS[0:NS, 6, 0:NS], tab[0:NS, bass.ds(b * NS + D_BN, NS)], ALU.add))
                chain(dve.tensor_reduce(s_mx[:, 0:1], d_sm[0:NS, 0:NKD + NS], AXX, ALU.max))
                dve.tensor_scalar(s_nm[:, 0:1], s_mx[:, 0:1], -1.0, None, ALU.mult).then_inc(sem("dil_nm"), 1)
                dve.wait_ge(sem("dil_exp"), b + 1)
                chain(dve.reciprocal(s_r[:, 0:1], s_l[:, 0:1]))
                dve.tensor_scalar(d_p[0:NS, 0:NKD + NS], d_p[0:NS, 0:NKD + NS], s_r[:, 0:1], None, ALU.mult).then_inc(sem("dil_p"), 1)
                dve.wait_ge(sem("dil_turned"), b + 1)
                dve.tensor_copy(d_pt, PS[:, 7, 0:6 * NS]).then_inc(sem("dil_pt"), 1)
                dve.wait_ge(ring_used, seg.used(3, b))
                dve.tensor_copy(HT[:, H:2 * H, bass.ds(b * TS + TP, TS)],
                                PS[:, 3, 0:NS].rearrange("p (h t) -> p h t", h=H)).then_inc(sem("dil_done"), 1)
            chain.leave(NB)

        MR = HM * TS
        (m_qb, m_sm, m_p, m_pt) = carve([HM * (MR + TS), NM, NM, 2 * MR])

        def mdec_act(act, st):
            with act.Fori(0, NB) as b:
                act.wait_ge(sem("mdec_nm"), st.at(b))
                act.activation(m_p[0:MR, :], m_sm[0:MR, :], ACT.Exp, bias=s_nm[0:MR, 1:2], accum_out=s_l[0:MR, 1:2]).then_inc(sem("mdec_exp"), 1)

        def mdec_pe(pe, st, seg):
            with pe.Fori(0, NB // SLOTS) as it:
                for j in range(SLOTS):
                    now = it * SLOTS + (st.base + j + 1)
                    pe.wait_ge(sem("mdec_q"), now)
                    pe.wait_ge(ring_full[seg.slot(j)], seg.arrived(j, it))
                    K = slot(seg, j)[:, 0:HM * NM].rearrange("p (h k) -> p h k", h=HM)
                    V = slot(seg, j)[:, HM * NM:2 * HM * NM].rearrange("p (t h d) -> p t h d", t=2, h=HM)
                    for h in range(HM):
                        mm = pe.matmul(PS[0:MR, 4, 0:NM], m_qb[:, h * MR:(h + 1) * MR], K[:, h, :], start=(h == 0), stop=(h == HM - 1))
                    mm.then_inc(sem("mdec_sc"), 1)
                    pe.wait_ge(sem("mdec_p"), now)
                    for i in range(2):
                        mm = pe.matmul(PS[:, 5, i * MR:(i + 1) * MR], m_p[0:MR, i * P:(i + 1) * P], IDENT[0:MR, 0:MR], start=True, stop=True)
                    mm.then_inc(sem("mdec_turned"), 1)
                    pe.wait_ge(sem("mdec_pt"), now)
                    for h in range(HM):
                        for i in range(2):
                            mm = pe.matmul(PS[:, 6, h * TS:(h + 1) * TS], V[:, i, h, :], m_pt[:, i * MR + h * TS:i * MR + (h + 1) * TS],
                                           start=(i == 0), stop=(i == 1))
                    mm.then_inc(ring_used, 1)

        def mdec_dve(dve, chain, st, seg):
            chain(dve.memset(m_qb, 0.0))
            with dve.Fori(0, NB // SLOTS) as it:
                chain.enter(it, 3 * SLOTS)
                for j in range(SLOTS):
                    now = it * SLOTS + (st.base + j + 1)
                    cols = bass.ds(it * (SLOTS * TS) + (TP + j * TS), TS)
                    dve.tensor_copy(diag(m_qb, HM, TS), BIG[:, MQ:MQ + HM, cols]).then_inc(sem("mdec_q"), 1)
                    dve.wait_ge(sem("mdec_sc"), now)
                    chain(dve.tensor_copy(m_sm[0:MR, :], PS[0:MR, 4, 0:NM]))
                    chain(dve.tensor_reduce(s_mx[0:MR, 1:2], m_sm[0:MR, :], AXX, ALU.max))
                    dve.tensor_scalar(s_nm[0:MR, 1:2], s_mx[0:MR, 1:2], -1.0, None, ALU.mult).then_inc(sem("mdec_nm"), 1)
                    dve.wait_ge(sem("mdec_exp"), now)
                    chain(dve.reciprocal(s_r[0:MR, 1:2], s_l[0:MR, 1:2]))
                    dve.tensor_scalar(m_p[0:MR, :], m_p[0:MR, :], s_r[0:MR, 1:2], None, ALU.mult).then_inc(sem("mdec_p"), 1)
                    dve.wait_ge(sem("mdec_turned"), now)
                    dve.tensor_copy(m_pt, PS[:, 5, 0:2 * MR]).then_inc(sem("mdec_pt"), 1)
                    dve.wait_ge(ring_used, it * SLOTS + (seg.used(j)))
                    dve.tensor_copy(HT[:, 0:HM, cols], PS[:, 6, 0:MR].rearrange("p (h t) -> p h t", h=HM)).then_inc(sem("mdec_done"), 1)
            chain.leave(NB // SLOTS)

        (l_xin, l_xc, l_wa, l_wi, l_den, l_par, l_sp, l_s, l_zero) = carve([LW + 3, LW, P, P, LW, 320, 8 * 8, 8, NB])
        L_CONV, L_H0, L_CW, L_CB, L_BA, L_BI, L_LAM = 0, 192, 256, 288, 296, 304, 312
        l_r, l_i, l_a = (ODT[:, i * H * LW:(i + 1) * H * LW].rearrange("p (h t) -> p h t", h=H) for i in range(3))

        def seqs(ap):
            return ap.rearrange("p (b t) -> p b t", t=7)

        def lru_act(act, st, seg):
            lam = l_par[:, L_LAM:L_LAM + 8]
            act.wait_ge(tables_in, table_value["lru"])
            act.activation(l_sp[:, 0:8], lam, ACT.Abs).then_inc(sem("lru_abs"), 1)
            act.wait_ge(sem("lru_abs"), 1)
            act.activation(l_sp[:, 8:16], l_sp[:, 0:8], ACT.Exp, scale=-1.0).then_inc(sem("lru_e"), 1)
            act.wait_ge(ring_full[seg.slot(0)], seg.arrived(0))
            W = slot(seg, 0)[:, 0:2 * H * P]
            with act.Fori(0, H) as h:
                act.wait_ge(sem("lru_xc"), h + 1)
                act.activation(l_wa, row(W, h * P, P), ACT.Copy)
                act.activation(l_wi, row(W, h * P + H * P, P), ACT.Copy).then_inc(sem("lru_w"), 1)
                act.wait_ge(sem("lru_mm"), h + 1)
                act.activation(dyn(l_r, h, 0, LW), PS[:, 4, 0:LW], ACT.Sigmoid, bias=row(l_par, h + L_BA, 1))
                act.activation(dyn(l_i, h, 0, LW), PS[:, 5, 0:LW], ACT.Sigmoid, bias=row(l_par, h + L_BI, 1)).then_inc(sem("lru_sig"), 1)
            act.wait_ge(sem("lru_la"), 1 + H)
            act.activation(l_a[:, :, :], l_r[:, :, :], ACT.Exp).then_inc(sem("lru_exp"), 1)
            act.wait_ge(sem("lru_exp"), 1)
            act.activation(l_r[:, :, :], l_r[:, :, :], ACT.Tanh, scale=-1.0).then_inc(sem("lru_tanh"), 1)
            ly = BIG[:, LY:LY + H, :]
            act.activation(ly, ly, ACT.Gelu_apprx_tanh).then_inc(sem("lru_gelu"), 1)
            act.wait_ge(sem("lru_b2"), 1 + H)
            act.activation(l_r[:, :, :], l_r[:, :, :], ACT.Sqrt).then_inc(sem("lru_sqrt"), 1)

        def lru_pe(pe, st):
            with pe.Fori(0, H) as h:
                pe.wait_ge(sem("lru_w"), h + 1)
                pe.matmul(PS[:, 4, 0:LW], l_wa, l_xc, start=True, stop=True)
                pe.matmul(PS[:, 5, 0:LW], l_wi, l_xc, start=True, stop=True).then_inc(sem("lru_mm"), 1)

        def lru_dve(dve, chain, st):
            dve.wait_ge(tables_in, table_value["lru"])
            dve.wait_ge(sem("lru_e"), 1)
            c = [l_sp[:, i * 8:i * 8 + 8] for i in range(8)]
            chain(dve.tensor_scalar(c[2], c[1], 2.0, None, ALU.add))
            chain(dve.reciprocal(c[3], c[2]))
            chain(dve.tensor_tensor(c[4], c[1], c[3], ALU.mult))
            chain(dve.tensor_tensor(c[5], c[4], c[4], ALU.mult))
            chain(dve.tensor_scalar(c[6], c[5], 1.0 / 17, 1.0 / 15, ALU.mult, ALU.add))
            for n in (13, 11, 9, 7, 5, 3, 1):
                chain(dve.tensor_tensor(c[6], c[6], c[5], ALU.mult))
                chain(dve.tensor_scalar(c[6], c[6], 1.0 / n, None, ALU.add))
            chain(dve.tensor_tensor(c[6], c[6], c[4], ALU.mult))
            chain(dve.tensor_scalar(c[7], l_par[:, L_LAM:L_LAM + 8], -1.0, 0.0, ALU.mult, ALU.max))
            chain(dve.scalar_tensor_tensor(out=c[7], in0=c[6], scalar=2.0, in1=c[7], op0=ALU.mult, op1=ALU.add))
            chain(dve.tensor_scalar(l_s, c[7], -8.0, None, ALU.mult))
            chain(dve.memset(l_xin[:, 0:3], 0.0))
            chain(dve.memset(l_zero, 0.0))
            with dve.Fori(0, H) as h:
                chain.enter(h, 4)
                dve.wait_ge(sem("lru_la"), h + 1)
                dve.tensor_copy(l_xin[:, 3:3 + TP], dyn(BIG, h + LX, 0, TP))
                xs = seqs(l_xin[:, 3 + TP:3 + LW])
                dve.tensor_copy(xs[:, :, 0:3], row(l_par, h * 24, 24).rearrange("p (b t) -> p b t", t=3))
                chain(dve.tensor_copy(xs[:, :, 3:7], dyn(BIG, h + LX, TP, T).rearrange("p (b t) -> p b t", t=TS)))
                chain(dve.tensor_scalar(l_xc, l_xin[:, 0:LW], row(l_par, h * 4 + L_CW, 1), row(l_par, h + L_CB, 1), ALU.mult, ALU.add))
                for j in range(1, 4):
                    ins = dve.scalar_tensor_tensor(out=l_xc, in0=l_xin[:, j:j + LW], scalar=row(l_par, h * 4 + (L_CW + j), 1), in1=l_xc,
                                                   op0=ALU.mult, op1=ALU.add)
                    if j < 3:
                        chain(ins)
                ins.then_inc(sem("lru_xc"), 1)
                dve.wait_ge(sem("lru_xc"), h + 1)
                dve.wait_ge(sem("lru_sig"), h + 1)
                dve.tensor_tensor(dyn(l_i, h, 0, LW), dyn(l_i, h, 0, LW), l_xc, ALU.mult)
                dve.tensor_scalar(dyn(l_r, h, 0, LW), dyn(l_r, h, 0, LW), row(l_s, h, 1), None, ALU.mult).then_inc(sem("lru_la"), 1)
            chain.leave(H)
            dve.wait_ge(sem("lru_tanh"), 1)
            with dve.Fori(0, H) as h:
                chain.enter(h, 2)
                dve.wait_ge(sem("lru_b2"), h + 1)
                chain(dve.tensor_scalar(l_den, dyn(l_r, h, 0, LW), 1.0, None, ALU.add))
                chain(dve.reciprocal(l_den, l_den))
                dve.scalar_tensor_tensor(out=dyn(l_r, h, 0, LW), in0=dyn(l_r, h, 0, LW), scalar=2.0, in1=l_den,
                                         op0=ALU.mult, op1=ALU.mult).then_inc(sem("lru_b2"), 1)
            chain.leave(H)
            dve.wait_ge(sem("lru_sqrt"), 1)
            dve.wait_ge(sem("lru_gelu"), 1)
            with dve.Fori(0, H) as h:
                chain.enter(h, 3)
                chain(dve.tensor_tensor(dyn(l_i, h, 0, LW), dyn(l_i, h, 0, LW), dyn(l_r, h, 0, LW), ALU.mult))
                sa, si = seqs(dyn(l_a, h, TP, LW)), seqs(dyn(l_i, h, TP, LW))
                dve.tensor_copy(sa[:, :, 0:3], l_zero.unsqueeze(2).broadcast_to([P, NB, 3]))
                h0 = row(l_par, h * NB + L_H0, NB).unsqueeze(2).broadcast_to([P, NB, 3])
                chain(dve.tensor_copy(si[:, :, 0:3], h0))
                chain(dve.tensor_tensor_scan(dyn(l_r, h, 0, LW), dyn(l_a, h, 0, LW), dyn(l_i, h, 0, LW), 0.0, ALU.mult, ALU.add))
                dve.tensor_tensor(dyn(HT, h + H, 0, TP), dyn(l_r, h, 0, TP), dyn(BIG, h + LY, 0, TP), ALU.mult)
                dve.tensor_tensor(dyn(HT, h + H, TP, T).rearrange("p (b t) -> p b t", t=TS), seqs(dyn(l_r, h, TP, LW))[:, :, 3:7],
                                  dyn(BIG, h + LY, TP, T).rearrange("p (b t) -> p b t", t=TS), ALU.mult).then_inc(sem("lru_done"), 1)
            chain.leave(H)

        N_B, N_CB, N_CM, N_WB, N_NB, N_SEL = 0, 512, 520, 528, 528 + WIN, 528 + WIN + NB * NS
        N_PWT, N_PWV, N_PVT = N_SEL + NPG * NBS, N_SEL + NPG * NBS + P, N_SEL + NPG * NBS + 2 * P
        N_END = N_PVT + BLK
        n_v = ODT[:, N_END:N_END + 4 * 384].rearrange("p (i c) -> p i c", i=4)
        n_kc = ODT[:, N_END + 1536:N_END + 1544]
        n_vt = ODT[:, N_END + 1544:N_END + 1552]
        n_vc = ODT[:, N_END + 1552:N_END + 1552 + 256]
        (n_tmp,) = carve([2 * TP])
        v_tiles = [VSL, VSL + 1, VWN, VWN + 1]

        def gate_pe(pe):
            for i, w in ((0, P), (1, P), (2, NS)):
                mm = pe.matmul(PS[0:w, 4, i * 24:(i + 1) * 24], BIG[0:24, GT, i * P:i * P + w], IDENT[0:24, 0:24], start=True, stop=True)
            mm.then_inc(sem("gate_rows"), 1)
            for i in range(4):
                for c, w in ((0, P), (1, P), (2, NS)):
                    mm = pe.matmul(PS[0:w, i, c * P:(c + 1) * P], BIG[:, v_tiles[i], c * P:c * P + w], IDENT, start=True, stop=True)
            mm.then_inc(sem("nsv_rows"), 1)
            pe.wait_ge(sem("nsc_vt"), 1)
            for g in range(G):
                mm = pe.matmul(PS[0:NBP, 5, g * P:(g + 1) * P], n_vt[:, g * NBP:(g + 1) * NBP], IDENT, start=True, stop=True)
            mm.then_inc(sem("nsc_rows"), 1)

        def gate_act(act):
            act.wait_ge(sem("gate_rows"), 1)
            g = GROW[:, :, :].rearrange("p i c -> p (i c)")
            act.activation(g[:, 0:48], PS[:, 4, 0:48], ACT.Exp, scale=-1.0)
            act.activation(g[0:NS, 48:72], PS[0:NS, 4, 48:72], ACT.Exp, scale=-1.0).then_inc(sem("gate_exp"), 1)
            act.wait_ge(sem("nsv_rows"), 1)
            act.wait_ge(sem("lru_done"), H)
            act.wait_ge(outs_out, out_value["lru"])
            act.activation(n_v[:, :, 0:256], PS[:, 0:4, 0:256], ACT.Copy)
            act.activation(n_v[0:NS, :, 256:384], PS[0:NS, 0:4, 256:384], ACT.Copy)
            act.wait_ge(sem("nsc_rows"), 1)
            act.activation(n_vc[0:NBP, :], PS[0:NBP, 5, 0:256], ACT.Copy).then_inc(sem("nsc_done"), 1)

        def gate_dve(dve, chain):
            g = GROW[:, :, :].rearrange("p i c -> p (i c)")
            dve.wait_ge(sem("gate_exp"), 1)
            dve.tensor_scalar(g[:, 0:48], g[:, 0:48], 1.0, None, ALU.add)
            chain(dve.tensor_scalar(g[0:NS, 48:72], g[0:NS, 48:72], 1.0, None, ALU.add))
            dve.reciprocal(g[:, 0:48], g[:, 0:48])
            dve.reciprocal(g[0:NS, 48:72], g[0:NS, 48:72]).then_inc(sem("gates"), 1)
            dve.wait_ge(tables_in, table_value["nsa"])
            for n, (tile, pw, out) in enumerate(((KCM, N_PWT, n_kc), (VCM, N_PVT, n_vt))):
                w = ODT[:, pw:pw + BLK].unsqueeze(1).broadcast_to([P, NBP, BLK])
                for g_ in range(G):
                    t = n_tmp[:, g_ * TP:(g_ + 1) * TP].rearrange("p (b r) -> p b r", r=BLK)
                    chain(dve.tensor_tensor(t, BIG[:, tile + g_, 0:TP].rearrange("p (b r) -> p b r", r=BLK), w, ALU.mult))
                    ins = dve.tensor_reduce(out[:, g_ * NBP:(g_ + 1) * NBP], t, AXX, ALU.add)
                    if n == 1 and g_ == 1:
                        ins.then_inc(sem("nsc_vt"), 1)
                    else:
                        chain(ins)

        (n_q, n_sm, n_p, n_pt) = carve([T, 1032, 1032, 1280])
        n_mx, n_nm, n_l, n_r = (PMEM[:, 24 + i * 6:30 + i * 6] for i in range(4))

        def parts(buf):
            return [buf[:, (b * 2 + q) * TP:(b * 2 + q + 1) * TP] for b in range(2) for q in range(2)] + \
                   [buf[:, 1024 + q * NBP:1024 + (q + 1) * NBP] for q in range(2)]

        def nsp_act(act, g):
            with act.Fori(0, H // G) as it:
                now = it + (g * (H // G) + 1)
                act.wait_ge(sem("nsp_done"), now)
                act.activation(n_q, dyn(BIG, it + (NQ + g * (H // G))), ACT.Copy).then_inc(sem("nsp_q"), 1)
                act.wait_ge(sem("nsp_nm"), now)
                for i, (p, s) in enumerate(zip(parts(n_p), parts(n_sm))):
                    ins = act.activation(p, s, ACT.Exp, bias=n_nm[:, i:i + 1], accum_out=n_l[:, i:i + 1])
                ins.then_inc(sem("nsp_exp"), 1)
                act.wait_ge(sem("nsp_turned"), now)
                act.activation(n_pt[:, 0:512], PS[:, 7, 0:512], ACT.Copy)
                act.activation(n_pt[:, 512:1024], PS[:, 3, 0:512], ACT.Copy)
                act.activation(n_pt[0:NBP, 1024:1280], PS[0:NBP, 2, 0:256], ACT.Copy).then_inc(sem("nsp_pt"), 1)

        def nsp_pe(pe, g):
            with pe.Fori(0, H // G) as it:
                now = it + (g * (H // G) + 1)
                pe.wait_ge(sem("nsp_q"), now)
                for q in range(2):
                    qs = n_q[:, q * P:(q + 1) * P]
                    pe.matmul(PS[:, 4, q * TP:(q + 1) * TP], qs, BIG[:, KSL + g, 0:TP], start=True, stop=True)
                    pe.matmul(PS[:, 5, q * TP:(q + 1) * TP], qs, BIG[:, KWN + g, 0:TP], start=True, stop=True)
                    mm = pe.matmul(PS[:, 6, q * NBP:(q + 1) * NBP], qs, n_kc[:, g * NBP:(g + 1) * NBP], start=True, stop=True)
                mm.then_inc(sem("nsp_sc"), 1)
                pe.wait_ge(sem("nsp_p"), now)
                pp = parts(n_p)
                for b, bank in ((0, 7), (1, 3)):
                    for k in range(2):
                        for q in range(2):
                            pe.transpose(PS[:, bank, k * TP + q * P:k * TP + (q + 1) * P], pp[2 * b + q][:, k * P:(k + 1) * P], IDENT)
                for q in range(2):
                    mm = pe.matmul(PS[0:NBP, 2, q * P:(q + 1) * P], pp[4 + q], IDENT, start=True, stop=True)
                mm.then_inc(sem("nsp_turned"), 1)
                pe.wait_ge(sem("nsp_pt"), now)
                for b in range(2):
                    for k in range(2):
                        pe.matmul(PS[:, 1, 0:TP], n_v[:, 2 * b + g, k * P:(k + 1) * P], n_pt[:, b * 512 + k * TP:b * 512 + (k + 1) * TP],
                                  start=(b == 0 and k == 0), stop=False)
                pe.matmul(PS[:, 1, 0:TP], n_vc[0:NBP, g * P:(g + 1) * P], n_pt[0:NBP, 1024:1280], start=False, stop=True).then_inc(sem("nsp_o"), 1)

        def nsp_dve(dve, chain, g):
            with dve.Fori(0, H // G) as it:
                now = it + (g * (H // G) + 1)
                chain.enter(it, 10)
                dve.wait_ge(sem("nsp_sc"), now)
                dve.tensor_tensor(n_sm[:, 0:512], PS[:, 4, 0:512], ODT[:, N_B:N_B + 512], ALU.add)
                dve.tensor_tensor(n_sm[:, 512:1024], PS[:, 5, 0:512], ODT[:, N_B:N_B + 512], ALU.add)
                chain(dve.tensor_tensor(n_sm[:, 1024:1032], PS[:, 6, 0:8], ODT[:, N_CB:N_CB + 8], ALU.add))
                dve.tensor_reduce(n_mx[:, 0:4], n_sm[:, 0:1024].rearrange("p (i k) -> p i k", i=4), AXX, ALU.max)
                chain(dve.tensor_reduce(n_mx[:, 4:6], n_sm[:, 1024:1032].rearrange("p (i k) -> p i k", i=2), AXX, ALU.max))
                dve.tensor_scalar(n_nm, n_mx, -1.0, None, ALU.mult).then_inc(sem("nsp_nm"), 1)
                dve.wait_ge(sem("nsp_exp"), now)
                pc = n_p[:, 1024:1032]
                chain(dve.tensor_tensor(pc, pc, ODT[:, N_CM:N_CM + 8], ALU.mult))
                chain(dve.tensor_reduce(n_l[:, 4:6], pc.rearrange("p (q k) -> p q k", q=2), AXX, ALU.add))
                chain(dve.tensor_scalar(n_l, n_l, 1e-30, None, ALU.max))
                chain(dve.reciprocal(n_r, n_l))
                for b, c in ((0, 1), (1, 2), (2, 0)):
                    r2 = n_r[:, 2 * b:2 * b + 2].unsqueeze(2)
                    chain(dve.tensor_tensor(r2, r2, GROW[:, 0:2, bass.ds(it * 3 + (g * 12 + c), 1)], ALU.mult))
                for i, p in enumerate(parts(n_p)):
                    ins = dve.tensor_scalar(p, p, n_r[:, i:i + 1], None, ALU.mult)
                    if i == 0:
                        chain(ins)
                ins.then_inc(sem("nsp_p"), 1)
                dve.wait_ge(sem("nsp_o"), now)
                dve.tensor_copy(dyn(HT, it + g * (H // G), 0, TP), PS[:, 1, 0:TP]).then_inc(sem("nsp_done"), 1)
            chain.leave(H // G)

        C_SN, C_W, C_WN, C_C, C_END = 1024, 1152, 1664, 1792, 1920
        GR = NS // G
        (e_qb, e_sm, e_p, e_pt, e_kc, e_vc) = carve([G * 3 * GR, C_END, C_END, 15 * NS, G * NBS, 2 * P])
        E_BR = ((0, C_SN + NS), (C_W, C_WN + NS), (C_C, C_C + NBS))

        def nsd_act(act, st):
            with act.Fori(0, NB) as b:
                act.wait_ge(sem("nsd_nm"), b + 1)
                for i, (c0, c1) in enumerate(E_BR):
                    ins = act.activation(e_p[0:NS, c0:c1], e_sm[0:NS, c0:c1], ACT.Exp, bias=s_nm[:, i:i + 1], accum_out=s_l[:, i:i + 1])
                ins.then_inc(sem("nsd_exp"), 1)

        def nsd_pe(pe, st, seg):
            full = [ring_full[seg.slot(j)] for j in range(4)]
            with pe.Fori(0, NB) as b:
                pe.wait_ge(sem("nsd_prod"), b + 1)
                VC = slot(seg, 0)[:, 2048:4096].rearrange("p (i c) -> p i c", i=NPG)
                for i in range(NPG):
                    mm = pe.matmul(PS[0:NBS, 3, 0:256], ODT[:, N_SEL + i * NBS:N_SEL + (i + 1) * NBS], VC[:, i, :], start=(i == 0), stop=(i == NPG - 1))
                mm.then_inc(ring_used, 1)
                pe.wait_ge(full[1], seg.arrived(1, b))
                pe.wait_ge(full[3], seg.arrived(3, b))
                KS = slot(seg, 1)[:, 0:2048].rearrange("p (i g r) -> p g i r", i=NPG, g=G)
                KW = slot(seg, 3)[:, 0:1024].rearrange("p (g k) -> p g k", g=G)
                for g in range(G):
                    q = e_qb[:, g * NS:(g + 1) * NS]
                    f, l = g == 0, g == G - 1
                    pe.matmul(PS[0:NS, 6, 0:512], q, KW[:, g, :], start=f, stop=l)
                    pe.matmul(PS[0:NS, 7, 0:NS], q, BIG[:, KSL + g, TP:T], start=f, stop=True, skip_group_check=True)
                    pe.matmul(PS[0:NS, 7, NS:2 * NS], q, BIG[:, KWN + g, TP:T], start=False, stop=True, skip_group_check=True)
                    pe.matmul(PS[0:NS, 7, 2 * NS:2 * NS + NBS], q, e_kc[:, g * NBS:(g + 1) * NBS], start=False, stop=True, skip_group_check=True)
                    for half in range(2):
                        mm = pe.matmul(PS[0:NS, 4 + half, 0:512].rearrange("p (i r) -> p i r", i=4), q, KS[:, g, 4 * half:4 * half + 4, :], start=f, stop=l)
                mm.then_inc(ring_used, 1)
                pe.wait_ge(sem("nsd_p"), b + 1)
                for i in range(15):
                    mm = pe.matmul(PS[:, 2, i * NS:(i + 1) * NS], e_p[0:NS, i * P:(i + 1) * P], IDENT[0:NS, 0:NS], start=True, stop=True)
                mm.then_inc(sem("nsd_turned"), 1)
                pe.wait_ge(sem("nsd_pt"), b + 1)
                pe.wait_ge(full[2], seg.arrived(2, b))
                VS = slot(seg, 2)[:, 0:2048].rearrange("p (i g d) -> p i g d", i=NPG, g=G)
                VW_ = slot(seg, 3)[:, 1024:2048].rearrange("p (i g d) -> p i g d", i=4, g=G)
                for g in range(G):
                    out = PS[:, 1, g * GR:(g + 1) * GR]
                    for i in range(NPG):
                        mm = pe.matmul(out, VS[:, i, g, :], e_pt[:, i * NS + g * GR:i * NS + (g + 1) * GR], start=(g == 0 and i == 0), stop=True,
                                       skip_group_check=True)
                mm.then_inc(ring_used, 1)
                for g in range(G):
                    out = PS[:, 1, g * GR:(g + 1) * GR]

                    def pt(i, n=P):
                        return e_pt[0:n, i * NS + g * GR:i * NS + (g + 1) * GR]
                    pe.matmul(out, n_v[0:NS, g, 256:384], pt(8, NS), start=False, stop=True, skip_group_check=True)
                    pe.matmul(out, n_v[0:NS, 2 + g, 256:384], pt(13, NS), start=False, stop=True, skip_group_check=True)
                    pe.matmul(out, e_vc[0:NBS, g * P:(g + 1) * P], pt(14, NBS), start=False, stop=True, skip_group_check=True)
                    for i in range(4):
                        mm = pe.matmul(out, VW_[:, i, g, :], pt(9 + i), start=False, stop=True, skip_group_check=True)
                mm.then_inc(ring_used, 1)

        def nsd_dve(dve, chain, st, seg):
            chain(dve.memset(e_qb, 0.0))
            dve.memset(e_p, 0.0)
            chain(dve.memset(e_sm, 0.0))
            with dve.Fori(0, NB) as b:
                chain.enter(b, 8)
                dve.tensor_copy(diag(e_qb, G, GR).rearrange("p g (h t) -> p g h t", t=TS),
                                BIG[:, NQ:NQ + H, bass.ds(b * TS + TP, TS)].rearrange("p (g h) t -> p g h t", g=G))
                dve.wait_ge(ring_full[seg.slot(0)], seg.arrived(0, b))
                S = slot(seg, 0)
                KC = S[:, 0:2048].rearrange("p (i r) -> p i r", r=P)
                chain(dve.tensor_tensor(KC, KC, ODT[:, N_PWT:N_PWT + P].unsqueeze(1).broadcast_to([P, 16, P]), ALU.mult))
                for g in range(G):
                    chain(dve.tensor_reduce(e_kc[:, g * NBS:(g + 1) * NBS].rearrange("p (i x) -> p i x", x=2),
                                            S[:, 0:2048].rearrange("p (i g x r) -> p g i x r", i=NPG, g=G, r=BLK)[:, g], AXX, ALU.add))
                VC = S[:, 2048:4096].rearrange("p (i r) -> p i r", r=P)
                dve.tensor_tensor(VC, VC, ODT[:, N_PWV:N_PWV + P].unsqueeze(1).broadcast_to([P, 16, P]), ALU.mult).then_inc(sem("nsd_prod"), 1)
                dve.wait_ge(ring_used, seg.used(1, b))
                dve.tensor_copy(e_vc[0:NBS, :], PS[0:NBS, 3, 0:256])
                dve.tensor_copy(e_sm[0:NS, 0:1024], PS[0:NS, 4:6, :].rearrange("p a c -> p (a c)"))
                dve.tensor_tensor(e_sm[0:NS, C_W:C_W + WIN], PS[0:NS, 6, 0:WIN], ODT[0:NS, N_WB:N_WB + WIN], ALU.add)
                nb = ODT[0:NS, bass.ds(b * NS + N_NB, NS)]
                dve.tensor_tensor(e_sm[0:NS, C_SN:C_SN + NS], PS[0:NS, 7, 0:NS], nb, ALU.add)
                dve.tensor_tensor(e_sm[0:NS, C_WN:C_WN + NS], PS[0:NS, 7, NS:2 * NS], nb, ALU.add)
                chain(dve.tensor_copy(e_sm[0:NS, C_C:C_C + NBS], PS[0:NS, 7, 2 * NS:2 * NS + NBS]))
                for i, (c0, c1) in enumerate(E_BR):
                    ins = dve.tensor_reduce(s_mx[:, i:i + 1], e_sm[0:NS, c0:c1], AXX, ALU.max)
                chain(ins)
                dve.tensor_scalar(s_nm[:, 0:3], s_mx[:, 0:3], -1.0, None, ALU.mult).then_inc(sem("nsd_nm"), 1)
                dve.wait_ge(sem("nsd_exp"), b + 1)
                chain(dve.reciprocal(s_r[:, 0:3], s_l[:, 0:3]))
                chain(dve.tensor_tensor(s_r[:, 0:2], s_r[:, 0:2], GDEC[:, bass.ds(b * 3 + 1, 2)], ALU.mult))
                chain(dve.tensor_tensor(s_r[:, 2:3], s_r[:, 2:3], GDEC[:, bass.ds(b * 3, 1)], ALU.mult))
                for i, (c0, c1) in enumerate(E_BR):
                    ins = dve.tensor_scalar(e_p[0:NS, c0:c1], e_p[0:NS, c0:c1], s_r[:, i:i + 1], None, ALU.mult)
                ins.then_inc(sem("nsd_p"), 1)
                dve.wait_ge(sem("nsd_turned"), b + 1)
                dve.tensor_copy(e_pt, PS[:, 2, 0:15 * NS]).then_inc(sem("nsd_pt"), 1)
                dve.wait_ge(ring_used, seg.used(3, b))
                dve.tensor_copy(HT[:, 0:H, bass.ds(b * TS + TP, TS)],
                                PS[:, 1, 0:NS].rearrange("p (h t) -> p h t", h=H)).then_inc(sem("nsd_done"), 1)
            chain.leave(NB)

        def after_ret(eng):
            eng.wait_ge(sem("ret_done"), 1 + H)
            eng.wait_ge(sem("ret_saved"), 32 + 32 * H)

        def after_nsp(eng):
            eng.wait_ge(sem("nsp_done"), 1 + H)

        def after_used(eng, seg):
            eng.wait_ge(ring_used, seg.first + seg.units + SLOTS)

        def after_squares(eng, n):
            eng.wait_ge(squared_hid, 32 * (n + 1))

        block = ctx.enter_context(nc.Block())

        @block.sync
        def _(sp):
            for dst, name in ((X[:, :, :], "x"), (CORE[:, :], "core"), (GAIN[:, :], "gain"), (SCL[:, :], "scl"), (PT[:, :], "pages")):
                sp.dma_start(dst, a[name]).then_inc(consts_in, 16)

            def fill(seg, loads, loops):
                def unit(j, it):
                    copies = loads(j, it)
                    sp.wait_ge(ring_used, seg.may_fill(j, it))
                    for dst, src in copies:
                        sp.dma_start(dst, src).then_inc(ring_full[seg.slot(j)], 16)
                if loops:
                    with sp.Fori(0, loops) as it:
                        for j in range(SLOTS):
                            unit(j, it)
                for j in range(SLOTS * loops, seg.units):
                    unit(j, 0)

            def weights(seg, name, loops, n=SLOT, first=0):
                def loads(j, it):
                    if isinstance(it, int):
                        return [(slot(seg, j)[:, 0:n], a[name][first + j])]
                    return [(slot(seg, j)[:, 0:n], a[name][bass.ds(it * SLOTS + (first + j), 1)].rearrange("o p n -> (o p) n"))]
                fill(seg, loads, loops)

            def one(ap, i):
                return ap[bass.ds(i, 1)].rearrange("o p n -> (o p) n")

            sp.wait_ge(consts_in, 80)
            for s in layers:
                layer = layers.index(s)
                if layer == 0:
                    weights(s.w_in, "ev_w_in", 7)
                    seg = s.dil_seg

                    def dil_loads(j, b):
                        src = "dil_k" if j < 2 else "dil_v"
                        return [(slot(seg, j)[:, 0:4 * NKD], one(a[src], b * 2 + j % 2))]
                    fill(seg, dil_loads, NB)
                else:
                    weights(s.w_in, "od_w_in", 2)
                    weights(s.w_gt, "od_w_gt", 0, KT * 24)
                    weights(s.w_in2, "od_w_in", 2, first=10)
                    fill(s.lru_seg, lambda j, it: [(slot(s.lru_seg, 0)[:, 0:2 * H * P], a["lru_w"])], 0)
                    seg = s.nsd_seg

                    def nsd_loads(j, b):
                        S = slot(seg, j)
                        if j == 3:
                            return [(S[:, 0:1024], one(a["win_k"], b)), (S[:, 1024:2048], one(a["win_v"], b))]
                        out = []
                        for i in range(NPG):
                            page = sp.value_load(PT[0:1, bass.ds(b * NPG + i, 1)], min_val=0, max_val=a["cmp_k"].shape[0] - 1)
                            for n, name in enumerate((("cmp_k", "cmp_v"), ("slc_k",), ("slc_v",))[j]):
                                at = n * 2048 + i * 256
                                out.append((S[:, at:at + 256], one(a[name], page)))
                        return out
                    fill(seg, nsd_loads, NB)
                weights(s.w_out, f"w_out{layer}", 2)
                fill(s.mem_x, lambda j, it: [(slot(s.mem_x, 0), a["mem_x"])], 0)
                weights(s.w_kv, f"mem_w_kv{layer}", 1)
                weights(s.w_q, f"mem_w_q{layer}", 0)
                mseg = s.mdec_seg

                def mem_loads(j, it):
                    b = it * SLOTS + (layer * NB + j)
                    return [(slot(mseg, j)[:, 0:1024], one(a["mem_k"], b)), (slot(mseg, j)[:, 1024:2048], one(a["mem_v"], b))]
                fill(mseg, mem_loads, NB // SLOTS)
                weights(s.w_o, f"mem_w_o{layer}", 2, 1024)
                weights(s.w_1, f"mlp_w1_{layer}", 8)
                weights(s.w_2, f"mlp_w2_{layer}", 8)

        @block.gpsimd
        def _(pool):
            pool.dma_start(EVT[:, 0:RTAB1], a["ret_tab"][:, 0:RTAB1]).then_inc(tables_in, 16)
            after_pairs(pool, ev.pairs_in)
            pool.dma_start(r_tab2[:, 0:2 * H * NS], a["ret_tab"][:, RTAB1:RTAB1 + 2 * H * NS]).then_inc(tables_in, 16)
            after_ret(pool)
            pool.dma_start(EVT[:, 0:D_BN + NB * NS], a["dil_tab"]).then_inc(tables_in, 16)
            after_prep(pool, ev.prep[-1][0])
            pool.dma_start(o["dil_kv"], BIG[:, DK:DK + 2 * H, :]).then_inc(outs_out, 16)
            after_prep(pool, ev.prep_k[0])
            pool.dma_start(o["mem_kv0"], BIG[:, 0:2 * HM, 0:NM]).then_inc(outs_out, 16)
            after_pairs(pool, od.pairs_in2)
            pool.dma_start(l_par, a["lru_par"]).then_inc(tables_in, 16)
            pool.dma_start(o["lx"], BIG[:, LX:LX + H, :]).then_inc(outs_out, 16)
            pool.wait_ge(sem("lru_done"), H)
            pool.dma_start(o["lru_h"], l_r[:, :, :]).then_inc(outs_out, 16)
            pool.wait_ge(outs_out, out_value["lru"])
            pool.dma_start(ODT[:, 0:N_PWT], a["nsa_tab"]).then_inc(tables_in, 16)
            pool.dma_start(ODT[:, N_PWT:N_END], a["pw"]).then_inc(tables_in, 16)
            pool.wait_ge(sem("gates"), 1)
            pool.dma_start(scratch, GROW[0:NS, 2, :]).then_inc(sem("gates_out"), 16)
            pool.wait_ge(sem("gates_out"), 16)
            for h in range(H):
                pool.dma_start(GDEC[h * TS:(h + 1) * TS, :].rearrange("t (b j) -> t b j", j=3),
                               scratch.rearrange("(b t) c -> t b c", t=TS)[:, :, 3 * h:3 * h + 3]).then_inc(sem("gates_in"), 16)
            after_prep(pool, od.prep[-1][0])
            pool.dma_start(o["nsa_kv"], BIG[:, KCM:KCM + 12, :]).then_inc(outs_out, 16)
            after_prep(pool, od.prep_k[0])
            pool.dma_start(o["mem_kv1"], BIG[:, 0:2 * HM, 0:NM]).then_inc(outs_out, 16)
            after_pairs(pool, od.pairs_2)
            pool.dma_start(o["y"], X[:, :, :]).then_inc(outs_out, 16)
            pool.wait_ge(outs_out, 112)

        @block.tensor
        def _(pe):
            pe.sem_inc(ring_used, SLOTS)
            pe.sem_inc(pair_free, 2)
            pe.sem_inc(sem("ret_saved"), 32)
            pe.wait_ge(consts_in, 80)
            for s in layers:
                layer = layers.index(s)
                norm_pe(pe, s.n_mix, T)
                after_norm(pe, s.n_mix)
                if layer == 0:
                    lin_pe(pe, s.w_in, s.pairs_in, HT, KT, T, 7)
                    ret_pe(pe, s.ret)
                    after_ret(pe)
                    for st, tile0, gain, scl in s.prep:
                        prep_pe(pe, st, T, True)
                        after_prep(pe, st)
                    att_pe(pe, s.att, DK, True)
                    after_att(pe, s.att)
                    dil_pe(pe, s.dil, s.dil_seg)
                    pe.wait_ge(sem("dil_done"), NB)
                else:
                    lin_pe(pe, s.w_in, s.pairs_in, HT, KT, T, 2, width=256)
                    lin_pe(pe, s.w_gt, s.pair_gt, HT, KT, T, 0, width=24)
                    lin_pe(pe, s.w_in2, s.pairs_in2, HT, KT, T, 2)
                    after_pairs(pe, s.pairs_in2)
                    lru_pe(pe, s.lru)
                    pe.wait_ge(sem("lru_done"), H)
                    pe.sem_inc(ring_used, 1)
                    for st, tile0, gain, scl in s.prep:
                        prep_pe(pe, st, T, True)
                        after_prep(pe, st)
                    gate_pe(pe)
                    pe.wait_ge(sem("nsc_done"), 1)
                    for g in range(G):
                        nsp_pe(pe, g)
                    after_nsp(pe)
                    nsd_pe(pe, s.nsd, s.nsd_seg)
                    pe.wait_ge(sem("nsd_done"), NB)
                lin_pe(pe, s.w_out, s.pairs_out, HT, KT, T, 2)
                norm_pe(pe, s.n_kv, NM)
                after_norm(pe, s.n_kv)
                pe.sem_inc(ring_used, 1)
                lin_pe(pe, s.w_kv, s.pairs_kv, HT, KT, NM, 1)
                after_pairs(pe, s.pairs_kv)
                prep_pe(pe, s.prep_k[0], NM, False)
                after_prep(pe, s.prep_k[0])
                norm_pe(pe, s.n_mem, T)
                after_norm(pe, s.n_mem)
                lin_pe(pe, s.w_q, s.pairs_q, HT, KT, T, 0)
                after_pairs(pe, s.pairs_q)
                prep_pe(pe, s.prep_q[0], T, False)
                after_prep(pe, s.prep_q[0])
                att_pe(pe, s.matt, MK, False)
                after_att(pe, s.matt)
                mdec_pe(pe, s.mdec, s.mdec_seg)
                pe.wait_ge(sem("mdec_done"), s.mdec.end)
                lin_pe(pe, s.w_o, s.pairs_o, HT, HM, T, 2)
                norm_pe(pe, s.n_mlp, T)
                after_norm(pe, s.n_mlp)
                lin_pe(pe, s.w_1, s.pairs_1, HT, KT, T, 8)
                after_squares(pe, layer)
                w2_pe(pe, s.w_2, s.pairs_2)

        @block.scalar
        def _(act):
            act.wait_ge(consts_in, 80)
            for s in layers:
                layer = layers.index(s)
                norm_act(act, s.n_mix, X, T)
                if layer == 0:
                    lin_act(act, s.w_in, s.pairs_in, BIG, 0, T, 7)
                    ret_act(act, s.ret)
                    after_ret(act)
                    for st, tile0, gain, scl in s.prep:
                        prep_act(act, st, tile0, T)
                        after_prep(act, st)
                    att_act(act, s.att, DQ, DV, True)
                    after_att(act, s.att)
                    dil_act(act, s.dil)
                    act.wait_ge(sem("dil_done"), NB)
                else:
                    lin_act(act, s.w_in, s.pairs_in, BIG, 0, T, 2)
                    lin_act(act, s.w_gt, s.pair_gt, BIG, GT, T, 0, width=24)
                    lin_act(act, s.w_in2, s.pairs_in2, BIG, LX, T, 2)
                    after_pairs(act, s.pairs_in2)
                    lru_act(act, s.lru, s.lru_seg)
                    act.wait_ge(sem("lru_done"), H)
                    for st, tile0, gain, scl in s.prep:
                        prep_act(act, st, tile0, T)
                        after_prep(act, st)
                    gate_act(act)
                    for g in range(G):
                        nsp_act(act, g)
                    after_nsp(act)
                    nsd_act(act, s.nsd)
                    act.wait_ge(sem("nsd_done"), NB)
                act.wait_ge(ring_full[s.mem_x.slot(0)], s.mem_x.arrived(0))
                norm_act(act, s.n_kv, slot(s.mem_x, 0).rearrange("p (k t) -> p k t", t=NM), NM)
                act.wait_ge(outs_out, out_value["nsa" if layer else "dil"])
                lin_act(act, s.w_kv, s.pairs_kv, BIG, 0, NM, 1)
                after_pairs(act, s.pairs_kv)
                prep_act(act, s.prep_k[0], MK, NM)
                after_prep(act, s.prep_k[0])
                after_pairs(act, s.pairs_out)
                norm_act(act, s.n_mem, X, T)
                lin_act(act, s.w_q, s.pairs_q, BIG, MQ, T, 0)
                after_pairs(act, s.pairs_q)
                prep_act(act, s.prep_q[0], MQ, T)
                after_prep(act, s.prep_q[0])
                att_act(act, s.matt, MQ, MV, False)
                after_att(act, s.matt)
                mdec_act(act, s.mdec)
                after_pairs(act, s.pairs_o)
                norm_act(act, s.n_mlp, X, T)
                act.wait_ge(outs_out, out_value[f"mem{layer}"])
                lin_act(act, s.w_1, s.pairs_1, BIG, 0, T, 8, ACT.Relu)
                after_pairs(act, s.pairs_2)

        @block.vector
        def _(dve):
            chain = Chain(dve, sem("dve_chain"))
            for name in ("prep_done", "ret_done", "att_done", "nsp_done", "lru_la", "lru_b2"):
                dve.sem_inc(sem(name), 1)
            dve.wait_ge(consts_in, 80)
            for s in layers:
                layer = layers.index(s)
                norm_dve(dve, s.n_mix, X, GN_MIX + KT * layer, T)
                if layer == 0:
                    ret_dve(dve, chain, s.ret)
                    after_ret(dve)
                    for st, tile0, gain, scl in s.prep:
                        prep_dve(dve, chain, st, tile0, gain, scl, T, True)
                        after_prep(dve, st)
                    dve.wait_ge(tables_in, table_value["dil"])
                    att_dve(dve, chain, s.att, EVT[:, D_B:D_B + 512], H)
                    after_att(dve, s.att)
                    dil_dve(dve, chain, s.dil, s.dil_seg)
                else:
                    after_pairs(dve, s.pairs_in2)
                    lru_dve(dve, chain, s.lru)
                    dve.wait_ge(sem("lru_done"), H)
                    for st, tile0, gain, scl in s.prep:
                        prep_dve(dve, chain, st, tile0, gain, scl, T, True)
                        after_prep(dve, st)
                    gate_dve(dve, chain)
                    dve.wait_ge(sem("nsc_done"), 1)
                    for g in range(G):
                        nsp_dve(dve, chain, g)
                    after_nsp(dve)
                    dve.wait_ge(sem("gates_in"), 16 * H)
                    nsd_dve(dve, chain, s.nsd, s.nsd_seg)
                resid_dve(dve, s.w_out, s.pairs_out, 1, 2)
                after_used(dve, s.w_out)
                norm_dve(dve, s.n_kv, slot(s.mem_x, 0).rearrange("p (k t) -> p k t", t=NM), GN_KV + KT * layer, NM)
                after_pairs(dve, s.pairs_kv)
                prep_dve(dve, chain, *s.prep_k, NM, False)
                norm_dve(dve, s.n_mem, X, GN_MEM + KT * layer, T)
                after_pairs(dve, s.pairs_q)
                prep_dve(dve, chain, *s.prep_q, T, False)
                att_dve(dve, chain, s.matt, None, 0)
                after_att(dve, s.matt)
                mdec_dve(dve, chain, s.mdec, s.mdec_seg)
                resid_dve(dve, s.w_o, s.pairs_o, 1, 2)
                norm_dve(dve, s.n_mlp, X, GN_MLP + KT * layer, T)
                square_dve(dve, s.pairs_1)
                resid_dve(dve, s.w_2, s.pairs_2, 4, 4)


def tiles(w):
    k, n = w.shape
    return w.reshape(k // P, P, n // 256, 256).transpose(2, 1, 0, 3).reshape(n // 256, P, -1)


def columns(v):
    return v.reshape(-1, P).T


def layout(i):
    xs = np.concatenate([i["x_prompt"][0], i["x_sample"].reshape(NS, D)], 0)
    w_od = i["od_w_in"][0]
    nq = H * HD + 6 * G * HD
    rows = dilated_rows()
    kd = i["cache_dil_k"][0][:, rows].reshape(NB, NKD, 2, 4, HD).transpose(0, 2, 4, 3, 1)
    vd = i["cache_dil_v"][0][:, rows].reshape(NB, NKD // P, P, 2, 4, HD).transpose(0, 3, 2, 1, 4, 5)
    pool_k = lambda c: c[0].transpose(0, 3, 2, 1).reshape(-1, P, G * PAGE)
    pool_v = lambda c: c[0].reshape(-1, P, G * HD)
    gains = [columns(g) for name in ("norm_mix_g", "norm_mem_g", "norm_mlp_g", "mem_norm_g") for g in i[name]]
    rep = lambda v, n: np.repeat(v.reshape(P, 1), n, 1)
    kg = i["nsa_k_norm_g"][0]
    gains += [rep(i["dil_q_norm_g"][0], H), rep(i["dil_k_norm_g"][0], H), rep(i["nsa_q_norm_g"][0], H), rep(kg[0], G), rep(kg[1], G),
              rep(kg[2], G), rep(i["mem_q_norm_g"][0], HM), rep(i["mem_q_norm_g"][1], HM), rep(i["mem_k_norm_g"][0], HM),
              rep(i["mem_k_norm_g"][1], HM), columns(i["ret_gn_g"][0].reshape(-1))]
    pwk, pwv = i["nsa_pw_k"][0], i["nsa_pw_v"][0]
    par = [i["state_lru_conv"][0].reshape(NB, 3, H, P).transpose(3, 2, 0, 1).reshape(P, -1),
           i["state_lru_h"][0].reshape(NB, H, P).transpose(2, 1, 0).reshape(P, -1),
           i["lru_conv_w"][0].reshape(4, H, P).transpose(2, 1, 0).reshape(P, -1)]
    par += [columns(i[n][0]) for n in ("lru_conv_b", "lru_b_a", "lru_b_i", "lru_lambda")]
    out = {
        "x": xs.reshape(T, KT, P).transpose(2, 1, 0),
        "core": core_table(), "scl": scales_table(), "gain": np.concatenate(gains, 1),
        "pages": i["page_table"].reshape(1, -1),
        "ret_tab": retention_table(), "dil_tab": dilated_table(), "nsa_tab": sparse_table(),
        "pw": np.concatenate([pwk.T, pwk.T, np.concatenate([pwv, pwv], 0), pwv.T], 1),
        "lru_par": np.concatenate(par, 1),
        "lru_w": np.concatenate([i[n][0].transpose(1, 0, 2).reshape(P, -1) for n in ("lru_w_a", "lru_w_i")], 1),
        "state_ret": i["state_ret"][0].transpose(1, 2, 0, 3).reshape(H, P, -1),
        "dil_k": kd.reshape(2 * NB, P, -1), "dil_v": vd.reshape(2 * NB, P, -1),
        "cmp_k": pool_k(i["cache_nsa_cmp_k"]), "cmp_v": pool_v(i["cache_nsa_cmp_v"]),
        "slc_k": pool_k(i["cache_nsa_slc_k"]), "slc_v": pool_v(i["cache_nsa_slc_v"]),
        "win_k": i["cache_nsa_win_k"][0].transpose(0, 3, 2, 1).reshape(NB, P, -1),
        "win_v": i["cache_nsa_win_v"][0].reshape(NB, 4, P, G * HD).transpose(0, 2, 1, 3).reshape(NB, P, -1),
        "mem_k": i["cache_mem_k"].transpose(0, 1, 4, 3, 2).reshape(2 * NB, P, -1),
        "mem_v": i["cache_mem_v"].reshape(2 * NB, 2, P, HM * HD).transpose(0, 2, 1, 3).reshape(2 * NB, P, -1),
        "mem_x": i["mem_prompt"][0].reshape(NM, KT, P).transpose(2, 1, 0).reshape(P, -1),
        "ev_w_in": tiles(i["ev_w_in"][0]),
        "od_w_in": tiles(np.concatenate([w_od[:, :nq], w_od[:, nq + 3 * H:]], 1)),
        "od_w_gt": w_od[:, nq:nq + 3 * H].reshape(KT, P, 3 * H).transpose(1, 0, 2).reshape(1, P, -1),
        "w_out0": tiles(i["ev_w_out"][0]), "w_out1": tiles(i["od_w_out"][0]),
    }
    for l in range(2):
        out[f"mem_w_kv{l}"] = np.concatenate([tiles(i["mem_w_k"][l]), tiles(i["mem_w_v"][l])], 0)
        out[f"mem_w_q{l}"] = tiles(i["mem_w_q"][l])
        out[f"mem_w_o{l}"] = tiles(i["mem_w_o"][l])
        out[f"mlp_w1_{l}"] = tiles(i["mlp_w1"][l])
        w2 = i["mlp_w2"][l].reshape(4, KT, P, D // 256, 256)
        out[f"mlp_w2_{l}"] = w2.transpose(3, 0, 2, 1, 4).reshape(-1, P, SLOT)
    return {n: np.ascontiguousarray(v) for n, v in out.items()}


_OUTS = {"y": (P, KT, T), "ret_s": (H, P, NB * P), "ret_p": (H, P, P), "dil_kv": (P, 2 * H, T), "nsa_kv": (P, 12, T), "lx": (P, H, T),
         "lru_h": (P, H, LW), "mem_kv0": (P, 2 * HM, NM), "mem_kv1": (P, 2 * HM, NM)}


def kernel(**inputs):
    import concourse.bacc as bacc
    from concourse.bass_utils import run_bass_kernel_spmd

    nc = bacc.Bacc("TRN2", target_bir_lowering=False, num_devices=1)
    arrays = {f"in_{n}": v for n, v in layout({k: np.asarray(v) for k, v in inputs.items()}).items()}
    a = {n[3:]: nc.dram_tensor(n, v.shape, mybir.dt.from_np(v.dtype), kind="ExternalInput").ap() for n, v in arrays.items()}
    o = {n: nc.dram_tensor(f"out_{n}", s, F32, kind="ExternalOutput").ap() for n, s in _OUTS.items()}
    scratch = nc.dram_tensor("gate_scratch", (NS, 3 * H), F32).ap()
    build(nc, a, o, scratch)
    r = run_bass_kernel_spmd(nc, [arrays], core_ids=[0]).results[0]
    r = {n: np.asarray(r[f"out_{n}"]) for n in _OUTS}

    def heads(x, first, n, cols, lead):
        return np.ascontiguousarray(x[:, first:first + n, cols].transpose(2, 1, 0)).reshape(lead + (n, P))

    prompt, sample = slice(0, TP), slice(TP, T)
    y = r["y"].transpose(2, 1, 0).reshape(T, D)
    out = [y[:TP].reshape(1, TP, D), y[TP:].reshape(NB, TS, D),
           r["ret_p"].reshape(1, 1, H, P, P), r["ret_s"].reshape(H, P, NB, P).transpose(2, 0, 1, 3)[None]]
    for cols, lead in ((prompt, (1, 1, TP)), (sample, (1, NB, TS))):
        out += [heads(r["dil_kv"], 0, H, cols, lead), heads(r["dil_kv"], H, H, cols, lead)]
    for first in (0, 4, 8):
        for cols, lead in ((prompt, (1, 1, TP)), (sample, (1, NB, TS))):
            out += [heads(r["nsa_kv"], first, G, cols, lead), heads(r["nsa_kv"], first + G, G, cols, lead)]
    h = r["lru_h"]
    out += [h[:, :, TP - 1].T.reshape(1, 1, -1), h[:, :, TP:].reshape(P, H, NB, 7)[..., 6].transpose(2, 1, 0).reshape(1, NB, -1)]
    lx = r["lx"]
    out += [lx[:, :, TP - 3:TP].transpose(2, 1, 0).reshape(1, 1, 3, -1),
            lx[:, :, TP:].reshape(P, H, NB, TS)[..., 1:].transpose(2, 3, 1, 0).reshape(1, NB, 3, -1)]
    mem = [r["mem_kv0"], r["mem_kv1"]]
    out += [np.stack([heads(m, f, HM, slice(0, NM), (1, NM)) for m in mem]) for f in (0, HM)]
    return tuple(np.ascontiguousarray(v) for v in out)
```

```python
from contextlib import ExitStack

import numpy as np
import concourse.bass as bass
from concourse import mybir

F32 = mybir.dt.float32
F32R = mybir.dt.float32r
I32 = mybir.dt.int32
ALU = mybir.AluOpType
ACT = mybir.ActivationFunctionType
AXX = mybir.AxisListType.X

P = 128
D = 2048
KT = D // P
TP, NB, TS = 256, 8, 4
NS = NB * TS
T = TP + NS
HD = 128
H = 8
G = 2
HM = 4
NM = 256
PAST = 1024
PAGE = 128
NPG = PAST // PAGE
BLK = 64
NBP = TP // BLK
NBS = PAST // BLK
WIN = 512
FF = 4 * D
EPS = 1e-6
SCALE = HD ** -0.5
SLOT = 2048
SLOTS = 4
CH = 1024
CHUNKS = 4
ZF = 2 * KT * T
NKD = 640
LW = TP + 7 * NB
NEG = -1e30
PAD = 128

RQ, RK, RV, RG, DQ, DK, DV, EV_TILES = 0, 8, 16, 24, 32, 40, 48, 56
NQ, KCM, VCM, KSL, VSL, KWN, VWN, LX, LY, GT, OD_TILES = 0, 8, 10, 12, 14, 16, 18, 20, 28, 36, 37
BIG_TILES = 57
MK, MV, MQ = 0, 4, 8
GN_MIX, GN_MEM, GN_MLP, GN_KV = 0, 32, 64, 96
G_EV, G_OD, G_MQ, G_MK, G_RET, G_END = 128, 144, 158, 166, 174, 182
S_EV, S_OD, S_MQ, S_MK, S_END = 0, 16, 30, 38, 46


def log_decay():
    return np.log1p(-np.exp2(-5.0 - np.arange(H))).astype(np.float64)


def positions():
    return np.concatenate([np.arange(TP), np.tile(PAST + np.arange(TS), NB)]).astype(np.float32)


def rope_tables(n_rot, theta):
    half = n_rot // 2
    inv = (1.0 / (np.float32(theta) ** (np.arange(half, dtype=np.float32) * np.float32(2.0 / n_rot)))).astype(np.float32)
    ang = (positions()[:, None] * inv[None, :]).astype(np.float32).astype(np.float64)
    cos, sin = np.ones((HD, T)), np.zeros((HD, T))
    cos[:half] = cos[half:n_rot] = np.cos(ang).T
    sin[:half] = sin[half:n_rot] = np.sin(ang).T
    rot = np.zeros((HD, HD))
    for i in range(half):
        rot[i, i + half] = -1.0
        rot[i + half, i] = 1.0
    return cos, sin, rot.T


def core_table():
    r1 = rope_tables(HD, 10000.0)[2]
    c2, s2, r2 = rope_tables(HD // 4, 500000.0)
    return np.concatenate([np.eye(P), np.ones((P, P)), r1, r2, c2, s2], 1).astype(np.float32)


def scales_table():
    s = np.ones((P, S_END + 1))
    s[:, S_END] = EPS
    s[:, S_EV:S_EV + H] = SCALE
    s[:, S_OD:S_OD + H] = SCALE
    s[:, S_MQ:S_MQ + 2 * HM] = SCALE
    return s.astype(np.float32)


def retention_table():
    lg = log_decay()
    j, i = np.arange(P)[:, None], np.arange(TP)[None, :]
    dec = np.where(i >= j, np.exp(np.maximum(i - j, 0)[None] * lg[:, None, None]), 0.0)
    dec = dec.transpose(1, 0, 2).reshape(P, H * TP)
    n = np.arange(NS)
    same = (n[:, None] // TS == n[None, :] // TS)
    dif = (n[None, :] % TS) - (n[:, None] % TS)
    ds_ = np.where(same & (dif >= 0), np.exp(np.maximum(dif, 0)[None] * lg[:, None, None]), 0.0)
    decs = np.zeros((P, H, NS))
    decs[:NS] = ds_.transpose(1, 0, 2)
    qd = np.broadcast_to(np.exp((n % TS + 1.0)[None, :] * lg[:, None])[None], (P, H, NS))
    kd = np.stack([np.exp((TP - 1.0 - np.arange(P))[:, None] * lg), np.exp((P - 1.0 - np.arange(P))[:, None] * lg)], 2)
    g4 = np.broadcast_to(np.exp(TS * lg)[None], (P, H))
    mb = np.zeros((P, H, NB))
    for r in range(NS):
        mb[r, :, r // TS] = np.exp((TS - 1.0 - r % TS) * lg)
    cos, sin, _ = rope_tables(HD, 10000.0)
    parts = [dec, kd.reshape(P, -1), g4, mb.reshape(P, -1), decs.reshape(P, -1), qd.reshape(P, -1), cos, sin]
    return np.concatenate(parts, 1).astype(np.float32)


def dilated_multiplicity(dist):
    n = np.zeros(dist.shape)
    for window, dil in ((128, 1), (512, 4), (2048, 16)):
        n += (dist >= 0) & (dist <= window) & (dist % dil == 0)
    return n


def dilated_rows():
    far = np.arange(512).reshape(32, 16)[:, :TS].ravel()
    return np.concatenate([far, 512 + np.arange(512)])


def log_mult(n):
    return np.where(n > 0, np.log(np.maximum(n, 1)), NEG)


def new_key_bias():
    r, b, k = np.arange(P)[:, None, None], np.arange(NB)[None, :, None], np.arange(NS)[None, None, :]
    return (r % TS) - (k % TS), (k // TS == b)


def dilated_table():
    q, k = np.arange(TP), np.arange(TP)
    bias = log_mult(dilated_multiplicity(q[:, None] - k[None, :])).reshape(2, P, TP).transpose(1, 0, 2).reshape(P, -1)
    qs = PAST + np.arange(P) % TS
    biasd = log_mult(dilated_multiplicity(qs[:, None] - dilated_rows()[None, :]))
    dist, own = new_key_bias()
    biasn = np.where(own, log_mult(dilated_multiplicity(dist)), NEG).reshape(P, -1)
    return np.concatenate([bias, biasd, biasn], 1).astype(np.float32)


def sparse_table():
    q, k = np.arange(TP), np.arange(TP)
    bias = np.where(q[:, None] >= k[None, :], 0.0, NEG).reshape(2, P, TP).transpose(1, 0, 2).reshape(P, -1)
    ok = (np.arange(NBP)[None, :] + 1) * BLK - 1 <= q[:, None]
    cb = np.where(ok, 0.0, NEG).reshape(2, P, NBP).transpose(1, 0, 2).reshape(P, -1)
    cm = ok.astype(float).reshape(2, P, NBP).transpose(1, 0, 2).reshape(P, -1)
    qs = PAST + np.arange(P) % TS
    kw = PAST - WIN + np.arange(WIN)
    wb = np.where(qs[:, None] - kw[None, :] < WIN, 0.0, NEG)
    dist, own = new_key_bias()
    nb = np.where(own & (dist >= 0), 0.0, NEG).reshape(P, -1)
    sel = np.zeros((P, NPG, NBS))
    for p in range(NPG):
        sel[:BLK, p, 2 * p] = 1.0
        sel[BLK:, p, 2 * p + 1] = 1.0
    return np.concatenate([bias, cb, cm, wb, nb, sel.reshape(P, -1)], 1).astype(np.float32)


class Ring:

    def __init__(self):
        self.unit = 0
        self.full = [0] * SLOTS

    def segment(self, units, dmas=(1,) * SLOTS):
        seg = Segment(self.unit, tuple(self.full), units, dmas)
        for u in range(units):
            self.full[(self.unit + u) % SLOTS] += 16 * dmas[u % len(dmas)]
        self.unit += units
        return seg


class Segment:

    def __init__(self, first, full, units, dmas):
        self.first, self.full, self.units, self.dmas, self.round = first, full, units, dmas, len(dmas)

    def slot(self, j):
        return (self.first + j) % SLOTS

    def arrived(self, j, it=0):
        in_round = sum(self.dmas[j % SLOTS::SLOTS])
        whole, rest = divmod(j, self.round)
        done = sum(self.dmas[j % SLOTS:rest + 1:SLOTS])
        return it * (16 * in_round) + (16 * (whole * in_round + done) + self.full[self.slot(j)])

    def may_fill(self, j, it=0):
        return it * self.round + (self.first + j + 1)

    def used(self, j, it=0):
        return it * self.round + (self.first + j + 1 + SLOTS)


class Stage:

    def __init__(self, kind, base, rounds):
        self.kind, self.base, self.rounds = kind, base, rounds

    def at(self, it=0):
        return it + (self.base + 1)

    @property
    def end(self):
        return self.base + self.rounds


class Linear:

    chunks = tiles = halves = 0

    def __init__(self, ring, units, kt=KT):
        self.seg, self.kt, self.n = ring.segment(units), kt, units
        self.per = 2 if kt == KT else 1
        self.chunk, self.tile, self.half = Linear.chunks, Linear.tiles, Linear.halves
        Linear.chunks += self.per * units
        Linear.tiles += units
        Linear.halves += (self.per - 1) * units
        self.ahead = CHUNKS // self.per

    @property
    def end(self):
        return 4 + self.tile + self.n


class Chain:

    def __init__(self, eng, sem):
        self.eng, self.sem, self.base, self.k, self.it, self.per = eng, sem, 0, 0, 0, 0

    def __call__(self, ins):
        self.k += 1
        ins.then_inc(self.sem, 1)
        self.eng.wait_ge(self.sem, self.it * self.per + (self.base + self.k))

    def enter(self, it, per):
        self.base, self.k, self.it, self.per = self.base + self.k, 0, it, per

    def leave(self, rounds):
        assert self.k == self.per, (self.k, self.per)
        self.base, self.k, self.it, self.per = self.base + rounds * self.per, 0, 0, 0


def build(nc, a, o, scratch):
    ring = Ring()
    Linear.chunks = Linear.tiles = Linear.halves = 0
    rounds = {}

    def stage(kind, n):
        st = Stage(kind, rounds.get(kind, 0), n)
        rounds[kind] = st.end
        return st

    class L:
        pass

    layers = []
    for layer in range(2):
        s = L()
        s.n_mix = stage("norm", 1)
        if layer == 0:
            s.w_in = Linear(ring, EV_TILES)
            s.ret = stage("ret", H)
            s.prep = [(stage("prep", 16), DQ, G_EV)]
            s.att = stage("att", H)
            s.dil = stage("dil", NB)
            s.dil_first = ring.segment(4)
            s.dil_seg = ring.segment(8 * (NB - 1), (1,) * 8)
            s.dil_last = ring.segment(4)
        else:
            s.w_in = Linear(ring, OD_TILES)
            s.lru_seg = ring.segment(1)
            s.lru = stage("lru", H)
            s.prep = [(stage("prep", 10), NQ, G_OD), (stage("prep", 2), KSL, G_OD + 10),
                      (stage("prep", 2), KWN, G_OD + 12)]
            s.att = stage("nsp", H)
            s.nsd = stage("nsd", NB)
            s.nsd_first = ring.segment(5, (8, 8, 4, 4, 1))
            s.nsd_seg = ring.segment(8 * (NB - 1), (8, 8, 4, 4, 1, 4, 4, 1))
            s.nsd_last = ring.segment(3, (4, 4, 1))
        s.w_out = Linear(ring, KT)
        s.n_kv = stage("norm", 1)
        s.w_kv = Linear(ring, 2 * HM)
        s.prep_k = (stage("prep", HM), MK, G_MK + HM * layer)
        s.n_mem = stage("norm", 1)
        s.w_q = Linear(ring, HM)
        s.prep_q = (stage("prep", HM), MQ, G_MQ + HM * layer)
        s.matt = stage("att", HM)
        s.mdec = stage("mdec", NB)
        s.mdec_seg = ring.segment(NB, (2,) * SLOTS)
        s.w_o = Linear(ring, KT, HM)
        s.n_mlp = stage("norm", 1)
        s.mlp = Linear(ring, 2 * FF // P)
        layers.append(s)
    ev, od = layers

    with ExitStack() as ctx:
        def sb(name, shape, dt=F32):
            return ctx.enter_context(nc.sbuf_tensor(name, shape, dt))

        sems = {}

        def sem(name):
            if name not in sems:
                sems[name] = ctx.enter_context(nc.semaphore(name))
            return sems[name]

        X = sb("x", [P, KT, T])
        HT = sb("ht", [P, KT, T])
        CORE = sb("core", [P, 4 * P + 2 * T])
        GAIN = sb("gain", [P, G_END])
        SCL = sb("scl", [P, S_END + 1])
        PT = sb("pages", [1, NB * NPG], I32)
        GROW = sb("gate_rows", [P, 3, 3 * H])
        GDEC = sb("gate_dec", [NS, NB * 3])
        PMEM = sb("stats", [P, 64])
        RING = sb("ring", [P, SLOTS, SLOT])
        RMS = sb("rms", [P, T])
        WH = sb("w_hi", [P, CHUNKS, CH], F32R)
        WL = sb("w_lo", [P, CHUNKS, CH], F32R)
        base = (nc.sbuf_base + 31) // 32 * 32
        sb("region", [P, ZF + BIG_TILES * T])

        def at(name, shape, offset, dt=F32):
            return nc.alloc_sbuf_tensor_at(name, shape, dt, offset=base + 4 * offset)

        A = at("arena", [P, ZF], 0)
        XH = at("x_hi", [P, KT, T], 0, F32R)
        XL = at("x_lo", [P, KT, T], KT * T, F32R)
        BIG = at("big", [P, BIG_TILES, T], ZF)
        HH = at("hid_hi", [P, KT, T], ZF, F32R)
        HL = at("hid_lo", [P, KT, T], ZF + KT * T, F32R)
        RB = at("relu", [P, 2, T], ZF + 2 * KT * T)
        QB = at("relu2", [P, 2, T], ZF + (2 * KT + 2) * T)
        MX = BIG[:, 16:16 + KT, 0:NM]
        PS = ctx.enter_context(nc.psum_tensor("ps", [P, 8, 512], F32))

        IDENT, ONES, ROT64, ROT32 = (CORE[:, i * P:(i + 1) * P] for i in range(4))
        COSD, SIND = (CORE[:, 4 * P + i * T:4 * P + (i + 1) * T] for i in range(2))
        bigf = BIG[:, :, :].rearrange("p k t -> p (k t)")
        EVT = A[:, 5888:]
        ODT = bigf[:, OD_TILES * T:]

        def dyn(buf, i, c0=0, c1=T):
            return buf[:, bass.ds(i, 1), c0:c1].rearrange("p o c -> p (o c)")

        def row(buf, i, n):
            return buf[:, bass.ds(i, n)]

        def carve(sizes, start=0):
            out, at = [], start
            for n in sizes:
                out.append(A[:, at:at + n])
                at += n
            assert at <= 5888, at
            return out

        ring_full = [sem(f"ring_full{i}") for i in range(SLOTS)]
        ring_used = sem("ring_used")
        w_hi, w_lo, w_used = sem("w_hi"), sem("w_lo"), sem("w_used")
        tile_free = sem("tile_free")
        hid_hi, hid_sq, hid_lo = sem("hid_hi"), sem("hid_sq"), sem("hid_lo")
        x_hi, x_lo = sem("x_hi"), sem("x_lo")
        mem_in = sem("mem_in")
        consts_in, tables_in, outs_out = sem("consts_in"), sem("tables_in"), sem("outs_out")
        table_value = {"ret": 16, "dil": 32, "lru": 48, "nsa": 80}
        out_value = {"dil": 16, "mem0": 32, "lx": 48, "lru": 64, "nsa": 80, "mem1": 96}
        EPSC = SCL[:, S_END:S_END + 1]

        def slot(seg, j):
            return RING[:, seg.slot(j), :]

        def skewed(eng, n, first, step, last):
            first()
            with eng.Fori(0, n - 1) as i:
                step(i)
            last(n - 1)

        scratch0 = 50 * T
        sqb = [bigf[:, scratch0 + i * T:scratch0 + (i + 1) * T] for i in range(4)]
        t_ln = bigf[:, scratch0 + 4 * T:scratch0 + 5 * T]

        def norm_act(act, st, src, n, groups):
            for i in range(KT):
                if i >= 4:
                    act.wait_ge(sem("norm_summed"), KT * st.base + i - 3)
                act.activation(sqb[i % 4][:, 0:n], src[:, i, 0:n], ACT.Square).then_inc(sem("norm_sq"), 1)
                if i % 4 == 3:
                    act.wait_ge(sem("scaled"), KT * st.base + i + 1)
                    act.activation(XH[:, i - 3:i + 1, 0:n], HT[:, i - 3:i + 1, 0:n], ACT.Copy).then_inc(x_hi, 1)
            act.wait_ge(sem("norm_summed"), KT * st.end)
            act.activation(t_ln[:, 0:n], PS[:, 4, 0:n], ACT.Ln, scale=1.0 / D, bias=EPSC).then_inc(sem("norm_ln"), 1)
            act.wait_ge(sem("norm_ln"), st.at())
            act.activation(RMS[:, 0:n], t_ln[:, 0:n], ACT.Exp, scale=-0.5).then_inc(sem("norm_rms"), 1)
            act.wait_ge(sem("norm_rms"), st.at())

        def norm_pe(pe, st, n):
            for i in range(KT):
                pe.wait_ge(sem("norm_sq"), KT * st.base + i + 1)
                pe.matmul(PS[:, 4, 0:n], ONES, sqb[i % 4][:, 0:n], start=(i == 0), stop=(i == KT - 1)).then_inc(sem("norm_summed"), 1)

        def norm_dve(dve, st, src, gain, n, groups):
            first = groups[0]
            for i in range(KT):
                dve.tensor_scalar(HT[:, i, 0:n], src[:, i, 0:n], GAIN[:, gain + i:gain + i + 1], None, ALU.mult).then_inc(sem("scaled"), 1)
                if i % 4 == 3 and i > 4:
                    split_dve(dve, range(first + i // 4 - 1, first + i // 4), n, i // 4 - 1)
            split_dve(dve, range(first + 3, first + 4), n, 3)

        class Groups:

            def __init__(self):
                self.n = 0

            def __call__(self, n):
                self.n += n
                return range(self.n - n, self.n)

        def split_act(act, groups, cols):
            for i, g in enumerate(groups):
                act.activation(XH[:, 4 * i:4 * i + 4, 0:cols], HT[:, 4 * i:4 * i + 4, 0:cols], ACT.Copy).then_inc(x_hi, 1)

        def split_dve(dve, groups, cols, first=0):
            for i, g in enumerate(groups, first):
                dve.wait_ge(x_hi, g + 1)
                dve.tensor_tensor(XL[:, 4 * i:4 * i + 4, 0:cols], HT[:, 4 * i:4 * i + 4, 0:cols],
                                  XH[:, 4 * i:4 * i + 4, 0:cols].bitcast(F32), ALU.subtract).then_inc(x_lo, 1)

        def after_split(eng, groups):
            eng.wait_ge(x_lo, groups[-1] + 1)

        def weights_act(act, w, j, it):
            cw = CH if w.per == 2 else w.kt * P
            act.wait_ge(ring_full[w.seg.slot(j)], w.seg.arrived(j, it))
            for half in range(w.per):
                c = w.per * j + half
                act.wait_ge(w_used, it * (4 * w.per) + (w.chunk + c + 1))
                act.activation(WH[:, (w.chunk + c) % CHUNKS, 0:cw], slot(w.seg, j)[:, half * CH:half * CH + cw], ACT.Copy).then_inc(w_hi, 1)

        def weights_dve(dve, w, j, it):
            cw = CH if w.per == 2 else w.kt * P
            for half in range(w.per):
                c = w.per * j + half
                dve.wait_ge(w_hi, it * (4 * w.per) + (w.chunk + c + 1))
                dve.tensor_tensor(WL[:, (w.chunk + c) % CHUNKS, 0:cw], slot(w.seg, j)[:, half * CH:half * CH + cw],
                                  WH[:, (w.chunk + c) % CHUNKS, 0:cw].bitcast(F32), ALU.subtract)\
                   .then_inc(ring_used if half == w.per - 1 else w_lo, 1)

        def unit_pe(pe, w, j, it, hi, lo, cols):
            bank = PS[:, (w.tile + j) % 4, 0:cols]
            pe.wait_ge(tile_free, it * 4 + (w.tile + j + 1))
            kc = w.kt // w.per
            for half in range(w.per):
                c = w.per * j + half
                buf = (w.chunk + c) % CHUNKS
                pe.wait_ge(w_hi, it * (4 * w.per) + (w.chunk + c + 1))
                for k in range(kc):
                    h = WH[:, buf, k * P:(k + 1) * P]
                    pe.matmul(bank, h, hi[:, half * kc + k, 0:cols], start=(half == 0 and k == 0), stop=False)
                    pe.matmul(bank, h, lo[:, half * kc + k, 0:cols], start=False, stop=False)
                if half == w.per - 1:
                    pe.wait_ge(ring_used, w.seg.used(j, it))
                else:
                    pe.wait_ge(w_lo, it * 4 + (w.half + j + 1))
                for k in range(kc):
                    mm = pe.matmul(bank, WL[:, buf, k * P:(k + 1) * P], hi[:, half * kc + k, 0:cols],
                                   start=False, stop=(half == w.per - 1 and k == kc - 1))
                mm.then_inc(w_used, 1)

        def multiplied(w, j, it):
            return it * (4 * w.per) + (4 + w.chunk + w.per * (j + 1))

        def lin_pe(pe, w, cols=T):
            with pe.Fori(0, w.n // 4) as it:
                for j in range(4):
                    unit_pe(pe, w, j, it, XH, XL, cols)
            for u in range(w.n // 4 * 4, w.n):
                unit_pe(pe, w, u, 0, XH, XL, cols)

        def mlp_pe(pe, w, n):
            with pe.Fori(0, 4) as q:
                with pe.Fori(0, 4) as it:
                    for j in range(4):
                        unit_pe(pe, w, j, q * 8 + it, XH, XL, T)
                with pe.Fori(0, 4) as it:
                    pe.wait_ge(hid_lo, q * KT + (n * 4 * KT + KT))
                    for j in range(4):
                        unit_pe(pe, w, j + 4 * 4, q * 8 + it, HH, HL, T)

        def weights_ahead(eng, w, split):
            for u in range(w.ahead):
                split(eng, w, u, 0)

        def rounds_of(eng, w, step, split):
            loops = (w.n - w.ahead) // 4
            if loops > 0:
                with eng.Fori(0, loops) as it:
                    for j in range(4):
                        step(j, it)
                        split(eng, w, j + w.ahead, it)
            for u in range(4 * loops, w.n):
                step(u, 0)
                if u + w.ahead < w.n:
                    split(eng, w, u + w.ahead, 0)

        def lin_act(act, w):
            rounds_of(act, w, lambda j, it: None, weights_act)

        def lin_dve(dve, w, norm=None, tile0=0, cols=T):
            if norm:
                dve.wait_ge(sem("norm_rms"), norm.at())

            def step(j, it):
                dve.wait_ge(w_used, multiplied(w, j, it))
                bank = PS[:, (w.tile + j) % 4, 0:cols]
                if norm:
                    out = dyn(BIG, it * 4 + (tile0 + j), 0, cols)
                    dve.tensor_tensor(out, bank, RMS[:, 0:cols], ALU.mult).then_inc(tile_free, 1)
                else:
                    x = dyn(X, it * 4 + j)
                    dve.tensor_tensor(x, x, bank, ALU.add).then_inc(tile_free, 1)
            rounds_of(dve, w, step, weights_dve)

        def mlp_rounds(eng, w, up, down, split):
            def quarter(q, last):
                for step, first in ((up, 0), (down, 16)):
                    with eng.Fori(0, 3 if last and first else 4) as it:
                        for j in range(4):
                            step(q, j, it)
                            split(eng, w, first + j + w.ahead, q * 8 + it)
            with eng.Fori(0, 3) as q:
                quarter(q, False)
            quarter(3, True)
            for j in range(4):
                down(3, j, 3)
                if j + w.ahead < 4:
                    split(eng, w, w.n - 4 + j + w.ahead, 0)

        def mlp_act(act, w, n):
            def up(q, j, it):
                act.wait_ge(tile_free, (q * 8 + it) * 4 + (5 + w.tile + j))
                act.activation(dyn(HH, it * 4 + j), RB[:, j % 2, :], ACT.Square).then_inc(hid_hi, 1)

            mlp_rounds(act, w, up, lambda q, j, it: None, weights_act)

        def mlp_dve(dve, w, n, norm):
            def up(q, j, it):
                now = q * KT + it * 4 + (n * 4 * KT + j + 1)
                dve.wait_ge(w_used, multiplied(w, j, q * 8 + it))
                dve.wait_ge(hid_hi, now)
                dve.scalar_tensor_tensor(out=RB[:, j % 2, :], in0=PS[:, (w.tile + j) % 4, 0:T], scalar=0.0, in1=RMS[:, 0:T],
                                         op0=ALU.max, op1=ALU.mult).then_inc(tile_free, 1)
                dve.wait_ge(tile_free, (q * 8 + it) * 4 + (5 + w.tile + j))
                dve.tensor_tensor(QB[:, j % 2, :], RB[:, j % 2, :], RB[:, j % 2, :], ALU.mult).then_inc(hid_sq, 1)
                dve.wait_ge(hid_sq, now)
                dve.wait_ge(hid_hi, now + 2)
                dve.tensor_tensor(dyn(HL, it * 4 + j), QB[:, j % 2, :], dyn(HH, it * 4 + j).bitcast(F32), ALU.subtract).then_inc(hid_lo, 1)

            def down(q, j, it):
                dve.wait_ge(w_used, multiplied(w, 16 + j, q * 8 + it))
                x = dyn(X, it * 4 + j)
                dve.tensor_tensor(x, x, PS[:, (w.tile + j) % 4, 0:T], ALU.add).then_inc(tile_free, 1)

            dve.wait_ge(sem("norm_rms"), norm.at())
            mlp_rounds(dve, w, up, down, weights_dve)

        def after_tiles(eng, w):
            eng.wait_ge(tile_free, w.end)

        psq, pxg, pt1, pt2, prr, pln = carve([T] * 6)

        def prep_act(act, st, tile0, n):
            def squares(i):
                act.activation(psq[:, 0:n], dyn(BIG, tile0 + i, 0, n), ACT.Square).then_inc(sem("prep_sq"), 1)

            def rms(i, more):
                act.wait_ge(sem("prep_sum"), st.at(i))
                act.activation(pln[:, 0:n], PS[:, 4, 0:n], ACT.Ln, scale=1.0 / HD, bias=EPSC).then_inc(sem("prep_ln"), 1)
                if more:
                    squares(i + 1)
                act.wait_ge(sem("prep_ln"), st.at(i))
                act.wait_ge(sem("prep_done"), i + (st.base + 1))
                act.activation(prr[:, 0:n], pln[:, 0:n], ACT.Exp, scale=-0.5).then_inc(sem("prep_rms"), 1)
                act.wait_ge(sem("prep_rms"), st.at(i))
            skewed(act, st.rounds, lambda: squares(0), lambda i: rms(i, True), lambda i: rms(i, False))

        def prep_pe(pe, st, n, rope):
            with pe.Fori(0, st.rounds) as it:
                if rope:
                    pe.wait_ge(sem("prep_xg"), st.at(it))
                    pe.matmul(PS[:, 5, 0:n], ROT32, pxg[:, 0:n], start=True, stop=True)
                pe.wait_ge(sem("prep_sq"), st.at(it))
                pe.matmul(PS[:, 4, 0:n], ONES, psq[:, 0:n], start=True, stop=True).then_inc(sem("prep_sum"), 1)

        def prep_dve(dve, chain, st, tile0, gain, n, rope):
            def scaled(i):
                dve.tensor_scalar(pxg[:, 0:n], dyn(BIG, tile0 + i, 0, n), row(GAIN, gain + i, 1), None, ALU.mult).then_inc(sem("prep_xg"), 1)

            def rotated(i, more):
                dve.wait_ge(sem("prep_xg"), st.at(i))
                dve.wait_ge(sem("prep_sum"), st.at(i))
                dve.tensor_tensor(pt1[:, 0:n], pxg[:, 0:n], COSD[:, 0:n], ALU.mult)
                chain(dve.tensor_tensor(pt2[:, 0:n], PS[:, 5, 0:n], SIND[:, 0:n], ALU.mult))
                if more:
                    scaled(i + 1)
                chain(dve.tensor_tensor(pt1[:, 0:n], pt1[:, 0:n], pt2[:, 0:n], ALU.add))
                dve.wait_ge(sem("prep_rms"), st.at(i))
                dve.tensor_tensor(dyn(BIG, tile0 + i, 0, n), pt1[:, 0:n], prr[:, 0:n], ALU.mult).then_inc(sem("prep_done"), 1)
                dve.wait_ge(sem("prep_done"), i + (st.base + 2))

            def step(i):
                chain.enter(i, 2)
                rotated(i, True)

            def last(i):
                chain.leave(i)
                rotated(i, False)
            if rope:
                skewed(dve, st.rounds, lambda: scaled(0), step, last)
            else:
                dve.sem_inc(sem("prep_xg"), st.rounds)
                with dve.Fori(0, st.rounds) as i:
                    dve.wait_ge(sem("prep_rms"), st.at(i))
                    tile = dyn(BIG, i + tile0, 0, n)
                    dve.scalar_tensor_tensor(out=tile, in0=tile, scalar=row(GAIN, i + gain, 1), in1=prr[:, 0:n],
                                             op0=ALU.mult, op1=ALU.mult).then_inc(sem("prep_done"), 1)

        def after_prep(eng, st):
            eng.wait_ge(sem("prep_done"), 1 + st.end)

        (r_q, r_k, r_v, r_t1, r_t2, r_in, r_vr, r_kr, r_st, r_sn, r_vb, r_sp, r_ins, r_qd) = carve(
            [T, T, T, T, T, 384, 384, 384, 1024, 1024, 1024, P, NS, NS])
        r_o, r_c, r_sq, r_ln = r_q, r_k, r_t1, r_t2
        R_DEC, R_KD, R_G4, R_MB = 0, H * TP, H * TP + 2 * H, H * TP + 3 * H
        R_DS = R_MB + H * NB
        R_QD = R_DS + H * NS
        R_COS, R_SIN, R_END = R_QD + H * NS, R_QD + H * NS + T, R_QD + H * NS + 2 * T
        COSR, SINR = EVT[:, R_COS:R_COS + T], EVT[:, R_SIN:R_SIN + T]

        def ret_act(act, st):
            after_tiles(act, ev.w_in)
            gate = BIG[:, RG:RG + H, :]
            act.activation(gate, gate, ACT.Silu).then_inc(sem("ret_silu"), 1)
            with act.Fori(0, H) as h:
                act.wait_ge(sem("ret_done"), h + 1)
                act.dma_start(r_st, a["state_ret"][bass.ds(h, 1)].rearrange("o d n -> (o d) n")).then_inc(sem("ret_st"), 16)
                act.activation(r_v, dyn(BIG, h + RV), ACT.Copy).then_inc(sem("ret_v"), 1)
                act.wait_ge(sem("ret_rows"), h + 1)
                act.activation(r_vr[:, 0:256], PS[:, 3, 0:256], ACT.Copy)
                act.activation(r_vr[0:NS, 256:384], PS[0:NS, 3, 256:384], ACT.Copy).then_inc(sem("ret_vr"), 1)
                act.wait_ge(sem("ret_sn"), h + 1)
                act.dma_start(o["ret_s"][bass.ds(h, 1)].rearrange("o d n -> (o d) n"), r_sn).then_inc(sem("ret_saved"), 16)
                act.dma_start(o["ret_p"][bass.ds(h, 1)].rearrange("o d n -> (o d) n"), r_sp).then_inc(sem("ret_saved"), 16)
                act.wait_ge(sem("ret_cen"), h + 1)
                act.activation(r_sq, r_c, ACT.Square).then_inc(sem("ret_sq"), 1)
                act.wait_ge(sem("ret_var"), h + 1)
                act.activation(r_ln, PS[:, 4, 0:T], ACT.Sqrt, scale=1.0 / HD, bias=EPSC).then_inc(sem("ret_std"), 1)

        def ret_pe(pe, st):
            after_tiles(pe, ev.w_in)
            with pe.Fori(0, H) as h:
                pe.wait_ge(sem("ret_done"), h + 1)
                pe.matmul(PS[:, 0, 0:T], ROT64, dyn(BIG, h + RQ), start=True, stop=True)
                pe.matmul(PS[:, 1, 0:T], ROT64, dyn(BIG, h + RK), start=True, stop=True).then_inc(sem("ret_rot"), 1)
                pe.wait_ge(sem("ret_v"), h + 1)
                for i, w in ((0, P), (1, P), (2, NS)):
                    pe.matmul(PS[0:w, 3, i * P:(i + 1) * P], r_v[:, i * P:i * P + w], IDENT, start=True, stop=True)
                pe.wait_ge(sem("ret_qk"), h + 1)
                for i, w in ((0, P), (1, P), (2, NS)):
                    mm = pe.matmul(PS[0:w, 2, i * P:(i + 1) * P], r_k[:, i * P:i * P + w], IDENT, start=True, stop=True)
                mm.then_inc(sem("ret_rows"), 1)
                pe.matmul(PS[:, 4, 0:256], r_k[:, 0:P], r_q[:, 0:256], start=True, stop=True)
                pe.matmul(PS[:, 4, 256:384], r_k[:, P:256], r_q[:, P:256], start=True, stop=True)
                pe.matmul(PS[0:NS, 5, 0:NS], r_k[:, 256:T], r_q[:, 256:T], start=True, stop=True).then_inc(sem("ret_sc"), 1)
                pe.wait_ge(sem("ret_in"), h + 1)
                pe.matmul(PS[:, 6, 0:256], r_vr[:, 0:P], r_in[:, 0:256], start=True, stop=True)
                pe.matmul(PS[:, 6, P:256], r_vr[:, P:256], r_in[:, 256:384], start=False, stop=True, skip_group_check=True)
                pe.wait_ge(sem("ret_st"), 16 * h + 16)
                pe.matmul(PS[:, 7, 0:NS], r_vr[0:NS, 256:384], r_ins[0:NS, :], start=True, stop=True, skip_group_check=True)
                for b in range(NB):
                    mm = pe.matmul(PS[:, 7, b * TS:(b + 1) * TS], r_st[:, b * P:(b + 1) * P], r_qd[:, b * TS:(b + 1) * TS],
                                   start=False, stop=True, skip_group_check=True)
                mm.then_inc(sem("ret_o"), 1)
                pe.matmul(PS[:, 0, 0:P], r_kr[:, 0:P], r_vr[:, 0:P], start=True, stop=False)
                pe.matmul(PS[:, 0, 0:P], r_kr[:, P:256], r_vr[:, P:256], start=False, stop=True)
                for half in range(2):
                    mm = pe.matmul(PS[:, 1 + half, 0:512], r_kr[0:NS, 256:384], r_vb[0:NS, half * 512:(half + 1) * 512], start=True, stop=True)
                mm.then_inc(sem("ret_new"), 1)
                pe.wait_ge(sem("ret_os"), h + 1)
                pe.matmul(PS[:, 3, 0:T], ONES, r_o, start=True, stop=True).then_inc(sem("ret_mean"), 1)
                pe.wait_ge(sem("ret_sq"), h + 1)
                pe.matmul(PS[:, 4, 0:T], ONES, r_sq, start=True, stop=True).then_inc(sem("ret_var"), 1)

        def ret_dve(dve, chain, st):
            tab = EVT
            after_tiles(dve, ev.w_in)
            dve.wait_ge(tables_in, table_value["ret"])
            dve.wait_ge(sem("ret_silu"), 1)
            with dve.Fori(0, H) as h:
                chain.enter(h, 5)
                dve.wait_ge(sem("ret_rot"), h + 1)
                for src, bank, dst, s in ((RK, 1, r_k, 1.0), (RQ, 0, r_q, SCALE)):
                    dve.scalar_tensor_tensor(out=r_t1, in0=dyn(BIG, h + src), scalar=s, in1=COSR, op0=ALU.mult, op1=ALU.mult)
                    chain(dve.scalar_tensor_tensor(out=r_t2, in0=PS[:, bank, 0:T], scalar=s, in1=SINR, op0=ALU.mult, op1=ALU.mult))
                    ins = dve.tensor_tensor(dst, r_t1, r_t2, ALU.add)
                    if src == RK:
                        chain(ins)
                ins.then_inc(sem("ret_qk"), 1)
                dve.wait_ge(sem("ret_qk"), h + 1)
                dve.wait_ge(sem("ret_rows"), h + 1)
                kd = tab[:, R_KD:R_KD + 2 * H]
                for i in range(2):
                    dve.tensor_scalar(r_kr[:, i * P:(i + 1) * P], PS[:, 2, i * P:(i + 1) * P], row(kd, h * 2 + i, 1), None, ALU.mult)
                dve.tensor_copy(r_kr[0:NS, 256:384], PS[0:NS, 2, 256:384])
                dve.wait_ge(sem("ret_sc"), h + 1)
                dve.tensor_tensor(r_in[:, 0:256], PS[:, 4, 0:256], row(tab, h * TP, TP), ALU.mult)
                dve.tensor_tensor(r_in[:, 256:384], PS[:, 4, 256:384], row(tab, h * TP, P), ALU.mult)
                dve.tensor_tensor(r_ins[0:NS, :], PS[0:NS, 5, 0:NS], tab[0:NS, bass.ds(h * NS + R_DS, NS)], ALU.mult)
                dve.tensor_tensor(r_qd, r_q[:, 256:T], row(tab, h * NS + R_QD, NS), ALU.mult)
                dve.wait_ge(sem("ret_vr"), h + 1)
                mb = tab[0:NS, bass.ds(h * NB + R_MB, NB)]
                dve.tensor_tensor(r_vb[0:NS, :].rearrange("p (b v) -> p b v", b=NB),
                                  r_vr[0:NS, 256:384].unsqueeze(1).broadcast_to([NS, NB, P]),
                                  mb.unsqueeze(2).broadcast_to([NS, NB, P]), ALU.mult).then_inc(sem("ret_in"), 1)
                dve.wait_ge(sem("ret_o"), h + 1)
                dve.tensor_copy(r_o[:, 0:256], PS[:, 6, 0:256])
                dve.tensor_copy(r_o[:, 256:T], PS[:, 7, 0:NS]).then_inc(sem("ret_os"), 1)
                dve.wait_ge(sem("ret_os"), h + 1)
                dve.wait_ge(sem("ret_new"), h + 1)
                dve.wait_ge(sem("ret_saved"), h * 32 + 32)
                dve.tensor_copy(r_sp, PS[:, 0, 0:P])
                g4 = row(tab, h + R_G4, 1)
                for half in range(2):
                    c = slice(half * 512, (half + 1) * 512)
                    ins = dve.scalar_tensor_tensor(out=r_sn[:, c], in0=r_st[:, c], scalar=g4, in1=PS[:, 1 + half, 0:512],
                                                   op0=ALU.mult, op1=ALU.add)
                ins.then_inc(sem("ret_sn"), 1)
                dve.wait_ge(sem("ret_mean"), h + 1)
                dve.scalar_tensor_tensor(out=r_c, in0=PS[:, 3, 0:T], scalar=-1.0 / HD, in1=r_o,
                                         op0=ALU.mult, op1=ALU.add).then_inc(sem("ret_cen"), 1)
                dve.wait_ge(sem("ret_cen"), h + 1)
                dve.wait_ge(sem("ret_std"), h + 1)
                chain(dve.reciprocal(r_ln, r_ln))
                chain(dve.scalar_tensor_tensor(out=r_c, in0=r_c, scalar=row(GAIN, h + G_RET, 1), in1=r_ln, op0=ALU.mult, op1=ALU.mult))
                dve.tensor_tensor(dyn(HT, h), r_c, dyn(BIG, h + RG), ALU.mult).then_inc(sem("ret_done"), 1)
            chain.leave(H)

        (a_q, a_v, a_sm, a_p, a_pt, a_vr, a_kn) = carve([T, T, 512, 512, 512, 384, 0])
        a_mx, a_nm, a_l, a_r = (PMEM[:, i * 2:i * 2 + 2] for i in range(4))
        VN = bigf[:, 0:H * P]

        def att_act(act, st, tq, tv, rows_out):
            def queries(i):
                act.activation(a_q, dyn(BIG, tq + i), ACT.Copy).then_inc(sem("att_q"), 1)

            def values(i):
                act.activation(a_v[:, 0:VW[rows_out]], dyn(BIG, tv + i, 0, VW[rows_out]), ACT.Copy).then_inc(sem("att_v"), 1)

            def exponentials(i):
                act.wait_ge(sem("att_nm"), st.at(i))
                for q in range(2):
                    ins = act.activation(a_p[:, q * TP:(q + 1) * TP], a_sm[:, q * TP:(q + 1) * TP], ACT.Exp, bias=a_nm[:, q:q + 1],
                                         accum_out=a_l[:, q:q + 1])
                ins.then_inc(sem("att_exp"), 1)

            def value_rows(i):
                act.wait_ge(sem("att_vt"), st.at(i))
                act.activation(a_vr[:, 0:256], PS[:, 5, 0:256], ACT.Copy)
                if rows_out:
                    act.activation(VN[0:NS, bass.ds(i * P, P)], PS[0:NS, 5, 256:384], ACT.Copy)

            def turned(i):
                act.wait_ge(sem("att_turned"), st.at(i))
                act.activation(a_pt, PS[:, 6, 0:512], ACT.Copy).then_inc(sem("att_pt"), 1)

            def first():
                queries(0)
                values(0)

            def step(i):
                act.wait_ge(sem("att_sc"), st.at(i))
                queries(i + 1)
                exponentials(i)
                value_rows(i)
                values(i + 1)
                turned(i)

            def last(i):
                exponentials(i)
                value_rows(i)
                turned(i)
            skewed(act, st.rounds, first, step, last)

        def att_pe(pe, st, tk, rows_out):
            def scores(i):
                pe.wait_ge(sem("att_q"), st.at(i))
                for q in range(2):
                    mm = pe.matmul(PS[:, 4, q * TP:(q + 1) * TP], a_q[:, q * P:(q + 1) * P], dyn(BIG, tk + i, 0, TP), start=True, stop=True)
                mm.then_inc(sem("att_sc"), 1)

            def value_rows(i):
                pe.wait_ge(sem("att_v"), st.at(i))
                for k, w in ((0, P), (1, P), (2, NS))[:3 if rows_out else 2]:
                    mm = pe.matmul(PS[0:w, 5, k * P:(k + 1) * P], a_v[:, k * P:k * P + w], IDENT, start=True, stop=True)
                mm.then_inc(sem("att_vt"), 1)

            def outputs(i):
                pe.wait_ge(sem("att_p"), st.at(i))
                for k in range(2):
                    for q in range(2):
                        mm = pe.transpose(PS[:, 6, k * TP + q * P:k * TP + (q + 1) * P], a_p[:, q * TP + k * P:q * TP + (k + 1) * P], IDENT)
                mm.then_inc(sem("att_turned"), 1)
                pe.wait_ge(sem("att_done"), i + (st.base + 1))
                pe.wait_ge(sem("att_pt"), st.at(i))
                for k in range(2):
                    mm = pe.matmul(PS[:, 7, 0:TP], a_vr[:, k * P:(k + 1) * P], a_pt[:, k * TP:(k + 1) * TP], start=(k == 0), stop=(k == 1))
                mm.then_inc(sem("att_o"), 1)

            def first():
                scores(0)
                value_rows(0)

            def step(i):
                pe.wait_ge(sem("att_nm"), st.at(i))
                scores(i + 1)
                outputs(i)
                value_rows(i + 1)
            skewed(pe, st.rounds, first, step, outputs)

        def att_dve(dve, chain, st, bias, cat):
            def probabilities(i):
                dve.wait_ge(sem("att_sc"), st.at(i))
                if bias is None:
                    chain(dve.tensor_copy(a_sm, PS[:, 4, 0:512]))
                else:
                    chain(dve.tensor_tensor(a_sm, PS[:, 4, 0:512], bias, ALU.add))
                chain(dve.tensor_reduce(a_mx, a_sm.rearrange("p (q k) -> p q k", q=2), AXX, ALU.max))
                dve.tensor_scalar(a_nm, a_mx, -1.0, None, ALU.mult).then_inc(sem("att_nm"), 1)
                dve.wait_ge(sem("att_exp"), st.at(i))
                chain(dve.reciprocal(a_r, a_l))
                for q in range(2):
                    ins = dve.tensor_scalar(a_p[:, q * TP:(q + 1) * TP], a_p[:, q * TP:(q + 1) * TP], a_r[:, q:q + 1], None, ALU.mult)
                ins.then_inc(sem("att_p"), 1)

            def output(i):
                dve.wait_ge(sem("att_o"), st.at(i))
                dve.tensor_copy(dyn(HT, i + cat, 0, TP), PS[:, 7, 0:TP]).then_inc(sem("att_done"), 1)

            def step(i):
                chain.enter(i, 3)
                probabilities(i + 1)
                output(i)
            skewed(dve, st.rounds, lambda: probabilities(0), step, lambda i: (chain.leave(i), output(i)))

        VW = {True: T, False: TP}

        def after_att(eng, st):
            eng.wait_ge(sem("att_done"), 1 + st.end)

        NKN = NKD + PAD
        (d_qb, d_sm, d_p, d_pt) = carve([H * 36, NKN, NKN, 6 * NS], 0)
        D_B, D_BD, D_BN = 0, 512, 512 + NKD
        s_mx, s_nm, s_l, s_r = (PMEM[0:NS, 8 + i * 4:12 + i * 4] for i in range(4))

        def diag(buf, n, w):
            return buf.rearrange("p (h c) -> p h c", c=n * w + w)[:, :, 0:w]

        def dil_act(act, st):
            with act.Fori(0, NB) as b:
                act.wait_ge(sem("dil_nm"), b + 1)
                act.activation(d_p[0:NS, 0:NKD + NS], d_sm[0:NS, 0:NKD + NS], ACT.Exp, bias=s_nm[:, 0:1], accum_out=s_l[:, 0:1]).then_inc(sem("dil_exp"), 1)

        def dil_pe(pe):
            def scores(b, seg, r):
                pe.wait_ge(sem("dil_q"), b + 1)
                for h in range(H):
                    j = h // 2
                    if h % 2 == 0:
                        pe.wait_ge(ring_full[seg.slot(j)], seg.arrived(j, r))
                    K = slot(seg, j)[:, 0:2 * NKD].rearrange("p (h k) -> p h k", h=2)[:, h % 2, :]
                    q = d_qb[:, h * NS:(h + 1) * NS]
                    first, last = h == 0, h == H - 1
                    pe.matmul(PS[0:NS, 6, 0:NS], q, BIG[:, DK + h, TP:T], start=first, stop=last)
                    pe.matmul(PS[0:NS, 5, 0:NKD - 512], q, K[:, 512:NKD], start=first, stop=last)
                    mm = pe.matmul(PS[0:NS, 4, 0:512], q, K[:, 0:512], start=first, stop=last)
                    if h % 2 == 1:
                        mm.then_inc(ring_used, 1)

            def outputs(b, seg, r, j0):
                pe.wait_ge(sem("dil_p"), b + 1)
                for i in range(6):
                    mm = pe.matmul(PS[:, 7, i * NS:(i + 1) * NS], d_p[0:NS, i * P:(i + 1) * P], IDENT[0:NS, 0:NS], start=True, stop=True)
                mm.then_inc(sem("dil_turned"), 1)
                pe.wait_ge(sem("dil_pt"), b + 1)
                for h in range(H):
                    j = j0 + h // 2
                    if h % 2 == 0:
                        pe.wait_ge(ring_full[seg.slot(j)], seg.arrived(j, r))
                    V = slot(seg, j)[:, 0:5 * 256].rearrange("p (t h d) -> p t h d", t=5, h=2)
                    out = PS[:, 3, h * TS:(h + 1) * TS]
                    pe.matmul(out, VN[0:NS, h * P:(h + 1) * P], d_pt[0:NS, 5 * NS + h * TS:5 * NS + (h + 1) * TS], start=True, stop=False)
                    for i in range(5):
                        mm = pe.matmul(out, V[:, i, h % 2, :], d_pt[:, i * NS + h * TS:i * NS + (h + 1) * TS], start=False, stop=(i == 4))
                    if h % 2 == 1:
                        mm.then_inc(ring_used, 1)

            def step(b):
                scores(b + 1, ev.dil_seg, b)
                outputs(b, ev.dil_seg, b, 4)
            skewed(pe, NB, lambda: scores(0, ev.dil_first, 0), step, lambda b: outputs(b, ev.dil_last, 0, 0))

        def dil_dve(dve, chain):
            tab = EVT
            chain(dve.memset(d_qb, 0.0))
            dve.memset(d_p[:, 0:NKN], 0.0)
            chain(dve.memset(d_sm[:, 0:NKN], 0.0))

            def queries(b):
                dve.tensor_copy(diag(d_qb, H, TS), BIG[:, DQ:DQ + H, bass.ds(b * TS + TP, TS)]).then_inc(sem("dil_q"), 1)

            def biased(b, scored):
                dve.wait_ge(ring_used, scored)
                dve.tensor_tensor(d_sm[0:NS, 0:512], PS[0:NS, 4, 0:512], tab[0:NS, D_BD:D_BD + 512], ALU.add)
                dve.tensor_tensor(d_sm[0:NS, 512:NKD], PS[0:NS, 5, 0:NKD - 512], tab[0:NS, D_BD + 512:D_BD + NKD], ALU.add)
                chain(dve.tensor_tensor(d_sm[0:NS, NKD:NKD + NS], PS[0:NS, 6, 0:NS], tab[0:NS, bass.ds(b * NS + D_BN, NS)], ALU.add))

            def probabilities(b):
                chain(dve.tensor_reduce(s_mx[:, 0:1], d_sm[0:NS, 0:NKD + NS], AXX, ALU.max))
                dve.tensor_scalar(s_nm[:, 0:1], s_mx[:, 0:1], -1.0, None, ALU.mult).then_inc(sem("dil_nm"), 1)
                dve.wait_ge(sem("dil_exp"), b + 1)
                chain(dve.reciprocal(s_r[:, 0:1], s_l[:, 0:1]))
                dve.tensor_scalar(d_p[0:NS, 0:NKD + NS], d_p[0:NS, 0:NKD + NS], s_r[:, 0:1], None, ALU.mult).then_inc(sem("dil_p"), 1)
                dve.wait_ge(sem("dil_turned"), b + 1)
                dve.tensor_copy(d_pt, PS[:, 7, 0:6 * NS]).then_inc(sem("dil_pt"), 1)

            def output(b, multiplied):
                dve.wait_ge(ring_used, multiplied)
                dve.tensor_copy(HT[:, H:2 * H, bass.ds(b * TS + TP, TS)],
                                PS[:, 3, 0:NS].rearrange("p (h t) -> p h t", h=H)).then_inc(sem("dil_done"), 1)

            def first():
                queries(0)
                biased(0, ev.dil_first.used(3))
                queries(1)
                probabilities(0)

            with_next = ev.dil_seg
            first()
            with dve.Fori(0, NB - 2) as b:
                chain.enter(b, 3)
                biased(b + 1, with_next.used(3, b))
                output(b, with_next.used(7, b))
                queries(b + 2)
                probabilities(b + 1)
            chain.leave(NB - 2)
            biased(NB - 1, with_next.used(3, NB - 2))
            output(NB - 2, with_next.used(7, NB - 2))
            probabilities(NB - 1)
            output(NB - 1, ev.dil_last.used(3))

        MSTEP = SLOTS
        MR = HM * TS
        (m_qb, m_sm, m_p, m_pt) = carve([HM * (MR + TS), NM, NM, 2 * MR])

        def mdec_act(act, st):
            with act.Fori(0, NB) as b:
                act.wait_ge(sem("mdec_nm"), st.at(b))
                act.activation(m_p[0:MR, :], m_sm[0:MR, :], ACT.Exp, bias=s_nm[0:MR, 1:2], accum_out=s_l[0:MR, 1:2]).then_inc(sem("mdec_exp"), 1)

        def mdec_pe(pe, st, seg):
            with pe.Fori(0, NB // MSTEP) as it:
                def scores(j):
                    pe.wait_ge(sem("mdec_q"), it * MSTEP + (st.base + j + 1))
                    pe.wait_ge(ring_full[seg.slot(j)], seg.arrived(j, it))
                    K = slot(seg, j)[:, 0:HM * NM].rearrange("p (h k) -> p h k", h=HM)
                    for h in range(HM):
                        mm = pe.matmul(PS[0:MR, 4, 0:NM], m_qb[:, h * MR:(h + 1) * MR], K[:, h, :], start=(h == 0), stop=(h == HM - 1))
                    mm.then_inc(sem("mdec_sc"), 1)

                def outputs(j):
                    now = it * MSTEP + (st.base + j + 1)
                    V = slot(seg, j)[:, HM * NM:2 * HM * NM].rearrange("p (t h d) -> p t h d", t=2, h=HM)
                    pe.wait_ge(sem("mdec_p"), now)
                    for i in range(2):
                        mm = pe.matmul(PS[:, 5, i * MR:(i + 1) * MR], m_p[0:MR, i * P:(i + 1) * P], IDENT[0:MR, 0:MR], start=True, stop=True)
                    mm.then_inc(sem("mdec_turned"), 1)
                    pe.wait_ge(sem("mdec_pt"), now)
                    for h in range(HM):
                        for i in range(2):
                            mm = pe.matmul(PS[:, 6, h * TS:(h + 1) * TS], V[:, i, h, :], m_pt[:, i * MR + h * TS:i * MR + (h + 1) * TS],
                                           start=(i == 0), stop=(i == 1))
                    mm.then_inc(ring_used, 1)

                scores(0)
                for j in range(MSTEP):
                    if j + 1 < MSTEP:
                        scores(j + 1)
                    outputs(j)

        def mdec_dve(dve, chain, st, seg):
            chain(dve.memset(m_qb, 0.0))
            with dve.Fori(0, NB // MSTEP) as it:
                chain.enter(it, 3 * MSTEP)

                def cols(j):
                    return bass.ds(it * (MSTEP * TS) + (TP + j * TS), TS)

                def queries(j):
                    dve.tensor_copy(diag(m_qb, HM, TS), BIG[:, MQ:MQ + HM, cols(j)]).then_inc(sem("mdec_q"), 1)

                def output(j):
                    dve.wait_ge(ring_used, seg.used(j, it))
                    dve.tensor_copy(HT[:, 0:HM, cols(j)], PS[:, 6, 0:MR].rearrange("p (h t) -> p h t", h=HM)).then_inc(sem("mdec_done"), 1)

                queries(0)
                for j in range(MSTEP):
                    now = it * MSTEP + (st.base + j + 1)
                    dve.wait_ge(sem("mdec_sc"), now)
                    chain(dve.tensor_copy(m_sm[0:MR, :], PS[0:MR, 4, 0:NM]))
                    if j + 1 < MSTEP:
                        queries(j + 1)
                    chain(dve.tensor_reduce(s_mx[0:MR, 1:2], m_sm[0:MR, :], AXX, ALU.max))
                    dve.tensor_scalar(s_nm[0:MR, 1:2], s_mx[0:MR, 1:2], -1.0, None, ALU.mult).then_inc(sem("mdec_nm"), 1)
                    if j:
                        output(j - 1)
                    dve.wait_ge(sem("mdec_exp"), now)
                    chain(dve.reciprocal(s_r[0:MR, 1:2], s_l[0:MR, 1:2]))
                    dve.tensor_scalar(m_p[0:MR, :], m_p[0:MR, :], s_r[0:MR, 1:2], None, ALU.mult).then_inc(sem("mdec_p"), 1)
                    dve.wait_ge(sem("mdec_turned"), now)
                    dve.tensor_copy(m_pt, PS[:, 5, 0:2 * MR]).then_inc(sem("mdec_pt"), 1)
                output(MSTEP - 1)
            chain.leave(NB // MSTEP)

        (l_xin, l_xc, l_wa, l_wi, l_par, l_sp, l_s, l_zero, l_inv) = carve([LW + 3, LW, P, P, 320, 8 * 8, 8, NB, H * LW])
        L_CONV, L_H0, L_CW, L_CB, L_BA, L_BI, L_LAM = 0, 192, 256, 288, 296, 304, 312
        l_r, l_i = (ODT[:, i * H * LW:(i + 1) * H * LW].rearrange("p (h t) -> p h t", h=H) for i in range(2))
        l_a = A[:, 5888:5888 + H * LW].rearrange("p (h t) -> p h t", h=H)

        def seqs(ap):
            return ap.rearrange("p (b t) -> p b t", t=7)

        def lru_act(act, st):
            lam = l_par[:, L_LAM:L_LAM + 8]
            act.wait_ge(tables_in, table_value["lru"])
            act.activation(l_sp[:, 0:8], lam, ACT.Abs).then_inc(sem("lru_abs"), 1)
            act.wait_ge(sem("lru_abs"), 1)
            act.activation(l_sp[:, 8:16], l_sp[:, 0:8], ACT.Exp, scale=-1.0).then_inc(sem("lru_e"), 1)
            with act.Fori(0, H) as h:
                act.wait_ge(sem("lru_mm"), h + 1)
                act.activation(dyn(l_r, h, 0, LW), PS[:, 4, 0:LW], ACT.Sigmoid, bias=row(l_par, h + L_BA, 1))
                act.activation(dyn(l_i, h, 0, LW), PS[:, 5, 0:LW], ACT.Sigmoid, bias=row(l_par, h + L_BI, 1)).then_inc(sem("lru_sig"), 1)
            act.wait_ge(sem("lru_la"), 1 + H)
            act.activation(l_a[:, :, :], l_r[:, :, :], ACT.Exp).then_inc(sem("lru_exp"), 1)
            act.wait_ge(sem("lru_exp"), 1)
            act.activation(l_r[:, :, :], l_r[:, :, :], ACT.Tanh, scale=-1.0).then_inc(sem("lru_tanh"), 1)
            ly = BIG[:, LY:LY + H, :]
            act.activation(ly, ly, ACT.Gelu_apprx_tanh).then_inc(sem("lru_gelu"), 1)
            act.wait_ge(sem("lru_tanh"), 1)
            act.activation(l_inv, l_r[:, :, :].rearrange("p h t -> p (h t)"), ACT.Ln, bias=1.0).then_inc(sem("lru_ln"), 1)
            act.wait_ge(sem("lru_ln"), 1)
            act.activation(l_inv, l_inv, ACT.Exp, scale=-1.0).then_inc(sem("lru_inv"), 1)
            act.wait_ge(sem("lru_b2"), 1)
            act.activation(l_r[:, :, :], l_r[:, :, :], ACT.Sqrt).then_inc(sem("lru_sqrt"), 1)

        def lru_pe(pe, st):
            with pe.Fori(0, H) as h:
                pe.wait_ge(sem("lru_xc"), h + 1)
                pe.matmul(PS[:, 4, 0:LW], l_wa, l_xc, start=True, stop=True)
                pe.matmul(PS[:, 5, 0:LW], l_wi, l_xc, start=True, stop=True).then_inc(sem("lru_mm"), 1)

        def lru_dve(dve, chain, st, seg):
            dve.wait_ge(tables_in, table_value["lru"])
            dve.wait_ge(sem("lru_e"), 1)
            c = [l_sp[:, i * 8:i * 8 + 8] for i in range(8)]
            chain(dve.tensor_scalar(c[2], c[1], 2.0, None, ALU.add))
            chain(dve.reciprocal(c[3], c[2]))
            chain(dve.tensor_tensor(c[4], c[1], c[3], ALU.mult))
            chain(dve.tensor_tensor(c[5], c[4], c[4], ALU.mult))
            chain(dve.tensor_scalar(c[6], c[5], 1.0 / 17, 1.0 / 15, ALU.mult, ALU.add))
            for n in (13, 11, 9, 7, 5, 3, 1):
                chain(dve.tensor_tensor(c[6], c[6], c[5], ALU.mult))
                chain(dve.tensor_scalar(c[6], c[6], 1.0 / n, None, ALU.add))
            chain(dve.tensor_tensor(c[6], c[6], c[4], ALU.mult))
            chain(dve.tensor_scalar(c[7], l_par[:, L_LAM:L_LAM + 8], -1.0, 0.0, ALU.mult, ALU.max))
            chain(dve.scalar_tensor_tensor(out=c[7], in0=c[6], scalar=2.0, in1=c[7], op0=ALU.mult, op1=ALU.add))
            chain(dve.tensor_scalar(l_s, c[7], -8.0, None, ALU.mult))
            chain(dve.memset(l_xin[:, 0:3], 0.0))
            chain(dve.memset(l_zero, 0.0))
            dve.wait_ge(ring_full[seg.slot(0)], seg.arrived(0))
            W = slot(seg, 0)
            with dve.Fori(0, H) as h:
                chain.enter(h, 4)
                dve.wait_ge(sem("lru_la"), h + 1)
                dve.tensor_copy(l_wa, row(W, h * P, P))
                dve.tensor_copy(l_wi, row(W, h * P + H * P, P))
                dve.tensor_copy(l_xin[:, 3:3 + TP], dyn(BIG, h + LX, 0, TP))
                xs = seqs(l_xin[:, 3 + TP:3 + LW])
                dve.tensor_copy(xs[:, :, 0:3], row(l_par, h * 24, 24).rearrange("p (b t) -> p b t", t=3))
                chain(dve.tensor_copy(xs[:, :, 3:7], dyn(BIG, h + LX, TP, T).rearrange("p (b t) -> p b t", t=TS)))
                chain(dve.tensor_scalar(l_xc, l_xin[:, 0:LW], row(l_par, h * 4 + L_CW, 1), row(l_par, h + L_CB, 1), ALU.mult, ALU.add))
                for j in range(1, 4):
                    ins = dve.scalar_tensor_tensor(out=l_xc, in0=l_xin[:, j:j + LW], scalar=row(l_par, h * 4 + (L_CW + j), 1), in1=l_xc,
                                                   op0=ALU.mult, op1=ALU.add)
                    if j < 3:
                        chain(ins)
                ins.then_inc(sem("lru_xc"), 1)
                dve.wait_ge(sem("lru_xc"), h + 1)
                dve.wait_ge(sem("lru_sig"), h + 1)
                dve.tensor_tensor(dyn(l_i, h, 0, LW), dyn(l_i, h, 0, LW), l_xc, ALU.mult)
                dve.tensor_scalar(dyn(l_r, h, 0, LW), dyn(l_r, h, 0, LW), row(l_s, h, 1), None, ALU.mult).then_inc(sem("lru_la"), 1)
            chain.leave(H)
            dve.wait_ge(sem("lru_inv"), 1)
            r = l_r[:, :, :].rearrange("p h t -> p (h t)")
            dve.scalar_tensor_tensor(out=r, in0=r, scalar=2.0, in1=l_inv, op0=ALU.mult, op1=ALU.mult).then_inc(sem("lru_b2"), 1)
            dve.wait_ge(sem("lru_sqrt"), 1)
            dve.wait_ge(sem("lru_gelu"), 1)
            with dve.Fori(0, H) as h:
                chain.enter(h, 3)
                chain(dve.tensor_tensor(dyn(l_i, h, 0, LW), dyn(l_i, h, 0, LW), dyn(l_r, h, 0, LW), ALU.mult))
                sa, si = seqs(dyn(l_a, h, TP, LW)), seqs(dyn(l_i, h, TP, LW))
                dve.tensor_copy(sa[:, :, 0:3], l_zero.unsqueeze(2).broadcast_to([P, NB, 3]))
                h0 = row(l_par, h * NB + L_H0, NB).unsqueeze(2).broadcast_to([P, NB, 3])
                chain(dve.tensor_copy(si[:, :, 0:3], h0))
                chain(dve.tensor_tensor_scan(dyn(l_r, h, 0, LW), dyn(l_a, h, 0, LW), dyn(l_i, h, 0, LW), 0.0, ALU.mult, ALU.add))
                dve.tensor_tensor(dyn(HT, h + H, 0, TP), dyn(l_r, h, 0, TP), dyn(BIG, h + LY, 0, TP), ALU.mult)
                dve.tensor_tensor(dyn(HT, h + H, TP, T).rearrange("p (b t) -> p b t", t=TS), seqs(dyn(l_r, h, TP, LW))[:, :, 3:7],
                                  dyn(BIG, h + LY, TP, T).rearrange("p (b t) -> p b t", t=TS), ALU.mult).then_inc(sem("lru_done"), 1)
            chain.leave(H)

        N_B, N_CB, N_CM, N_WB, N_NB, N_SEL = 0, 512, 520, 528, 528 + WIN, 528 + WIN + NB * NS
        N_PWT, N_PWV, N_PVT = N_SEL + NPG * NBS, N_SEL + NPG * NBS + P, N_SEL + NPG * NBS + 2 * P
        N_END = N_PVT + BLK
        n_v = ODT[:, N_END:N_END + 4 * 384].rearrange("p (i c) -> p i c", i=4)
        n_kc = ODT[:, N_END + 1536:N_END + 1544]
        n_vt = ODT[:, N_END + 1544:N_END + 1552]
        n_vc = ODT[:, N_END + 1552:N_END + 1552 + 256]
        (n_tmp,) = carve([2 * TP])
        v_tiles = [VSL, VSL + 1, VWN, VWN + 1]

        def gate_pe(pe):
            for i, w in ((0, P), (1, P), (2, NS)):
                mm = pe.matmul(PS[0:w, 4, i * 24:(i + 1) * 24], BIG[0:24, GT, i * P:i * P + w], IDENT[0:24, 0:24], start=True, stop=True)
            mm.then_inc(sem("gate_rows"), 1)
            for i in range(4):
                for c, w in ((0, P), (1, P), (2, NS)):
                    mm = pe.matmul(PS[0:w, i, c * P:(c + 1) * P], BIG[:, v_tiles[i], c * P:c * P + w], IDENT, start=True, stop=True)
            mm.then_inc(sem("nsv_rows"), 1)
            pe.wait_ge(sem("nsc_vt"), 1)
            for g in range(G):
                mm = pe.matmul(PS[0:NBP, 5, g * P:(g + 1) * P], n_vt[:, g * NBP:(g + 1) * NBP], IDENT, start=True, stop=True)
            mm.then_inc(sem("nsc_rows"), 1)

        def gate_act(act):
            act.wait_ge(sem("gate_rows"), 1)
            g = GROW[:, :, :].rearrange("p i c -> p (i c)")
            act.activation(g[:, 0:48], PS[:, 4, 0:48], ACT.Exp, scale=-1.0)
            act.activation(g[0:NS, 48:72], PS[0:NS, 4, 48:72], ACT.Exp, scale=-1.0).then_inc(sem("gate_exp"), 1)
            act.wait_ge(sem("nsv_rows"), 1)
            act.wait_ge(sem("lru_done"), H)
            act.wait_ge(outs_out, out_value["lru"])
            act.activation(n_v[:, :, 0:256], PS[:, 0:4, 0:256], ACT.Copy)
            act.activation(n_v[0:NS, :, 256:384], PS[0:NS, 0:4, 256:384], ACT.Copy)
            act.wait_ge(sem("nsc_rows"), 1)
            act.activation(n_vc[0:NBP, :], PS[0:NBP, 5, 0:256], ACT.Copy).then_inc(sem("nsc_done"), 1)

        def gate_dve(dve, chain):
            g = GROW[:, :, :].rearrange("p i c -> p (i c)")
            dve.wait_ge(sem("gate_exp"), 1)
            dve.tensor_scalar(g[:, 0:48], g[:, 0:48], 1.0, None, ALU.add)
            chain(dve.tensor_scalar(g[0:NS, 48:72], g[0:NS, 48:72], 1.0, None, ALU.add))
            dve.reciprocal(g[:, 0:48], g[:, 0:48])
            dve.reciprocal(g[0:NS, 48:72], g[0:NS, 48:72]).then_inc(sem("gates"), 1)
            dve.wait_ge(tables_in, table_value["nsa"])
            for n, (tile, pw, out) in enumerate(((KCM, N_PWT, n_kc), (VCM, N_PVT, n_vt))):
                w = ODT[:, pw:pw + BLK].unsqueeze(1).broadcast_to([P, NBP, BLK])
                for g_ in range(G):
                    t = n_tmp[:, g_ * TP:(g_ + 1) * TP].rearrange("p (b r) -> p b r", r=BLK)
                    chain(dve.tensor_tensor(t, BIG[:, tile + g_, 0:TP].rearrange("p (b r) -> p b r", r=BLK), w, ALU.mult))
                    ins = dve.tensor_reduce(out[:, g_ * NBP:(g_ + 1) * NBP], t, AXX, ALU.add)
                    if n == 1 and g_ == 1:
                        ins.then_inc(sem("nsc_vt"), 1)
                    else:
                        chain(ins)

        (n_q, n_sm, n_p, n_pt) = carve([T, 1032, 1032, 1280])
        n_mx, n_nm, n_l, n_r = (PMEM[:, 24 + i * 6:30 + i * 6] for i in range(4))

        def parts(buf):
            return [buf[:, (b * 2 + q) * TP:(b * 2 + q + 1) * TP] for b in range(2) for q in range(2)] + \
                   [buf[:, 1024 + q * NBP:1024 + (q + 1) * NBP] for q in range(2)]

        def nsp_act(act, g):
            h0 = g * (H // G)

            def queries(i):
                act.activation(n_q, dyn(BIG, NQ + h0 + i), ACT.Copy).then_inc(sem("nsp_q"), 1)

            def finish(i):
                act.wait_ge(sem("nsp_nm"), i + (h0 + 1))
                for k, (p, x) in enumerate(zip(parts(n_p), parts(n_sm))):
                    ins = act.activation(p, x, ACT.Exp, bias=n_nm[:, k:k + 1], accum_out=n_l[:, k:k + 1])
                ins.then_inc(sem("nsp_exp"), 1)
                act.wait_ge(sem("nsp_turned"), i + (h0 + 1))
                act.activation(n_pt[:, 0:512], PS[:, 7, 0:512], ACT.Copy)
                act.activation(n_pt[:, 512:1024], PS[:, 3, 0:512], ACT.Copy)
                act.activation(n_pt[0:NBP, 1024:1280], PS[0:NBP, 2, 0:256], ACT.Copy).then_inc(sem("nsp_pt"), 1)

            def step(i):
                act.wait_ge(sem("nsp_sc"), i + (h0 + 1))
                queries(i + 1)
                finish(i)
            act.wait_ge(sem("nsp_done"), h0 + 1)
            skewed(act, H // G, lambda: queries(0), step, finish)

        def nsp_pe(pe, g):
            h0 = g * (H // G)

            def scores(i):
                pe.wait_ge(sem("nsp_q"), i + (h0 + 1))
                for q in range(2):
                    qs = n_q[:, q * P:(q + 1) * P]
                    pe.matmul(PS[:, 4, q * TP:(q + 1) * TP], qs, BIG[:, KSL + g, 0:TP], start=True, stop=True)
                    pe.matmul(PS[:, 5, q * TP:(q + 1) * TP], qs, BIG[:, KWN + g, 0:TP], start=True, stop=True)
                    mm = pe.matmul(PS[:, 6, q * NBP:(q + 1) * NBP], qs, n_kc[:, g * NBP:(g + 1) * NBP], start=True, stop=True)
                mm.then_inc(sem("nsp_sc"), 1)

            def outputs(i):
                pe.wait_ge(sem("nsp_p"), i + (h0 + 1))
                pp = parts(n_p)
                for b, bank in ((0, 7), (1, 3)):
                    for k in range(2):
                        for q in range(2):
                            pe.transpose(PS[:, bank, k * TP + q * P:k * TP + (q + 1) * P], pp[2 * b + q][:, k * P:(k + 1) * P], IDENT)
                for q in range(2):
                    mm = pe.matmul(PS[0:NBP, 2, q * P:(q + 1) * P], pp[4 + q], IDENT, start=True, stop=True)
                mm.then_inc(sem("nsp_turned"), 1)
                pe.wait_ge(sem("nsp_done"), i + (h0 + 1))
                pe.wait_ge(sem("nsp_pt"), i + (h0 + 1))
                for b in range(2):
                    for k in range(2):
                        pe.matmul(PS[:, 1, 0:TP], n_v[:, 2 * b + g, k * P:(k + 1) * P], n_pt[:, b * 512 + k * TP:b * 512 + (k + 1) * TP],
                                  start=(b == 0 and k == 0), stop=False)
                pe.matmul(PS[:, 1, 0:TP], n_vc[0:NBP, g * P:(g + 1) * P], n_pt[0:NBP, 1024:1280], start=False, stop=True).then_inc(sem("nsp_o"), 1)

            def step(i):
                pe.wait_ge(sem("nsp_nm"), i + (h0 + 1))
                scores(i + 1)
                outputs(i)
            skewed(pe, H // G, lambda: scores(0), step, outputs)

        def nsp_dve(dve, chain, g):
            h0 = g * (H // G)

            def probabilities(i):
                dve.wait_ge(sem("nsp_sc"), i + (h0 + 1))
                dve.tensor_tensor(n_sm[:, 0:512], PS[:, 4, 0:512], ODT[:, N_B:N_B + 512], ALU.add)
                dve.tensor_tensor(n_sm[:, 512:1024], PS[:, 5, 0:512], ODT[:, N_B:N_B + 512], ALU.add)
                chain(dve.tensor_tensor(n_sm[:, 1024:1032], PS[:, 6, 0:8], ODT[:, N_CB:N_CB + 8], ALU.add))
                dve.tensor_reduce(n_mx[:, 0:4], n_sm[:, 0:1024].rearrange("p (i k) -> p i k", i=4), AXX, ALU.max)
                chain(dve.tensor_reduce(n_mx[:, 4:6], n_sm[:, 1024:1032].rearrange("p (i k) -> p i k", i=2), AXX, ALU.max))
                dve.tensor_scalar(n_nm, n_mx, -1.0, None, ALU.mult).then_inc(sem("nsp_nm"), 1)
                dve.wait_ge(sem("nsp_exp"), i + (h0 + 1))
                pc = n_p[:, 1024:1032]
                chain(dve.tensor_tensor(pc, pc, ODT[:, N_CM:N_CM + 8], ALU.mult))
                chain(dve.tensor_reduce(n_l[:, 4:6], pc.rearrange("p (q k) -> p q k", q=2), AXX, ALU.add))
                chain(dve.tensor_scalar(n_l, n_l, 1e-30, None, ALU.max))
                chain(dve.reciprocal(n_r, n_l))
                for b, c in ((0, 1), (1, 2), (2, 0)):
                    r2 = n_r[:, 2 * b:2 * b + 2].unsqueeze(2)
                    chain(dve.tensor_tensor(r2, r2, GROW[:, 0:2, bass.ds(i * 3 + (h0 * 3 + c), 1)], ALU.mult))
                for k, p in enumerate(parts(n_p)):
                    ins = dve.tensor_scalar(p, p, n_r[:, k:k + 1], None, ALU.mult)
                    if k == 0:
                        chain(ins)
                ins.then_inc(sem("nsp_p"), 1)

            def output(i):
                dve.wait_ge(sem("nsp_o"), i + (h0 + 1))
                dve.tensor_copy(dyn(HT, h0 + i, 0, TP), PS[:, 1, 0:TP]).then_inc(sem("nsp_done"), 1)

            def step(i):
                chain.enter(i, 10)
                probabilities(i + 1)
                output(i)
            skewed(dve, H // G, lambda: probabilities(0), step, lambda i: (chain.leave(i), output(i)))

        C_SN, C_W, C_WN, C_C, C_END = 1024, 1152, 1664, 1792, 1920
        GR = NS // G
        (e_qb, e_sm, e_p, e_pt, e_kc, e_vc) = carve([G * 3 * GR, C_END, C_END, 15 * NS, G * NBS, 2 * P])
        E_BR = ((0, C_SN + NS), (C_W, C_WN + NS), (C_C, C_C + NBS))

        def nsd_act(act, st):
            with act.Fori(0, NB) as b:
                act.wait_ge(sem("nsd_nm"), b + 1)
                for i, (c0, c1) in enumerate(E_BR):
                    ins = act.activation(e_p[0:NS, c0:c1], e_sm[0:NS, c0:c1], ACT.Exp, bias=s_nm[:, i:i + 1], accum_out=s_l[:, i:i + 1])
                ins.then_inc(sem("nsd_exp"), 1)

        def nsd_pe(pe):
            def scores(b, seg, r):
                pe.wait_ge(sem("nsd_prod"), b + 1)
                pe.sem_inc(ring_used, 1)
                VC = slot(seg, 1).rearrange("p (i c) -> p i c", i=NPG)
                for i in range(NPG):
                    mm = pe.matmul(PS[0:NBS, 3, 0:256], ODT[:, N_SEL + i * NBS:N_SEL + (i + 1) * NBS], VC[:, i, :], start=(i == 0), stop=(i == NPG - 1))
                mm.then_inc(ring_used, 1)
                for half in range(2):
                    pe.wait_ge(ring_full[seg.slot(2 + half)], seg.arrived(2 + half, r))
                    KS = slot(seg, 2 + half)[:, 0:1024].rearrange("p (i g r) -> p g i r", i=4, g=G)
                    for g in range(G):
                        mm = pe.matmul(PS[0:NS, 4 + half, 0:512].rearrange("p (i r) -> p i r", i=4), e_qb[:, g * NS:(g + 1) * NS], KS[:, g],
                                       start=(g == 0), stop=(g == G - 1))
                    mm.then_inc(ring_used, 1)
                pe.wait_ge(ring_full[seg.slot(4)], seg.arrived(4, r))
                KW = slot(seg, 4)[:, 0:1024].rearrange("p (g k) -> p g k", g=G)
                for g in range(G):
                    q = e_qb[:, g * NS:(g + 1) * NS]
                    f, l = g == 0, g == G - 1
                    pe.matmul(PS[0:NS, 7, 0:NS], q, BIG[:, KSL + g, TP:T], start=f, stop=True, skip_group_check=True)
                    pe.matmul(PS[0:NS, 7, NS:2 * NS], q, BIG[:, KWN + g, TP:T], start=False, stop=True, skip_group_check=True)
                    pe.matmul(PS[0:NS, 7, 2 * NS:2 * NS + NBS], q, e_kc[:, g * NBS:(g + 1) * NBS], start=False, stop=True, skip_group_check=True)
                    mm = pe.matmul(PS[0:NS, 6, 0:512], q, KW[:, g, :], start=f, stop=l)
                mm.then_inc(ring_used, 1)

            def outputs(b, seg, r, j0):
                pe.wait_ge(sem("nsd_p"), b + 1)
                for i in range(15):
                    mm = pe.matmul(PS[:, 2, i * NS:(i + 1) * NS], e_p[0:NS, i * P:(i + 1) * P], IDENT[0:NS, 0:NS], start=True, stop=True)
                mm.then_inc(sem("nsd_turned"), 1)
                pe.wait_ge(sem("nsd_pt"), b + 1)

                def out(g):
                    return PS[:, 1, g * GR:(g + 1) * GR]

                def pt(i, g, n=P):
                    return e_pt[0:n, i * NS + g * GR:i * NS + (g + 1) * GR]
                for half in range(2):
                    j = j0 + half
                    pe.wait_ge(ring_full[seg.slot(j)], seg.arrived(j, r))
                    VS = slot(seg, j)[:, 0:1024].rearrange("p (i g d) -> p i g d", i=4, g=G)
                    for g in range(G):
                        for i in range(4):
                            mm = pe.matmul(out(g), VS[:, i, g, :], pt(4 * half + i, g), start=(half == 0 and g == 0 and i == 0), stop=True,
                                           skip_group_check=True)
                    mm.then_inc(ring_used, 1)
                j = j0 + 2
                pe.wait_ge(ring_full[seg.slot(j)], seg.arrived(j, r))
                VW_ = slot(seg, j)[:, 0:1024].rearrange("p (i g d) -> p i g d", i=4, g=G)
                for g in range(G):
                    pe.matmul(out(g), n_v[0:NS, g, 256:384], pt(8, g, NS), start=False, stop=True, skip_group_check=True)
                    pe.matmul(out(g), n_v[0:NS, 2 + g, 256:384], pt(13, g, NS), start=False, stop=True, skip_group_check=True)
                    pe.matmul(out(g), e_vc[0:NBS, g * P:(g + 1) * P], pt(14, g, NBS), start=False, stop=True, skip_group_check=True)
                    for i in range(4):
                        mm = pe.matmul(out(g), VW_[:, i, g, :], pt(9 + i, g), start=False, stop=True, skip_group_check=True)
                mm.then_inc(ring_used, 1)

            def step(b):
                scores(b + 1, od.nsd_seg, b)
                outputs(b, od.nsd_seg, b, 5)
            skewed(pe, NB, lambda: scores(0, od.nsd_first, 0), step, lambda b: outputs(b, od.nsd_last, 0, 0))

        def nsd_dve(dve, chain):
            first, seg, last = od.nsd_first, od.nsd_seg, od.nsd_last
            chain(dve.memset(e_qb, 0.0))
            dve.memset(e_p, 0.0)
            chain(dve.memset(e_sm, 0.0))

            def compress(b, seg, r):
                dve.tensor_copy(diag(e_qb, G, GR).rearrange("p g (h t) -> p g h t", t=TS),
                                BIG[:, NQ:NQ + H, bass.ds(b * TS + TP, TS)].rearrange("p (g h) t -> p g h t", g=G))
                dve.wait_ge(ring_full[seg.slot(0)], seg.arrived(0, r))
                S = slot(seg, 0)
                KC = S.rearrange("p (i r) -> p i r", r=P)
                chain(dve.tensor_tensor(KC, KC, ODT[:, N_PWT:N_PWT + P].unsqueeze(1).broadcast_to([P, 16, P]), ALU.mult))
                for g in range(G):
                    chain(dve.tensor_reduce(e_kc[:, g * NBS:(g + 1) * NBS].rearrange("p (i x) -> p i x", x=2),
                                            S.rearrange("p (i g x r) -> p g i x r", i=NPG, g=G, r=BLK)[:, g], AXX, ALU.add))
                dve.wait_ge(ring_full[seg.slot(1)], seg.arrived(1, r))
                VC = slot(seg, 1).rearrange("p (i r) -> p i r", r=P)
                return dve.tensor_tensor(VC, VC, ODT[:, N_PWV:N_PWV + P].unsqueeze(1).broadcast_to([P, 16, P]), ALU.mult)

            def biased(b, scored):
                dve.wait_ge(ring_used, scored)
                dve.tensor_copy(e_sm[0:NS, 0:1024], PS[0:NS, 4:6, :].rearrange("p a c -> p (a c)"))
                dve.tensor_tensor(e_sm[0:NS, C_W:C_W + WIN], PS[0:NS, 6, 0:WIN], ODT[0:NS, N_WB:N_WB + WIN], ALU.add)
                nb = ODT[0:NS, bass.ds(b * NS + N_NB, NS)]
                dve.tensor_tensor(e_sm[0:NS, C_SN:C_SN + NS], PS[0:NS, 7, 0:NS], nb, ALU.add)
                dve.tensor_tensor(e_sm[0:NS, C_WN:C_WN + NS], PS[0:NS, 7, NS:2 * NS], nb, ALU.add)
                chain(dve.tensor_copy(e_sm[0:NS, C_C:C_C + NBS], PS[0:NS, 7, 2 * NS:2 * NS + NBS]))

            def values():
                return dve.tensor_copy(e_vc[0:NBS, :], PS[0:NBS, 3, 0:256])

            def probabilities(b):
                for i, (c0, c1) in enumerate(E_BR):
                    ins = dve.tensor_reduce(s_mx[:, i:i + 1], e_sm[0:NS, c0:c1], AXX, ALU.max)
                chain(ins)
                dve.tensor_scalar(s_nm[:, 0:3], s_mx[:, 0:3], -1.0, None, ALU.mult).then_inc(sem("nsd_nm"), 1)
                dve.wait_ge(sem("nsd_exp"), b + 1)
                chain(dve.reciprocal(s_r[:, 0:3], s_l[:, 0:3]))
                chain(dve.tensor_tensor(s_r[:, 0:2], s_r[:, 0:2], GDEC[:, bass.ds(b * 3 + 1, 2)], ALU.mult))
                chain(dve.tensor_tensor(s_r[:, 2:3], s_r[:, 2:3], GDEC[:, bass.ds(b * 3, 1)], ALU.mult))
                for i, (c0, c1) in enumerate(E_BR):
                    ins = dve.tensor_scalar(e_p[0:NS, c0:c1], e_p[0:NS, c0:c1], s_r[:, i:i + 1], None, ALU.mult)
                ins.then_inc(sem("nsd_p"), 1)
                dve.wait_ge(sem("nsd_turned"), b + 1)
                dve.tensor_copy(e_pt, PS[:, 2, 0:15 * NS]).then_inc(sem("nsd_pt"), 1)

            def output(b, multiplied):
                dve.wait_ge(ring_used, multiplied)
                dve.tensor_copy(HT[:, 0:H, bass.ds(b * TS + TP, TS)],
                                PS[:, 1, 0:NS].rearrange("p (h t) -> p h t", h=H)).then_inc(sem("nsd_done"), 1)

            compress(0, first, 0).then_inc(sem("nsd_prod"), 1)
            biased(0, first.used(4))
            compress(1, seg, 0)
            values().then_inc(sem("nsd_prod"), 1)
            probabilities(0)
            with dve.Fori(0, NB - 2) as b:
                chain.enter(b, 8)
                biased(b + 1, seg.used(4, b))
                compress(b + 2, seg, b + 1)
                output(b, seg.used(7, b))
                values().then_inc(sem("nsd_prod"), 1)
                probabilities(b + 1)
            chain.leave(NB - 2)
            biased(NB - 1, seg.used(4, NB - 2))
            output(NB - 2, seg.used(7, NB - 2))
            values()
            probabilities(NB - 1)
            output(NB - 1, last.used(2))

        def after_ret(eng):
            eng.wait_ge(sem("ret_done"), 1 + H)
            eng.wait_ge(sem("ret_saved"), 32 + 32 * H)

        def after_nsp(eng):
            eng.wait_ge(sem("nsp_done"), 1 + H)

        block = ctx.enter_context(nc.Block())

        @block.sync
        def _(sp):
            for dst, name in ((X[:, :, :], "x"), (CORE[:, :], "core"), (GAIN[:, :], "gain"), (SCL[:, :], "scl"), (PT[:, :], "pages")):
                sp.dma_start(dst, a[name]).then_inc(consts_in, 16)

            def fill(seg, loads):
                def unit(j, it):
                    copies = loads(j, it)
                    sp.wait_ge(ring_used, seg.may_fill(j, it))
                    for dst, src in copies:
                        sp.dma_start(dst, src).then_inc(ring_full[seg.slot(j)], 16)
                whole = seg.units // seg.round
                if whole > 1:
                    with sp.Fori(0, whole) as it:
                        for j in range(seg.round):
                            unit(j, it)
                for j in range(seg.round * whole if whole > 1 else 0, seg.units):
                    unit(j, 0)

            def one(ap, i):
                return ap[bass.ds(i, 1)].rearrange("o p n -> (o p) n")

            def weights(w, name):
                n = w.kt * P
                fill(w.seg, lambda j, it: [(slot(w.seg, j)[:, 0:n], a[name][j] if isinstance(it, int) else one(a[name], it * SLOTS + j))])

            for s in layers:
                layer = layers.index(s)
                if layer == 0:
                    weights(s.w_in, "ev_w_in")

                    def dil_loads(seg, j, k, b):
                        n, src, x = (2 * NKD, "dil_k", k) if b is None or (k is not None and j < 4) else (5 * 256, "dil_v", b)
                        return [(slot(seg, j)[:, 0:n], one(a[src], x * 4 + j % 4))]
                    fill(s.dil_first, lambda j, it: dil_loads(s.dil_first, j, 0, None))
                    fill(s.dil_seg, lambda j, b: dil_loads(s.dil_seg, j, b + 1, b))
                    fill(s.dil_last, lambda j, it: dil_loads(s.dil_last, j, None, NB - 1))
                else:
                    weights(s.w_in, "od_w_in")
                    fill(s.lru_seg, lambda j, it: [(slot(s.lru_seg, 0), a["lru_w"])])
                    sp.wait_ge(consts_in, 80)
                    pages = []

                    def nsd_loads(seg, j, kind, b):
                        S = slot(seg, j)
                        if kind in (4, 7):
                            return [(S[:, 0:1024], one(a["win_k" if kind == 4 else "win_v"], b))]
                        if kind in (0, 5):
                            pages[:] = [sp.value_load(PT[0:1, bass.ds(b * NPG + i, 1)], min_val=0, max_val=a["cmp_k"].shape[0] - 1)
                                        for i in range(NPG)]
                        name, mine = {0: ("cmp_k", pages), 1: ("cmp_v", pages), 2: ("slc_k", pages[:4]), 3: ("slc_k", pages[4:]),
                                      5: ("slc_v", pages[:4]), 6: ("slc_v", pages[4:])}[kind]
                        return [(S[:, i * 256:(i + 1) * 256], one(a[name], page)) for i, page in enumerate(mine)]
                    fill(s.nsd_first, lambda j, it: nsd_loads(s.nsd_first, j, j, 0))
                    fill(s.nsd_seg, lambda j, b: nsd_loads(s.nsd_seg, j, j, b + 1 if j < 5 else b))
                    fill(s.nsd_last, lambda j, it: nsd_loads(s.nsd_last, j, 5 + j, NB - 1))
                weights(s.w_out, f"w_out{layer}")
                weights(s.w_kv, f"mem_w_kv{layer}")
                weights(s.w_q, f"mem_w_q{layer}")
                mseg = s.mdec_seg

                def mem_loads(j, it):
                    b = it * MSTEP + (layer * NB + j)
                    return [(slot(mseg, j)[:, 0:1024], one(a["mem_k"], b)), (slot(mseg, j)[:, 1024:2048], one(a["mem_v"], b))]
                fill(mseg, mem_loads)
                weights(s.w_o, f"mem_w_o{layer}")
                weights(s.mlp, f"mlp{layer}")

        @block.gpsimd
        def _(pool):
            after_tiles(pool, ev.w_in)
            pool.dma_start(EVT[:, 0:R_END], a["ret_tab"]).then_inc(tables_in, 16)
            after_ret(pool)
            pool.dma_start(EVT[:, 0:D_BN + NB * NS], a["dil_tab"]).then_inc(tables_in, 16)
            pool.dma_start(MX, a["mem_x"]).then_inc(mem_in, 16)
            after_prep(pool, ev.prep[-1][0])
            pool.dma_start(o["dil_kv"], BIG[:, DK:DK + 2 * H, :]).then_inc(outs_out, 16)
            after_prep(pool, ev.prep_k[0])
            pool.dma_start(o["mem_kv0"], BIG[:, 0:2 * HM, 0:NM]).then_inc(outs_out, 16)
            after_tiles(pool, od.w_in)
            pool.dma_start(l_par, a["lru_par"]).then_inc(tables_in, 16)
            pool.dma_start(o["lx"], BIG[:, LX:LX + H, :]).then_inc(outs_out, 16)
            pool.wait_ge(sem("lru_done"), H)
            pool.dma_start(o["lru_h"], l_r[:, :, :]).then_inc(outs_out, 16)
            pool.wait_ge(outs_out, out_value["lru"])
            pool.dma_start(ODT[:, 0:N_PWT], a["nsa_tab"]).then_inc(tables_in, 16)
            pool.dma_start(ODT[:, N_PWT:N_END], a["pw"]).then_inc(tables_in, 16)
            pool.wait_ge(sem("gates"), 1)
            pool.dma_start(scratch, GROW[0:NS, 2, :]).then_inc(sem("gates_out"), 16)
            pool.wait_ge(sem("gates_out"), 16)
            for h in range(H):
                pool.dma_start(GDEC[h * TS:(h + 1) * TS, :].rearrange("t (b j) -> t b j", j=3),
                               scratch.rearrange("(b t) c -> t b c", t=TS)[:, :, 3 * h:3 * h + 3]).then_inc(sem("gates_in"), 16)
            after_prep(pool, od.prep[-1][0])
            pool.dma_start(o["nsa_kv"], BIG[:, KCM:KCM + 12, :]).then_inc(outs_out, 16)
            pool.wait_ge(sem("nsd_done"), NB)
            pool.wait_ge(outs_out, out_value["nsa"])
            pool.dma_start(MX, a["mem_x"]).then_inc(mem_in, 16)
            after_prep(pool, od.prep_k[0])
            pool.dma_start(o["mem_kv1"], BIG[:, 0:2 * HM, 0:NM]).then_inc(outs_out, 16)
            after_tiles(pool, od.mlp)
            pool.dma_start(o["y"], X[:, :, :]).then_inc(outs_out, 16)
            pool.wait_ge(outs_out, 112)

        @block.tensor
        def _(pe):
            for name in ("ring_used", "w_used", "tile_free"):
                pe.sem_inc(sem(name), 4)
            pe.sem_inc(hid_hi, 2)
            pe.sem_inc(sem("ret_saved"), 32)
            pe.wait_ge(consts_in, 80)
            groups = Groups()
            for s in layers:
                layer = layers.index(s)
                norm_pe(pe, s.n_mix, T)
                after_split(pe, groups(4))
                lin_pe(pe, s.w_in)
                after_tiles(pe, s.w_in)
                if layer == 0:
                    ret_pe(pe, s.ret)
                    after_ret(pe)
                    for st, tile0, gain in s.prep:
                        prep_pe(pe, st, T, True)
                        after_prep(pe, st)
                    att_pe(pe, s.att, DK, True)
                    after_att(pe, s.att)
                    dil_pe(pe)
                    pe.wait_ge(sem("dil_done"), NB)
                else:
                    lru_pe(pe, s.lru)
                    pe.wait_ge(sem("lru_done"), H)
                    pe.sem_inc(ring_used, 1)
                    for st, tile0, gain in s.prep:
                        prep_pe(pe, st, T, True)
                        after_prep(pe, st)
                    gate_pe(pe)
                    pe.wait_ge(sem("nsc_done"), 1)
                    for g in range(G):
                        nsp_pe(pe, g)
                    after_nsp(pe)
                    nsd_pe(pe)
                    pe.wait_ge(sem("nsd_done"), NB)
                after_split(pe, groups(4))
                lin_pe(pe, s.w_out)
                norm_pe(pe, s.n_kv, NM)
                after_split(pe, groups(4))
                lin_pe(pe, s.w_kv, NM)
                after_tiles(pe, s.w_kv)
                prep_pe(pe, s.prep_k[0], NM, False)
                after_prep(pe, s.prep_k[0])
                norm_pe(pe, s.n_mem, T)
                after_split(pe, groups(4))
                lin_pe(pe, s.w_q)
                after_tiles(pe, s.w_q)
                prep_pe(pe, s.prep_q[0], T, False)
                after_prep(pe, s.prep_q[0])
                att_pe(pe, s.matt, MK, False)
                after_att(pe, s.matt)
                mdec_pe(pe, s.mdec, s.mdec_seg)
                pe.wait_ge(sem("mdec_done"), s.mdec.end)
                after_split(pe, groups(1))
                lin_pe(pe, s.w_o)
                norm_pe(pe, s.n_mlp, T)
                after_split(pe, groups(4))
                mlp_pe(pe, s.mlp, layer)

        @block.scalar
        def _(act):
            act.wait_ge(consts_in, 80)
            groups = Groups()
            for s in layers:
                layer = layers.index(s)
                weights_ahead(act, s.w_in, weights_act)
                norm_act(act, s.n_mix, X, T, groups(4))
                lin_act(act, s.w_in)
                after_tiles(act, s.w_in)
                if layer == 0:
                    ret_act(act, s.ret)
                    after_ret(act)
                    for st, tile0, gain in s.prep:
                        prep_act(act, st, tile0, T)
                        after_prep(act, st)
                    att_act(act, s.att, DQ, DV, True)
                    after_att(act, s.att)
                    dil_act(act, s.dil)
                    act.wait_ge(sem("dil_done"), NB)
                else:
                    lru_act(act, s.lru)
                    act.wait_ge(sem("lru_done"), H)
                    for st, tile0, gain in s.prep:
                        prep_act(act, st, tile0, T)
                        after_prep(act, st)
                    gate_act(act)
                    for g in range(G):
                        nsp_act(act, g)
                    after_nsp(act)
                    nsd_act(act, s.nsd)
                    act.wait_ge(sem("nsd_done"), NB)
                split_act(act, groups(4), T)
                weights_ahead(act, s.w_out, weights_act)
                lin_act(act, s.w_out)
                weights_ahead(act, s.w_kv, weights_act)
                after_tiles(act, s.w_out)
                act.wait_ge(mem_in, 16 * (layer + 1))
                act.wait_ge(outs_out, out_value["nsa" if layer else "dil"])
                norm_act(act, s.n_kv, MX, NM, groups(4))
                lin_act(act, s.w_kv)
                after_tiles(act, s.w_kv)
                prep_act(act, s.prep_k[0], MK, NM)
                after_prep(act, s.prep_k[0])
                weights_ahead(act, s.w_q, weights_act)
                norm_act(act, s.n_mem, X, T, groups(4))
                lin_act(act, s.w_q)
                after_tiles(act, s.w_q)
                prep_act(act, s.prep_q[0], MQ, T)
                after_prep(act, s.prep_q[0])
                att_act(act, s.matt, MQ, MV, False)
                after_att(act, s.matt)
                mdec_act(act, s.mdec)
                act.wait_ge(sem("mdec_done"), s.mdec.end)
                split_act(act, groups(1), T)
                weights_ahead(act, s.w_o, weights_act)
                lin_act(act, s.w_o)
                weights_ahead(act, s.mlp, weights_act)
                after_tiles(act, s.w_o)
                norm_act(act, s.n_mlp, X, T, groups(4))
                act.wait_ge(outs_out, out_value[f"mem{layer}"])
                mlp_act(act, s.mlp, layer)
                after_tiles(act, s.mlp)

        @block.vector
        def _(dve):
            chain = Chain(dve, sem("dve_chain"))
            for name in ("prep_done", "ret_done", "att_done", "nsp_done", "lru_la"):
                dve.sem_inc(sem(name), 1)
            dve.wait_ge(consts_in, 80)
            gains = GAIN[:, G_EV:G_EV + S_END]
            chain(dve.tensor_tensor(gains, gains, SCL[:, 0:S_END], ALU.mult))
            groups = Groups()
            for s in layers:
                layer = layers.index(s)
                weights_ahead(dve, s.w_in, weights_dve)
                norm_dve(dve, s.n_mix, X, GN_MIX + KT * layer, T, groups(4))
                lin_dve(dve, s.w_in, s.n_mix)
                after_tiles(dve, s.w_in)
                if layer == 0:
                    ret_dve(dve, chain, s.ret)
                    after_ret(dve)
                    for st, tile0, gain in s.prep:
                        prep_dve(dve, chain, st, tile0, gain, T, True)
                        after_prep(dve, st)
                    dve.wait_ge(tables_in, table_value["dil"])
                    att_dve(dve, chain, s.att, EVT[:, D_B:D_B + 512], H)
                    after_att(dve, s.att)
                    dil_dve(dve, chain)
                else:
                    lru_dve(dve, chain, s.lru, s.lru_seg)
                    dve.wait_ge(sem("lru_done"), H)
                    for st, tile0, gain in s.prep:
                        prep_dve(dve, chain, st, tile0, gain, T, True)
                        after_prep(dve, st)
                    gate_dve(dve, chain)
                    dve.wait_ge(sem("nsc_done"), 1)
                    for g in range(G):
                        nsp_dve(dve, chain, g)
                    after_nsp(dve)
                    dve.wait_ge(sem("gates_in"), 16 * H)
                    nsd_dve(dve, chain)
                split_dve(dve, groups(4), T)
                weights_ahead(dve, s.w_out, weights_dve)
                lin_dve(dve, s.w_out)
                weights_ahead(dve, s.w_kv, weights_dve)
                dve.wait_ge(mem_in, 16 * (layer + 1))
                norm_dve(dve, s.n_kv, MX, GN_KV + KT * layer, NM, groups(4))
                dve.wait_ge(outs_out, out_value["nsa" if layer else "dil"])
                lin_dve(dve, s.w_kv, s.n_kv, 0, NM)
                after_tiles(dve, s.w_kv)
                prep_dve(dve, chain, *s.prep_k, NM, False)
                weights_ahead(dve, s.w_q, weights_dve)
                norm_dve(dve, s.n_mem, X, GN_MEM + KT * layer, T, groups(4))
                lin_dve(dve, s.w_q, s.n_mem, MQ)
                after_tiles(dve, s.w_q)
                prep_dve(dve, chain, *s.prep_q, T, False)
                att_dve(dve, chain, s.matt, None, 0)
                after_att(dve, s.matt)
                mdec_dve(dve, chain, s.mdec, s.mdec_seg)
                split_dve(dve, groups(1), T)
                weights_ahead(dve, s.w_o, weights_dve)
                lin_dve(dve, s.w_o)
                weights_ahead(dve, s.mlp, weights_dve)
                norm_dve(dve, s.n_mlp, X, GN_MLP + KT * layer, T, groups(4))
                dve.wait_ge(outs_out, out_value[f"mem{layer}"])
                mlp_dve(dve, s.mlp, layer, s.n_mlp)


def tiles(w):
    k, n = w.shape
    return w.reshape(k // P, P, n // P, P).transpose(2, 1, 0, 3).reshape(n // P, P, -1)


def columns(v):
    return v.reshape(-1, P).T


def layout(i):
    xs = np.concatenate([i["x_prompt"][0], i["x_sample"].reshape(NS, D)], 0)
    w_od = i["od_w_in"][0]
    nq = H * HD + 6 * G * HD
    rows = dilated_rows()
    kd = i["cache_dil_k"][0][:, rows].reshape(NB, NKD, 4, 2, HD).transpose(0, 2, 4, 3, 1)
    vd = i["cache_dil_v"][0][:, rows].reshape(NB, NKD // P, P, 4, 2, HD).transpose(0, 3, 2, 1, 4, 5)
    pool_k = lambda c: c[0].transpose(0, 3, 2, 1).reshape(-1, P, G * PAGE)
    pool_v = lambda c: c[0].reshape(-1, P, G * HD)
    gains = [columns(g) for name in ("norm_mix_g", "norm_mem_g", "norm_mlp_g", "mem_norm_g") for g in i[name]]
    rep = lambda v, n: np.repeat(v.reshape(P, 1), n, 1)
    kg = i["nsa_k_norm_g"][0]
    gains += [rep(i["dil_q_norm_g"][0], H), rep(i["dil_k_norm_g"][0], H), rep(i["nsa_q_norm_g"][0], H), rep(kg[0], G), rep(kg[1], G),
              rep(kg[2], G), rep(i["mem_q_norm_g"][0], HM), rep(i["mem_q_norm_g"][1], HM), rep(i["mem_k_norm_g"][0], HM),
              rep(i["mem_k_norm_g"][1], HM), columns(i["ret_gn_g"][0].reshape(-1))]
    pwk, pwv = i["nsa_pw_k"][0], i["nsa_pw_v"][0]
    par = [i["state_lru_conv"][0].reshape(NB, 3, H, P).transpose(3, 2, 0, 1).reshape(P, -1),
           i["state_lru_h"][0].reshape(NB, H, P).transpose(2, 1, 0).reshape(P, -1),
           i["lru_conv_w"][0].reshape(4, H, P).transpose(2, 1, 0).reshape(P, -1)]
    par += [columns(i[n][0]) for n in ("lru_conv_b", "lru_b_a", "lru_b_i", "lru_lambda")]
    out = {
        "x": xs.reshape(T, KT, P).transpose(2, 1, 0),
        "core": core_table(), "scl": scales_table(), "gain": np.concatenate(gains, 1),
        "pages": i["page_table"].reshape(1, -1),
        "ret_tab": retention_table(), "dil_tab": dilated_table(), "nsa_tab": sparse_table(),
        "pw": np.concatenate([pwk.T, pwk.T, np.concatenate([pwv, pwv], 0), pwv.T], 1),
        "lru_par": np.concatenate(par, 1),
        "lru_w": np.concatenate([i[n][0].transpose(1, 0, 2).reshape(P, -1) for n in ("lru_w_a", "lru_w_i")], 1),
        "state_ret": i["state_ret"][0].transpose(1, 2, 0, 3).reshape(H, P, -1),
        "dil_k": kd.reshape(4 * NB, P, -1), "dil_v": vd.reshape(4 * NB, P, -1),
        "cmp_k": pool_k(i["cache_nsa_cmp_k"]), "cmp_v": pool_v(i["cache_nsa_cmp_v"]),
        "slc_k": pool_k(i["cache_nsa_slc_k"]), "slc_v": pool_v(i["cache_nsa_slc_v"]),
        "win_k": i["cache_nsa_win_k"][0].transpose(0, 3, 2, 1).reshape(NB, P, -1),
        "win_v": i["cache_nsa_win_v"][0].reshape(NB, 4, P, G * HD).transpose(0, 2, 1, 3).reshape(NB, P, -1),
        "mem_k": i["cache_mem_k"].transpose(0, 1, 4, 3, 2).reshape(2 * NB, P, -1),
        "mem_v": i["cache_mem_v"].reshape(2 * NB, 2, P, HM * HD).transpose(0, 2, 1, 3).reshape(2 * NB, P, -1),
        "mem_x": i["mem_prompt"][0].reshape(NM, KT, P).transpose(2, 1, 0),
        "ev_w_in": tiles(i["ev_w_in"][0]),
        "od_w_in": tiles(np.pad(np.concatenate([w_od[:, :nq], w_od[:, nq + 3 * H:], w_od[:, nq:nq + 3 * H]], 1), ((0, 0), (0, P - 3 * H)))),
        "w_out0": tiles(i["ev_w_out"][0]), "w_out1": tiles(i["od_w_out"][0]),
    }
    for l in range(2):
        out[f"mem_w_kv{l}"] = np.concatenate([tiles(i["mem_w_k"][l]), tiles(i["mem_w_v"][l])], 0)
        out[f"mem_w_q{l}"] = tiles(i["mem_w_q"][l])
        out[f"mem_w_o{l}"] = tiles(i["mem_w_o"][l])
        w1 = tiles(i["mlp_w1"][l]).reshape(4, KT, P, SLOT)
        w2 = np.stack([tiles(q) for q in np.split(i["mlp_w2"][l], 4, 0)])
        out[f"mlp{l}"] = np.concatenate([w1, w2], 1).reshape(-1, P, SLOT)
    return {n: np.ascontiguousarray(v) for n, v in out.items()}


_OUTS = {"y": (P, KT, T), "ret_s": (H, P, NB * P), "ret_p": (H, P, P), "dil_kv": (P, 2 * H, T), "nsa_kv": (P, 12, T), "lx": (P, H, T),
         "lru_h": (P, H, LW), "mem_kv0": (P, 2 * HM, NM), "mem_kv1": (P, 2 * HM, NM)}


def kernel(**inputs):
    import concourse.bacc as bacc
    from concourse.bass_utils import run_bass_kernel_spmd

    nc = bacc.Bacc("TRN2", target_bir_lowering=False, num_devices=1)
    arrays = {f"in_{n}": v for n, v in layout({k: np.asarray(v) for k, v in inputs.items()}).items()}
    a = {n[3:]: nc.dram_tensor(n, v.shape, mybir.dt.from_np(v.dtype), kind="ExternalInput").ap() for n, v in arrays.items()}
    o = {n: nc.dram_tensor(f"out_{n}", s, F32, kind="ExternalOutput").ap() for n, s in _OUTS.items()}
    scratch = nc.dram_tensor("gate_scratch", (NS, 3 * H), F32).ap()
    build(nc, a, o, scratch)
    r = run_bass_kernel_spmd(nc, [arrays], core_ids=[0]).results[0]
    r = {n: np.asarray(r[f"out_{n}"]) for n in _OUTS}

    def heads(x, first, n, cols, lead):
        return np.ascontiguousarray(x[:, first:first + n, cols].transpose(2, 1, 0)).reshape(lead + (n, P))

    prompt, sample = slice(0, TP), slice(TP, T)
    y = r["y"].transpose(2, 1, 0).reshape(T, D)
    out = [y[:TP].reshape(1, TP, D), y[TP:].reshape(NB, TS, D),
           r["ret_p"].reshape(1, 1, H, P, P), r["ret_s"].reshape(H, P, NB, P).transpose(2, 0, 1, 3)[None]]
    for cols, lead in ((prompt, (1, 1, TP)), (sample, (1, NB, TS))):
        out += [heads(r["dil_kv"], 0, H, cols, lead), heads(r["dil_kv"], H, H, cols, lead)]
    for first in (0, 4, 8):
        for cols, lead in ((prompt, (1, 1, TP)), (sample, (1, NB, TS))):
            out += [heads(r["nsa_kv"], first, G, cols, lead), heads(r["nsa_kv"], first + G, G, cols, lead)]
    h = r["lru_h"]
    out += [h[:, :, TP - 1].T.reshape(1, 1, -1), h[:, :, TP:].reshape(P, H, NB, 7)[..., 6].transpose(2, 1, 0).reshape(1, NB, -1)]
    lx = r["lx"]
    out += [lx[:, :, TP - 3:TP].transpose(2, 1, 0).reshape(1, 1, 3, -1),
            lx[:, :, TP:].reshape(P, H, NB, TS)[..., 1:].transpose(2, 3, 1, 0).reshape(1, NB, 3, -1)]
    mem = [r["mem_kv0"], r["mem_kv1"]]
    out += [np.stack([heads(m, f, HM, slice(0, NM), (1, NM)) for m in mem]) for f in (0, HM)]
    return tuple(np.ascontiguousarray(v) for v in out)
```

```python
from contextlib import ExitStack

import numpy as np
import concourse.bass as bass
from concourse import mybir

F32 = mybir.dt.float32
F32R = mybir.dt.float32r
I32 = mybir.dt.int32
ALU = mybir.AluOpType
ACT = mybir.ActivationFunctionType
AXX = mybir.AxisListType.X

P = 128
D = 2048
KT = D // P
TP, NB, TS = 256, 8, 4
NS = NB * TS
T = TP + NS
HD = 128
H = 8
G = 2
HM = 4
NM = 256
PAST = 1024
PAGE = 128
NPG = PAST // PAGE
BLK = 64
NBP = TP // BLK
NBS = PAST // BLK
WIN = 512
FF = 4 * D
EPS = 1e-6
SCALE = HD ** -0.5
SLOT = 2048
SLOTS = 4
CH = 1024
CHUNKS = 4
ZF = 2 * KT * T
NKD = 640
LW = TP + 7 * NB
NEG = -1e30
PAD = 128

RQ, RK, RV, RG, DQ, DK, DV, EV_TILES = 0, 8, 16, 24, 32, 40, 48, 56
NQ, KCM, VCM, KSL, VSL, KWN, VWN, LX, LY, GT, OD_TILES = 0, 8, 10, 12, 14, 16, 18, 20, 28, 36, 37
BIG_TILES = 57
MK, MV, MQ = 0, 4, 8
GN_MIX, GN_MEM, GN_MLP, GN_KV = 0, 32, 64, 96
G_EV, G_OD, G_MQ, G_MK, G_RET, G_END = 128, 144, 158, 166, 174, 182
S_EV, S_OD, S_MQ, S_MK, S_END = 0, 16, 30, 38, 46


def log_decay():
    return np.log1p(-np.exp2(-5.0 - np.arange(H))).astype(np.float64)


def positions():
    return np.concatenate([np.arange(TP), np.tile(PAST + np.arange(TS), NB)]).astype(np.float32)


def rope_tables(n_rot, theta):
    half = n_rot // 2
    inv = (1.0 / (np.float32(theta) ** (np.arange(half, dtype=np.float32) * np.float32(2.0 / n_rot)))).astype(np.float32)
    ang = (positions()[:, None] * inv[None, :]).astype(np.float32).astype(np.float64)
    cos, sin = np.ones((HD, T)), np.zeros((HD, T))
    cos[:half] = cos[half:n_rot] = np.cos(ang).T
    sin[:half] = sin[half:n_rot] = np.sin(ang).T
    rot = np.zeros((HD, HD))
    for i in range(half):
        rot[i, i + half] = -1.0
        rot[i + half, i] = 1.0
    return cos, sin, rot.T


def core_table():
    r1 = rope_tables(HD, 10000.0)[2]
    c2, s2, r2 = rope_tables(HD // 4, 500000.0)
    return np.concatenate([np.eye(P), np.ones((P, P)), r1, r2, c2, s2], 1).astype(np.float32)


def scales_table():
    s = np.ones((P, S_END + 1))
    s[:, S_END] = EPS
    s[:, S_EV:S_EV + H] = SCALE
    s[:, S_OD:S_OD + H] = SCALE
    s[:, S_MQ:S_MQ + 2 * HM] = SCALE
    return s.astype(np.float32)


def retention_table():
    lg = log_decay()
    j, i = np.arange(P)[:, None], np.arange(TP)[None, :]
    dec = np.where(i >= j, np.exp(np.maximum(i - j, 0)[None] * lg[:, None, None]), 0.0)
    dec = dec.transpose(1, 0, 2).reshape(P, H * TP)
    n = np.arange(NS)
    same = (n[:, None] // TS == n[None, :] // TS)
    dif = (n[None, :] % TS) - (n[:, None] % TS)
    ds_ = np.where(same & (dif >= 0), np.exp(np.maximum(dif, 0)[None] * lg[:, None, None]), 0.0)
    decs = np.zeros((P, H, NS))
    decs[:NS] = ds_.transpose(1, 0, 2)
    qd = np.broadcast_to(np.exp((n % TS + 1.0)[None, :] * lg[:, None])[None], (P, H, NS))
    kd = np.stack([np.exp((TP - 1.0 - np.arange(P))[:, None] * lg), np.exp((P - 1.0 - np.arange(P))[:, None] * lg)], 2)
    g4 = np.broadcast_to(np.exp(TS * lg)[None], (P, H))
    mb = np.zeros((P, H, NB))
    for r in range(NS):
        mb[r, :, r // TS] = np.exp((TS - 1.0 - r % TS) * lg)
    cos, sin, _ = rope_tables(HD, 10000.0)
    parts = [dec, kd.reshape(P, -1), g4, mb.reshape(P, -1), decs.reshape(P, -1), qd.reshape(P, -1), cos, sin]
    return np.concatenate(parts, 1).astype(np.float32)


def dilated_multiplicity(dist):
    n = np.zeros(dist.shape)
    for window, dil in ((128, 1), (512, 4), (2048, 16)):
        n += (dist >= 0) & (dist <= window) & (dist % dil == 0)
    return n


def dilated_rows():
    far = np.arange(512).reshape(32, 16)[:, :TS].ravel()
    return np.concatenate([far, 512 + np.arange(512)])


def log_mult(n):
    return np.where(n > 0, np.log(np.maximum(n, 1)), NEG)


def new_key_bias():
    r, b, k = np.arange(P)[:, None, None], np.arange(NB)[None, :, None], np.arange(NS)[None, None, :]
    return (r % TS) - (k % TS), (k // TS == b)


def dilated_table():
    q, k = np.arange(TP), np.arange(TP)
    bias = log_mult(dilated_multiplicity(q[:, None] - k[None, :])).reshape(2, P, TP).transpose(1, 0, 2).reshape(P, -1)
    qs = PAST + np.arange(P) % TS
    biasd = log_mult(dilated_multiplicity(qs[:, None] - dilated_rows()[None, :]))
    dist, own = new_key_bias()
    biasn = np.where(own, log_mult(dilated_multiplicity(dist)), NEG).reshape(P, -1)
    return np.concatenate([bias, biasd, biasn], 1).astype(np.float32)


def sparse_table():
    q, k = np.arange(TP), np.arange(TP)
    bias = np.where(q[:, None] >= k[None, :], 0.0, NEG).reshape(2, P, TP).transpose(1, 0, 2).reshape(P, -1)
    ok = (np.arange(NBP)[None, :] + 1) * BLK - 1 <= q[:, None]
    cb = np.where(ok, 0.0, NEG).reshape(2, P, NBP).transpose(1, 0, 2).reshape(P, -1)
    cm = ok.astype(float).reshape(2, P, NBP).transpose(1, 0, 2).reshape(P, -1)
    qs = PAST + np.arange(P) % TS
    kw = PAST - WIN + np.arange(WIN)
    wb = np.where(qs[:, None] - kw[None, :] < WIN, 0.0, NEG)
    dist, own = new_key_bias()
    nb = np.where(own & (dist >= 0), 0.0, NEG).reshape(P, -1)
    sel = np.zeros((P, NPG, NBS))
    for p in range(NPG):
        sel[:BLK, p, 2 * p] = 1.0
        sel[BLK:, p, 2 * p + 1] = 1.0
    return np.concatenate([bias, cb, cm, wb, nb, sel.reshape(P, -1)], 1).astype(np.float32)


class Ring:

    def __init__(self):
        self.unit = 0
        self.full = [0] * SLOTS

    def segment(self, units, dmas=(1,) * SLOTS):
        seg = Segment(self.unit, tuple(self.full), units, dmas)
        for u in range(units):
            self.full[(self.unit + u) % SLOTS] += 16 * dmas[u % len(dmas)]
        self.unit += units
        return seg


class Segment:

    def __init__(self, first, full, units, dmas):
        self.first, self.full, self.units, self.dmas, self.round = first, full, units, dmas, len(dmas)

    def slot(self, j):
        return (self.first + j) % SLOTS

    def arrived(self, j, it=0):
        in_round = sum(self.dmas[j % SLOTS::SLOTS])
        whole, rest = divmod(j, self.round)
        done = sum(self.dmas[j % SLOTS:rest + 1:SLOTS])
        return it * (16 * in_round) + (16 * (whole * in_round + done) + self.full[self.slot(j)])

    def may_fill(self, j, it=0):
        return it * self.round + (self.first + j + 1)

    def used(self, j, it=0):
        return it * self.round + (self.first + j + 1 + SLOTS)


class Stage:

    def __init__(self, kind, base, rounds):
        self.kind, self.base, self.rounds = kind, base, rounds
        self.gather = self.whole = None
        self.gain = None

    def at(self, it=0):
        return it + (self.base + 1)

    @property
    def end(self):
        return self.base + self.rounds


class Linear:

    chunks = tiles = halves = 0

    def __init__(self, ring, units, kt=KT):
        self.seg, self.kt, self.n = ring.segment(units), kt, units
        self.per = 2 if kt == KT else 1
        self.chunk, self.tile, self.half = Linear.chunks, Linear.tiles, Linear.halves
        Linear.chunks += self.per * units
        Linear.tiles += units
        Linear.halves += (self.per - 1) * units
        self.ahead = CHUNKS // self.per

    @property
    def end(self):
        return 4 + self.tile + self.n


class Chain:

    def __init__(self, eng, sem):
        self.eng, self.sem, self.base, self.k, self.it, self.per = eng, sem, 0, 0, 0, 0

    def __call__(self, ins):
        self.k += 1
        ins.then_inc(self.sem, 1)
        self.eng.wait_ge(self.sem, self.it * self.per + (self.base + self.k))

    def enter(self, it, per):
        self.base, self.k, self.it, self.per = self.base + self.k, 0, it, per

    def leave(self, rounds):
        assert self.k == self.per, (self.k, self.per)
        self.base, self.k, self.it, self.per = self.base + rounds * self.per, 0, 0, 0


def build(nc, a, o, scratch):
    ring = Ring()
    Linear.chunks = Linear.tiles = Linear.halves = 0
    rounds = {}

    def stage(kind, n):
        st = Stage(kind, rounds.get(kind, 0), n)
        rounds[kind] = st.end
        return st

    class L:
        pass

    layers = []
    for layer in range(2):
        s = L()
        s.n_mix = stage("norm", 1)
        if layer == 0:
            s.w_in = Linear(ring, EV_TILES)
            s.ret = stage("ret", H)
            s.prep = [(stage("prep", H), DQ, G_EV), (stage("prep", H), DK, G_EV + H)]
            s.att = stage("att", H)
            s.dil = stage("dil", NB)
            s.dil_first = ring.segment(4)
            s.dil_seg = ring.segment(8 * (NB - 1), (1,) * 8)
            s.dil_last = ring.segment(4)
        else:
            s.w_in = Linear(ring, OD_TILES)
            s.lru_seg = ring.segment(1)
            s.lru = stage("lru", H)
            s.prep = [(stage("prep", H), NQ, G_OD), (stage("prep", G), KCM, G_OD + H), (stage("prep", G), KSL, G_OD + 10),
                      (stage("prep", G), KWN, G_OD + 12)]
            s.att = stage("nsp", H)
            s.nsd = stage("nsd", NB)
            s.nsd_first = ring.segment(5, (8, 8, 4, 4, 1))
            s.nsd_seg = ring.segment(8 * (NB - 1), (8, 8, 4, 4, 1, 4, 4, 1))
            s.nsd_last = ring.segment(3, (4, 4, 1))
        s.w_out = Linear(ring, KT)
        s.n_kv = stage("norm", 1)
        s.w_kv = Linear(ring, 2 * HM)
        s.prep_k = (stage("prep", HM), MK, G_MK + HM * layer)
        s.n_mem = stage("norm", 1)
        s.w_q = Linear(ring, HM)
        s.prep_q = (stage("prep", HM), MQ, G_MQ + HM * layer)
        s.matt = stage("att", HM)
        s.mdec = stage("mdec", NB)
        s.mdec_seg = ring.segment(NB, (2,) * SLOTS)
        s.w_o = Linear(ring, KT, HM)
        s.n_mlp = stage("norm", 1)
        s.mlp = Linear(ring, 2 * FF // P)
        layers.append(s)
    ev, od = layers
    gathered = [ev.n_mem, ev.n_mlp, od.n_mix, od.n_mem, od.n_mlp]
    for i, st in enumerate(gathered):
        st.gather = i
    ev.n_mlp.gain, od.n_mlp.gain, od.n_mix.gain = GN_MLP, GN_MLP + KT, GN_MIX + KT
    for i, st in enumerate([ev.n_mix, ev.n_kv, od.n_kv]):
        st.whole = i
    calls = [call for s in layers for call in (s.prep, [s.prep_k], [s.prep_q])]

    with ExitStack() as ctx:
        def sb(name, shape, dt=F32):
            return ctx.enter_context(nc.sbuf_tensor(name, shape, dt))

        sems = {}

        def sem(name):
            if name not in sems:
                sems[name] = ctx.enter_context(nc.semaphore(name))
            return sems[name]

        X = sb("x", [P, KT, T])
        HT = sb("ht", [P, KT, T])
        CORE = sb("core", [P, 4 * P + 2 * T])
        GAIN = sb("gain", [P, G_END])
        SCL = sb("scl", [P, S_END + 1])
        PT = sb("pages", [1, NB * NPG], I32)
        GROW = sb("gate_rows", [P, 3, 3 * H])
        GDEC = sb("gate_dec", [NS, NB * 3])
        PMEM = sb("stats", [P, 64])
        RING = sb("ring", [P, SLOTS, SLOT])
        RMS = sb("rms", [P, T])
        WH = sb("w_hi", [P, CHUNKS, CH], F32R)
        WL = sb("w_lo", [P, CHUNKS, CH], F32R)
        base = (nc.sbuf_base + 31) // 32 * 32
        sb("region", [P, ZF + BIG_TILES * T])

        def at(name, shape, offset, dt=F32):
            return nc.alloc_sbuf_tensor_at(name, shape, dt, offset=base + 4 * offset)

        A = at("arena", [P, ZF], 0)
        XH = at("x_hi", [P, KT, T], 0, F32R)
        XL = at("x_lo", [P, KT, T], KT * T, F32R)
        BIG = at("big", [P, BIG_TILES, T], ZF)
        HH = at("hid_hi", [P, KT, T], ZF, F32R)
        HL = at("hid_lo", [P, KT, T], ZF + KT * T, F32R)
        RB = at("relu", [P, 2, T], ZF + 2 * KT * T)
        QB = at("relu2", [P, 2, T], ZF + (2 * KT + 2) * T)
        MX = BIG[:, 16:16 + KT, 0:NM]
        PS = ctx.enter_context(nc.psum_tensor("ps", [P, 8, 512], F32))

        IDENT, ONES, ROT64, ROT32 = (CORE[:, i * P:(i + 1) * P] for i in range(4))
        COSD, SIND = (CORE[:, 4 * P + i * T:4 * P + (i + 1) * T] for i in range(2))
        bigf = BIG[:, :, :].rearrange("p k t -> p (k t)")
        EVT = A[:, 5888:]
        ODT = bigf[:, OD_TILES * T:]

        def dyn(buf, i, c0=0, c1=T):
            return buf[:, bass.ds(i, 1), c0:c1].rearrange("p o c -> p (o c)")

        def row(buf, i, n):
            return buf[:, bass.ds(i, n)]

        def carve(sizes, start=0):
            out, at = [], start
            for n in sizes:
                out.append(A[:, at:at + n])
                at += n
            assert at <= 5888, at
            return out

        ring_full = [sem(f"ring_full{i}") for i in range(SLOTS)]
        ring_used = sem("ring_used")
        w_hi, w_lo, w_used = sem("w_hi"), sem("w_lo"), sem("w_used")
        tile_free = sem("tile_free")
        hid_hi, hid_sq, hid_lo = sem("hid_hi"), sem("hid_sq"), sem("hid_lo")
        x_hi, x_lo = sem("x_hi"), sem("x_lo")
        mem_in = sem("mem_in")
        consts_in, tables_in, outs_out = sem("consts_in"), sem("tables_in"), sem("outs_out")
        table_value = {"ret": 16, "dil": 32, "lru": 48, "nsa": 80}
        out_value = {"dil": 16, "mem0": 32, "lx": 48, "lru": 64, "nsa": 80, "mem1": 96}
        EPSC = SCL[:, S_END:S_END + 1]

        def slot(seg, j):
            return RING[:, seg.slot(j), :]

        def skewed(eng, n, first, step, last):
            first()
            with eng.Fori(0, n - 1) as i:
                step(i)
            last(n - 1)

        scratch0 = 50 * T
        sqb = [bigf[:, scratch0 + i * T:scratch0 + (i + 1) * T] for i in range(4)]
        t_ln, t_acc = (bigf[:, scratch0 + i * T:scratch0 + (i + 1) * T] for i in (4, 5))
        sq_in, acc_in = sem("squares_in"), sem("squares_added")
        ADDS = KT + 2

        def gather_act(act, st, j, it):
            act.wait_ge(acc_in, it * 4 + (ADDS * st.gather + j + 3))
            act.activation(sqb[j % 4], dyn(X, it * 4 + j), ACT.Square).then_inc(sq_in, 1)
            if st.gain is not None:
                act.activation(dyn(HT, it * 4 + j), dyn(X, it * 4 + j), ACT.Identity,
                               scale=row(GAIN, it * 4 + (st.gain + j), 1)).then_inc(sem("scaled"), 1)

        def gather_start(dve, st):
            dve.memset(sqb[3], 0.0)
            dve.memset(t_acc, 0.0).then_inc(acc_in, 1)

        def gather_dve(dve, st, j, it):
            dve.wait_ge(acc_in, it * 4 + (ADDS * st.gather + 5 + j))
            dve.wait_ge(sq_in, it * 4 + (KT * st.gather + j + 1))
            dve.tensor_tensor(t_acc, t_acc, sqb[(j + 3) % 4], ALU.add).then_inc(acc_in, 1)

        def after_gather(eng, st):
            eng.wait_ge(acc_in, 4 + ADDS * (st.gather + 1))

        def norm_act(act, st, src, n, groups, w):
            weights_act(act, w, 0, 0, (0,))
            for i in range(KT):
                if st.gather is None:
                    if i >= 4:
                        act.wait_ge(sem("norm_summed"), KT * st.whole + i - 3)
                    act.activation(sqb[i % 4][:, 0:n], src[:, i, 0:n], ACT.Square).then_inc(sem("norm_sq"), 1)
                if i % 4 == 3:
                    act.wait_ge(sem("scaled"), KT * st.base + i + 1)
                    act.activation(XH[:, i - 3:i + 1, 0:n], HT[:, i - 3:i + 1, 0:n], ACT.Copy).then_inc(x_hi, 1)
            weights_act(act, w, 0, 0, (1,))
            weights_act(act, w, 1, 0)
            if st.gather is None:
                act.wait_ge(sem("norm_summed"), KT * (st.whole + 1))
            else:
                act.wait_ge(sem("gather_summed"), st.gather + 1)
            act.activation(t_ln[:, 0:n], PS[:, 4, 0:n], ACT.Ln, scale=1.0 / D, bias=EPSC).then_inc(sem("norm_ln"), 1)
            act.wait_ge(sem("norm_ln"), st.at())
            act.activation(RMS[:, 0:n], t_ln[:, 0:n], ACT.Exp, scale=-0.5).then_inc(sem("norm_rms"), 1)
            act.wait_ge(sem("norm_rms"), st.at())

        def norm_pe(pe, st, n):
            if st.gather is not None:
                after_gather(pe, st)
                pe.matmul(PS[:, 4, 0:n], ONES, t_acc, start=True, stop=True).then_inc(sem("gather_summed"), 1)
                return
            for i in range(KT):
                pe.wait_ge(sem("norm_sq"), KT * st.whole + i + 1)
                pe.matmul(PS[:, 4, 0:n], ONES, sqb[i % 4][:, 0:n], start=(i == 0), stop=(i == KT - 1)).then_inc(sem("norm_summed"), 1)

        def norm_dve(dve, st, src, gain, n, groups, w):
            def remainders(g):
                split_dve(dve, groups[g:g + 1], n, g)
                if g == 1:
                    weights_dve(dve, w, 0, 0, (0,))
                if g == 3:
                    weights_dve(dve, w, 0, 0, (1,))
                    weights_dve(dve, w, 1, 0)

            for i in range(KT):
                if st.gain is None:
                    dve.tensor_scalar(HT[:, i, 0:n], src[:, i, 0:n], GAIN[:, gain + i:gain + i + 1], None, ALU.mult).then_inc(sem("scaled"), 1)
                if i % 4 == 3 and i > 4:
                    remainders(i // 4 - 1)
            remainders(3)

        class Groups:

            def __init__(self):
                self.n = 0

            def __call__(self, n):
                self.n += n
                return range(self.n - n, self.n)

        def split_act(act, groups, cols):
            for i, g in enumerate(groups):
                act.activation(XH[:, 4 * i:4 * i + 4, 0:cols], HT[:, 4 * i:4 * i + 4, 0:cols], ACT.Copy).then_inc(x_hi, 1)

        def split_dve(dve, groups, cols, first=0):
            for i, g in enumerate(groups, first):
                dve.wait_ge(x_hi, g + 1)
                dve.tensor_tensor(XL[:, 4 * i:4 * i + 4, 0:cols], HT[:, 4 * i:4 * i + 4, 0:cols],
                                  XH[:, 4 * i:4 * i + 4, 0:cols].bitcast(F32), ALU.subtract).then_inc(x_lo, 1)

        def weights_act(act, w, j, it, halves=None):
            cw = CH if w.per == 2 else w.kt * P
            act.wait_ge(ring_full[w.seg.slot(j)], w.seg.arrived(j, it))
            for half in halves or range(w.per):
                c = w.per * j + half
                act.wait_ge(w_used, it * (4 * w.per) + (w.chunk + c + 1))
                act.activation(WH[:, (w.chunk + c) % CHUNKS, 0:cw], slot(w.seg, j)[:, half * CH:half * CH + cw], ACT.Copy).then_inc(w_hi, 1)

        def weights_dve(dve, w, j, it, halves=None):
            cw = CH if w.per == 2 else w.kt * P
            for half in halves or range(w.per):
                c = w.per * j + half
                dve.wait_ge(w_hi, it * (4 * w.per) + (w.chunk + c + 1))
                dve.tensor_tensor(WL[:, (w.chunk + c) % CHUNKS, 0:cw], slot(w.seg, j)[:, half * CH:half * CH + cw],
                                  WH[:, (w.chunk + c) % CHUNKS, 0:cw].bitcast(F32), ALU.subtract)\
                   .then_inc(ring_used if half == w.per - 1 else w_lo, 1)

        def unit_pe(pe, w, j, it, hi, lo, cols, groups=None):
            bank = PS[:, (w.tile + j) % 4, 0:cols]
            pe.wait_ge(tile_free, it * 4 + (w.tile + j + 1))
            kc = w.kt // w.per
            for half in range(w.per):
                c = w.per * j + half
                buf = (w.chunk + c) % CHUNKS
                pe.wait_ge(w_hi, it * (4 * w.per) + (w.chunk + c + 1))
                for k in range(kc):
                    if groups and (half * kc + k) % 4 == 0:
                        pe.wait_ge(x_lo, groups[(half * kc + k) // 4] + 1)
                    h = WH[:, buf, k * P:(k + 1) * P]
                    pe.matmul(bank, h, hi[:, half * kc + k, 0:cols], start=(half == 0 and k == 0), stop=False)
                    pe.matmul(bank, h, lo[:, half * kc + k, 0:cols], start=False, stop=False)
                if half == w.per - 1:
                    pe.wait_ge(ring_used, w.seg.used(j, it))
                else:
                    pe.wait_ge(w_lo, it * 4 + (w.half + j + 1))
                for k in range(kc):
                    mm = pe.matmul(bank, WL[:, buf, k * P:(k + 1) * P], hi[:, half * kc + k, 0:cols],
                                   start=False, stop=(half == w.per - 1 and k == kc - 1))
                mm.then_inc(w_used, 1)

        def multiplied(w, j, it):
            return it * (4 * w.per) + (4 + w.chunk + w.per * (j + 1))

        def lin_pe(pe, w, groups, cols=T):
            with pe.Fori(0, w.n // 4) as it:
                for j in range(4):
                    unit_pe(pe, w, j, it, XH, XL, cols, groups)
            for u in range(w.n // 4 * 4, w.n):
                unit_pe(pe, w, u, 0, XH, XL, cols, groups)

        def mlp_pe(pe, w, n, groups):
            with pe.Fori(0, 4) as q:
                with pe.Fori(0, 4) as it:
                    for j in range(4):
                        unit_pe(pe, w, j, q * 8 + it, XH, XL, T, groups)
                with pe.Fori(0, 4) as it:
                    pe.wait_ge(hid_lo, q * KT + (n * 4 * KT + KT))
                    for j in range(4):
                        unit_pe(pe, w, j + 4 * 4, q * 8 + it, HH, HL, T)

        def weights_ahead(eng, w, split):
            for u in range(w.ahead):
                split(eng, w, u, 0)

        def rounds_of(eng, w, step, split, split_first=False):
            def both(j, it, more=True):
                if more and split_first:
                    split(eng, w, j + w.ahead, it)
                step(j, it)
                if more and not split_first:
                    split(eng, w, j + w.ahead, it)
            loops = (w.n - w.ahead) // 4
            if loops > 0:
                with eng.Fori(0, loops) as it:
                    for j in range(4):
                        both(j, it)
            for u in range(4 * loops, w.n):
                both(u, 0, u + w.ahead < w.n)

        def lin_act(act, w, gather=None):
            def step(j, it):
                if gather:
                    act.wait_ge(tile_free, it * 4 + (5 + w.tile + j))
                    gather_act(act, gather, j, it)
            rounds_of(act, w, step, weights_act, split_first=True)
            if gather:
                after_gather(act, gather)

        def lin_dve(dve, w, norm=None, tile0=0, cols=T, gather=None):
            if norm:
                dve.wait_ge(sem("norm_rms"), norm.at())
            if gather:
                gather_start(dve, gather)

            def step(j, it):
                dve.wait_ge(w_used, multiplied(w, j, it))
                bank = PS[:, (w.tile + j) % 4, 0:cols]
                if norm:
                    out = dyn(BIG, it * 4 + (tile0 + j), 0, cols)
                    dve.tensor_tensor(out, bank, RMS[:, 0:cols], ALU.mult).then_inc(tile_free, 1)
                else:
                    x = dyn(X, it * 4 + j)
                    dve.tensor_tensor(x, x, bank, ALU.add).then_inc(tile_free, 1)
                    gather_dve(dve, gather, j, it)
            rounds_of(dve, w, step, weights_dve)
            if gather:
                gather_dve(dve, gather, KT, 0)

        def mlp_rounds(eng, w, up, down, split):
            def quarter(q, last):
                for step, first in ((up, 0), (down, 16)):
                    with eng.Fori(0, 3 if last and first else 4) as it:
                        for j in range(4):
                            step(q, j, it)
                            split(eng, w, first + j + w.ahead, q * 8 + it)
            with eng.Fori(0, 3) as q:
                quarter(q, False)
            quarter(3, True)
            for j in range(4):
                down(3, j, 3)
                if j + w.ahead < 4:
                    split(eng, w, w.n - 4 + j + w.ahead, 0)

        def mlp_act(act, w, n, gather):
            def down(q, j, it):
                if gather and isinstance(q, int):
                    act.wait_ge(tile_free, (q * 8 + it) * 4 + (16 + 5 + w.tile + j))
                    gather_act(act, gather, j, it)

            def up(q, j, it):
                act.wait_ge(tile_free, (q * 8 + it) * 4 + (5 + w.tile + j))
                act.activation(dyn(HH, it * 4 + j), RB[:, j % 2, :], ACT.Square).then_inc(hid_hi, 1)

            mlp_rounds(act, w, up, down, weights_act)
            if gather:
                after_gather(act, gather)

        def mlp_dve(dve, w, n, norm, gather):
            def up(q, j, it):
                now = q * KT + it * 4 + (n * 4 * KT + j + 1)
                dve.wait_ge(w_used, multiplied(w, j, q * 8 + it))
                dve.wait_ge(hid_hi, now)
                dve.scalar_tensor_tensor(out=RB[:, j % 2, :], in0=PS[:, (w.tile + j) % 4, 0:T], scalar=0.0, in1=RMS[:, 0:T],
                                         op0=ALU.max, op1=ALU.mult).then_inc(tile_free, 1)
                dve.wait_ge(tile_free, (q * 8 + it) * 4 + (5 + w.tile + j))
                dve.tensor_tensor(QB[:, j % 2, :], RB[:, j % 2, :], RB[:, j % 2, :], ALU.mult).then_inc(hid_sq, 1)
                dve.wait_ge(hid_sq, now)
                dve.wait_ge(hid_hi, now + 2)
                dve.tensor_tensor(dyn(HL, it * 4 + j), QB[:, j % 2, :], dyn(HH, it * 4 + j).bitcast(F32), ALU.subtract).then_inc(hid_lo, 1)

            def down(q, j, it):
                dve.wait_ge(w_used, multiplied(w, 16 + j, q * 8 + it))
                x = dyn(X, it * 4 + j)
                dve.tensor_tensor(x, x, PS[:, (w.tile + j) % 4, 0:T], ALU.add).then_inc(tile_free, 1)
                if gather and isinstance(q, int):
                    gather_dve(dve, gather, j, it)

            dve.wait_ge(sem("norm_rms"), norm.at())
            if gather:
                gather_start(dve, gather)
            mlp_rounds(dve, w, up, down, weights_dve)
            if gather:
                gather_dve(dve, gather, KT, 0)

        def after_tiles(eng, w):
            eng.wait_ge(tile_free, w.end)

        psq, prot, pt1, pt2, p_logs = carve([T, P, T, T, KT * T])
        plog = p_logs.rearrange("p (k t) -> p k t", t=T)

        def table(act, func):
            act.activation(PMEM[:, 63:64], EPSC, func)

        def prep_act(act, runs, n):
            table(act, ACT.Ln)
            for st, tile0, _ in runs:
                k0 = st.base - runs[0][0].base

                def squares(i):
                    act.activation(psq[:, 0:n], dyn(BIG, tile0 + i, 0, n), ACT.Square).then_inc(sem("prep_sq"), 1)

                def logarithm(i):
                    act.wait_ge(sem("prep_sum"), st.at(i))
                    act.activation(dyn(plog, k0 + i, 0, n), PS[:, 4, 0:n], ACT.Ln, scale=1.0 / HD, bias=EPSC).then_inc(sem("prep_ln"), 1)

                def step(i):
                    logarithm(i)
                    squares(i + 1)
                skewed(act, st.rounds, lambda: squares(0), step, logarithm)
            last = runs[-1][0]
            act.wait_ge(sem("prep_ln"), last.end)
            x = plog[:, 0:last.end - runs[0][0].base, 0:n]
            act.activation(x, x, ACT.Exp, scale=-0.5).then_inc(sem("prep_rms"), 1)

        def prep_pe(pe, runs, n, rope):
            for st, tile0, _ in runs:
                with pe.Fori(0, st.rounds) as it:
                    if rope:
                        pe.wait_ge(sem("prep_free"), st.at(it))
                        pe.matmul(PS[:, 5, 0:n], prot, dyn(BIG, it + tile0, 0, n), start=True, stop=True).then_inc(sem("prep_rot"), 1)
                    pe.wait_ge(sem("prep_sq"), st.at(it))
                    pe.matmul(PS[:, 4, 0:n], ONES, psq[:, 0:n], start=True, stop=True).then_inc(sem("prep_sum"), 1)

        def prep_dve(dve, chain, runs, run, n, rope):
            for st, tile0, gain in runs:
                if not rope:
                    dve.sem_inc(sem("prep_free"), st.rounds)
                    dve.sem_inc(sem("prep_rot"), st.rounds)
                    dve.wait_ge(sem("prep_sum"), st.end)
                    x = BIG[:, tile0:tile0 + st.rounds, 0:n]
                    g = GAIN[:, gain:gain + st.rounds].unsqueeze(2).broadcast_to([P, st.rounds, n])
                    chain(dve.tensor_tensor(x, x, g, ALU.mult))
                    continue

                if st.base > runs[0][0].base:
                    dve.wait_ge(sem("prep_rot"), st.base)
                dve.tensor_scalar(prot, ROT32, GAIN[:, gain:gain + 1], None, ALU.mult).then_inc(sem("prep_free"), 1)

                def rotated(i, more):
                    dve.wait_ge(sem("prep_rot"), st.at(i))
                    ins = dve.tensor_tensor(pt2[:, 0:n], PS[:, 5, 0:n], SIND[:, 0:n], ALU.mult)
                    if more:
                        ins.then_inc(sem("prep_free"), 1)
                    tile = dyn(BIG, tile0 + i, 0, n)
                    chain(dve.scalar_tensor_tensor(out=pt1[:, 0:n], in0=tile, scalar=GAIN[:, gain:gain + 1], in1=COSD[:, 0:n],
                                                   op0=ALU.mult, op1=ALU.mult))
                    dve.wait_ge(sem("prep_sum"), st.at(i))
                    chain(dve.tensor_tensor(tile, pt1[:, 0:n], pt2[:, 0:n], ALU.add))

                def step(i):
                    chain.enter(i, 2)
                    rotated(i, True)

                def last(i):
                    chain.leave(i)
                    rotated(i, False)
                skewed(dve, st.rounds, lambda: None, step, last)
            dve.wait_ge(sem("prep_rms"), run + 1)
            for st, tile0, _ in runs:
                k0 = st.base - runs[0][0].base
                x = BIG[:, tile0:tile0 + st.rounds, 0:n]
                dve.tensor_tensor(x, x, plog[:, k0:k0 + st.rounds, 0:n], ALU.mult).then_inc(sem("prep_done"), 1)

        prep_runs = {call[-1][0]: sum(len(c) for c in calls[:n + 1]) for n, call in enumerate(calls)}

        def after_prep(eng, st):
            eng.wait_ge(sem("prep_done"), prep_runs[st])

        (r_q, r_k, r_v, r_t1, r_t2, r_in, r_vr, r_kr, r_st, r_sn, r_vb, r_sp, r_ins, r_qd) = carve(
            [T, T, T, T, T, 384, 384, 384, 1024, 1024, 1024, P, NS, NS])
        R_DEC, R_KD, R_G4, R_MB = 0, H * TP, H * TP + 2 * H, H * TP + 3 * H
        R_DS = R_MB + H * NB
        R_QD = R_DS + H * NS
        R_COS, R_SIN, R_END = R_QD + H * NS, R_QD + H * NS + T, R_QD + H * NS + 2 * T
        COSR, SINR = EVT[:, R_COS:R_COS + T], EVT[:, R_SIN:R_SIN + T]

        def ret_act(act, st):
            after_tiles(act, ev.w_in)
            gate = BIG[:, RG:RG + H, :]
            act.activation(gate, gate, ACT.Silu).then_inc(sem("ret_silu"), 1)
            with act.Fori(0, H) as h:
                act.wait_ge(sem("ret_done"), h + 1)
                act.dma_start(r_st, a["state_ret"][bass.ds(h, 1)].rearrange("o d n -> (o d) n")).then_inc(sem("ret_st"), 16)
                act.activation(r_v, dyn(BIG, h + RV), ACT.Copy).then_inc(sem("ret_v"), 1)
                act.wait_ge(sem("ret_rows"), h + 1)
                act.activation(r_vr[:, 0:256], PS[:, 3, 0:256], ACT.Copy)
                act.activation(r_vr[0:NS, 256:384], PS[0:NS, 3, 256:384], ACT.Copy).then_inc(sem("ret_vr"), 1)
                act.wait_ge(sem("ret_sn"), h + 1)
                act.dma_start(o["ret_s"][bass.ds(h, 1)].rearrange("o d n -> (o d) n"), r_sn).then_inc(sem("ret_saved"), 16)
                act.dma_start(o["ret_p"][bass.ds(h, 1)].rearrange("o d n -> (o d) n"), r_sp).then_inc(sem("ret_saved"), 16)

        def ret_pe(pe, st):
            after_tiles(pe, ev.w_in)
            with pe.Fori(0, H) as h:
                pe.wait_ge(sem("ret_done"), h + 1)
                pe.matmul(PS[:, 0, 0:T], ROT64, dyn(BIG, h + RQ), start=True, stop=True)
                pe.matmul(PS[:, 1, 0:T], ROT64, dyn(BIG, h + RK), start=True, stop=True).then_inc(sem("ret_rot"), 1)
                pe.wait_ge(sem("ret_v"), h + 1)
                for i, w in ((0, P), (1, P), (2, NS)):
                    pe.matmul(PS[0:w, 3, i * P:(i + 1) * P], r_v[:, i * P:i * P + w], IDENT, start=True, stop=True)
                pe.wait_ge(sem("ret_qk"), h + 1)
                for i, w in ((0, P), (1, P), (2, NS)):
                    mm = pe.matmul(PS[0:w, 2, i * P:(i + 1) * P], r_k[:, i * P:i * P + w], IDENT, start=True, stop=True)
                mm.then_inc(sem("ret_rows"), 1)
                pe.matmul(PS[:, 4, 0:256], r_k[:, 0:P], r_q[:, 0:256], start=True, stop=True)
                pe.matmul(PS[:, 4, 256:384], r_k[:, P:256], r_q[:, P:256], start=True, stop=True)
                pe.matmul(PS[0:NS, 5, 0:NS], r_k[:, 256:T], r_q[:, 256:T], start=True, stop=True).then_inc(sem("ret_sc"), 1)
                pe.wait_ge(sem("ret_in"), h + 1)
                pe.matmul(PS[:, 6, 0:256], r_vr[:, 0:P], r_in[:, 0:256], start=True, stop=True)
                pe.matmul(PS[:, 6, P:256], r_vr[:, P:256], r_in[:, 256:384], start=False, stop=True, skip_group_check=True)
                pe.wait_ge(sem("ret_st"), 16 * h + 16)
                pe.matmul(PS[:, 7, 0:NS], r_vr[0:NS, 256:384], r_ins[0:NS, :], start=True, stop=True, skip_group_check=True)
                for b in range(NB):
                    mm = pe.matmul(PS[:, 7, b * TS:(b + 1) * TS], r_st[:, b * P:(b + 1) * P], r_qd[:, b * TS:(b + 1) * TS],
                                   start=False, stop=True, skip_group_check=True)
                mm.then_inc(sem("ret_o"), 1)
                pe.matmul(PS[:, 0, 0:P], r_kr[:, 0:P], r_vr[:, 0:P], start=True, stop=False)
                pe.matmul(PS[:, 0, 0:P], r_kr[:, P:256], r_vr[:, P:256], start=False, stop=True)
                for half in range(2):
                    mm = pe.matmul(PS[:, 1 + half, 0:512], r_kr[0:NS, 256:384], r_vb[0:NS, half * 512:(half + 1) * 512], start=True, stop=True)
                mm.then_inc(sem("ret_new"), 1)

        def ret_dve(dve, chain, st):
            tab = EVT
            after_tiles(dve, ev.w_in)
            dve.wait_ge(tables_in, table_value["ret"])
            dve.wait_ge(sem("ret_silu"), 1)
            with dve.Fori(0, H) as h:
                chain.enter(h, 3)
                dve.wait_ge(sem("ret_rot"), h + 1)
                for src, bank, dst, s in ((RK, 1, r_k, 1.0), (RQ, 0, r_q, SCALE)):
                    dve.scalar_tensor_tensor(out=r_t1, in0=dyn(BIG, h + src), scalar=s, in1=COSR, op0=ALU.mult, op1=ALU.mult)
                    chain(dve.scalar_tensor_tensor(out=r_t2, in0=PS[:, bank, 0:T], scalar=s, in1=SINR, op0=ALU.mult, op1=ALU.mult))
                    ins = dve.tensor_tensor(dst, r_t1, r_t2, ALU.add)
                    if src == RK:
                        chain(ins)
                ins.then_inc(sem("ret_qk"), 1)
                dve.wait_ge(sem("ret_qk"), h + 1)
                dve.wait_ge(sem("ret_rows"), h + 1)
                kd = tab[:, R_KD:R_KD + 2 * H]
                for i in range(2):
                    dve.tensor_scalar(r_kr[:, i * P:(i + 1) * P], PS[:, 2, i * P:(i + 1) * P], row(kd, h * 2 + i, 1), None, ALU.mult)
                dve.tensor_copy(r_kr[0:NS, 256:384], PS[0:NS, 2, 256:384])
                dve.wait_ge(sem("ret_sc"), h + 1)
                dve.tensor_tensor(r_in[:, 0:256], PS[:, 4, 0:256], row(tab, h * TP, TP), ALU.mult)
                dve.tensor_tensor(r_in[:, 256:384], PS[:, 4, 256:384], row(tab, h * TP, P), ALU.mult)
                dve.tensor_tensor(r_ins[0:NS, :], PS[0:NS, 5, 0:NS], tab[0:NS, bass.ds(h * NS + R_DS, NS)], ALU.mult)
                dve.tensor_tensor(r_qd, r_q[:, 256:T], row(tab, h * NS + R_QD, NS), ALU.mult)
                dve.wait_ge(sem("ret_vr"), h + 1)
                mb = tab[0:NS, bass.ds(h * NB + R_MB, NB)]
                dve.tensor_tensor(r_vb[0:NS, :].rearrange("p (b v) -> p b v", b=NB),
                                  r_vr[0:NS, 256:384].unsqueeze(1).broadcast_to([NS, NB, P]),
                                  mb.unsqueeze(2).broadcast_to([NS, NB, P]), ALU.mult).then_inc(sem("ret_in"), 1)
                dve.wait_ge(sem("ret_o"), h + 1)
                dve.tensor_copy(dyn(HT, h, 0, TP), PS[:, 6, 0:TP])
                dve.wait_ge(sem("ret_new"), h + 1)
                dve.wait_ge(sem("ret_saved"), h * 32 + 32)
                dve.tensor_copy(r_sp, PS[:, 0, 0:P])
                g4 = row(tab, h + R_G4, 1)
                for half in range(2):
                    c = slice(half * 512, (half + 1) * 512)
                    ins = dve.scalar_tensor_tensor(out=r_sn[:, c], in0=r_st[:, c], scalar=g4, in1=PS[:, 1 + half, 0:512],
                                                   op0=ALU.mult, op1=ALU.add)
                ins.then_inc(sem("ret_sn"), 1)
                dve.tensor_copy(dyn(HT, h, TP, T), PS[:, 7, 0:NS]).then_inc(sem("ret_done"), 1)
            chain.leave(H)

        def gn_act(act):
            table(act, ACT.Ln)

            def squares(h):
                act.wait_ge(sem("gn_cen"), h + 1)
                act.activation(psq, dyn(HT, h), ACT.Square).then_inc(sem("gn_sq"), 1)

            def logarithm(h):
                act.wait_ge(sem("gn_var"), h + 1)
                act.activation(dyn(plog, h), PS[:, 4, 0:T], ACT.Ln, scale=1.0 / HD, bias=EPSC).then_inc(sem("gn_ln"), 1)

            def step(h):
                logarithm(h)
                squares(h + 1)
            skewed(act, H, lambda: squares(0), step, logarithm)
            act.wait_ge(sem("gn_ln"), H)
            x = plog[:, 0:H, :]
            act.activation(x, x, ACT.Exp, scale=-0.5).then_inc(sem("gn_rstd"), 1)

        def gn_pe(pe):
            def mean(h):
                pe.matmul(PS[:, 3, 0:T], ONES, dyn(HT, h), start=True, stop=True).then_inc(sem("gn_mean"), 1)

            def variance(h):
                pe.wait_ge(sem("gn_sq"), h + 1)
                pe.matmul(PS[:, 4, 0:T], ONES, psq, start=True, stop=True).then_inc(sem("gn_var"), 1)

            def step(h):
                pe.wait_ge(sem("gn_cen"), h + 1)
                mean(h + 1)
                variance(h)
            skewed(pe, H, lambda: mean(0), step, variance)

        def gn_dve(dve, chain):
            with dve.Fori(0, H) as h:
                dve.wait_ge(sem("gn_mean"), h + 1)
                head = dyn(HT, h)
                dve.scalar_tensor_tensor(out=head, in0=PS[:, 3, 0:T], scalar=-1.0 / HD, in1=head,
                                         op0=ALU.mult, op1=ALU.add).then_inc(sem("gn_cen"), 1)
            gate, heads_ = BIG[:, RG:RG + H, :], HT[:, 0:H, :]
            gain = GAIN[:, G_RET:G_RET + H].unsqueeze(2).broadcast_to([P, H, T])
            chain(dve.tensor_tensor(gate, gate, gain, ALU.mult))
            dve.wait_ge(sem("gn_rstd"), 1)
            chain(dve.tensor_tensor(heads_, heads_, plog[:, 0:H, :], ALU.mult))
            dve.tensor_tensor(heads_, heads_, gate, ALU.mult).then_inc(sem("gn_done"), 1)

        (a_q, a_v, a_sm, a_p, a_pt, a_vr) = carve([T, T, 512, 512, 512, 384])
        a_mx, a_nm, a_l, a_r = (PMEM[:, i * 2:i * 2 + 2] for i in range(4))
        VN = bigf[:, 0:H * P]

        def att_act(act, st, tq, tv, rows_out):
            def queries(i):
                act.activation(a_q, dyn(BIG, tq + i), ACT.Copy).then_inc(sem("att_q"), 1)

            def values(i):
                act.activation(a_v[:, 0:VW[rows_out]], dyn(BIG, tv + i, 0, VW[rows_out]), ACT.Copy).then_inc(sem("att_v"), 1)

            def exponentials(i):
                act.wait_ge(sem("att_nm"), st.at(i))
                for q in range(2):
                    ins = act.activation(a_p[:, q * TP:(q + 1) * TP], a_sm[:, q * TP:(q + 1) * TP], ACT.Exp, bias=a_nm[:, q:q + 1],
                                         accum_out=a_l[:, q:q + 1])
                ins.then_inc(sem("att_exp"), 1)

            def value_rows(i):
                act.wait_ge(sem("att_vt"), st.at(i))
                act.activation(a_vr[:, 0:256], PS[:, 5, 0:256], ACT.Copy)
                if rows_out:
                    act.activation(VN[0:NS, bass.ds(i * P, P)], PS[0:NS, 5, 256:384], ACT.Copy)

            def turned(i):
                act.wait_ge(sem("att_turned"), st.at(i))
                act.activation(a_pt, PS[:, 6, 0:512], ACT.Copy).then_inc(sem("att_pt"), 1)

            def first():
                queries(0)
                values(0)

            def step(i):
                act.wait_ge(sem("att_sc"), st.at(i))
                queries(i + 1)
                exponentials(i)
                value_rows(i)
                values(i + 1)
                turned(i)

            def last(i):
                exponentials(i)
                value_rows(i)
                turned(i)
            skewed(act, st.rounds, first, step, last)

        def att_pe(pe, st, tk, rows_out):
            def scores(i):
                pe.wait_ge(sem("att_q"), st.at(i))
                for q in range(2):
                    mm = pe.matmul(PS[:, 4, q * TP:(q + 1) * TP], a_q[:, q * P:(q + 1) * P], dyn(BIG, tk + i, 0, TP), start=True, stop=True)
                mm.then_inc(sem("att_sc"), 1)

            def value_rows(i):
                pe.wait_ge(sem("att_v"), st.at(i))
                for k, w in ((0, P), (1, P), (2, NS))[:3 if rows_out else 2]:
                    mm = pe.matmul(PS[0:w, 5, k * P:(k + 1) * P], a_v[:, k * P:k * P + w], IDENT, start=True, stop=True)
                mm.then_inc(sem("att_vt"), 1)

            def outputs(i):
                pe.wait_ge(sem("att_p"), st.at(i))
                for k in range(2):
                    for q in range(2):
                        mm = pe.transpose(PS[:, 6, k * TP + q * P:k * TP + (q + 1) * P], a_p[:, q * TP + k * P:q * TP + (k + 1) * P], IDENT)
                mm.then_inc(sem("att_turned"), 1)
                pe.wait_ge(sem("att_done"), i + (st.base + 1))
                pe.wait_ge(sem("att_pt"), st.at(i))
                for k in range(2):
                    mm = pe.matmul(PS[:, 7, 0:TP], a_vr[:, k * P:(k + 1) * P], a_pt[:, k * TP:(k + 1) * TP], start=(k == 0), stop=(k == 1))
                mm.then_inc(sem("att_o"), 1)

            def first():
                scores(0)
                value_rows(0)

            def step(i):
                pe.wait_ge(sem("att_nm"), st.at(i))
                scores(i + 1)
                outputs(i)
                value_rows(i + 1)
            skewed(pe, st.rounds, first, step, outputs)

        def att_dve(dve, chain, st, bias, cat):
            def probabilities(i):
                dve.wait_ge(sem("att_sc"), st.at(i))
                if bias is None:
                    chain(dve.tensor_copy(a_sm, PS[:, 4, 0:512]))
                else:
                    chain(dve.tensor_tensor(a_sm, PS[:, 4, 0:512], bias, ALU.add))
                chain(dve.tensor_reduce(a_mx, a_sm.rearrange("p (q k) -> p q k", q=2), AXX, ALU.max))
                dve.tensor_scalar(a_nm, a_mx, -1.0, None, ALU.mult).then_inc(sem("att_nm"), 1)
                dve.wait_ge(sem("att_exp"), st.at(i))
                chain(dve.reciprocal(a_r, a_l))
                for q in range(2):
                    ins = dve.tensor_scalar(a_p[:, q * TP:(q + 1) * TP], a_p[:, q * TP:(q + 1) * TP], a_r[:, q:q + 1], None, ALU.mult)
                ins.then_inc(sem("att_p"), 1)

            def output(i):
                dve.wait_ge(sem("att_o"), st.at(i))
                dve.tensor_copy(dyn(HT, i + cat, 0, TP), PS[:, 7, 0:TP]).then_inc(sem("att_done"), 1)

            def step(i):
                chain.enter(i, 3)
                probabilities(i + 1)
                output(i)
            skewed(dve, st.rounds, lambda: probabilities(0), step, lambda i: (chain.leave(i), output(i)))

        VW = {True: T, False: TP}

        def after_att(eng, st):
            eng.wait_ge(sem("att_done"), 1 + st.end)

        NKN = NKD + PAD
        (d_qb, d_sm, d_p, d_pt) = carve([H * 36, NKN, NKN, 6 * NS], 0)
        D_B, D_BD, D_BN = 0, 512, 512 + NKD
        s_mx, s_nm, s_l, s_r = (PMEM[0:NS, 8 + i * 4:12 + i * 4] for i in range(4))

        def diag(buf, n, w):
            return buf.rearrange("p (h c) -> p h c", c=n * w + w)[:, :, 0:w]

        def dil_act(act, st):
            with act.Fori(0, NB) as b:
                act.wait_ge(sem("dil_nm"), b + 1)
                act.activation(d_p[0:NS, 0:NKD + NS], d_sm[0:NS, 0:NKD + NS], ACT.Exp, bias=s_nm[:, 0:1], accum_out=s_l[:, 0:1]).then_inc(sem("dil_exp"), 1)

        def dil_pe(pe):
            def scores(b, seg, r):
                pe.wait_ge(sem("dil_q"), b + 1)
                for h in range(H):
                    j = h // 2
                    if h % 2 == 0:
                        pe.wait_ge(ring_full[seg.slot(j)], seg.arrived(j, r))
                    K = slot(seg, j)[:, 0:2 * NKD].rearrange("p (h k) -> p h k", h=2)[:, h % 2, :]
                    q = d_qb[:, h * NS:(h + 1) * NS]
                    first, last = h == 0, h == H - 1
                    pe.matmul(PS[0:NS, 6, 0:NS], q, BIG[:, DK + h, TP:T], start=first, stop=last)
                    pe.matmul(PS[0:NS, 5, 0:NKD - 512], q, K[:, 512:NKD], start=first, stop=last)
                    mm = pe.matmul(PS[0:NS, 4, 0:512], q, K[:, 0:512], start=first, stop=last)
                    if h % 2 == 1:
                        mm.then_inc(ring_used, 1)

            def outputs(b, seg, r, j0):
                pe.wait_ge(sem("dil_p"), b + 1)
                for i in range(6):
                    mm = pe.matmul(PS[:, 7, i * NS:(i + 1) * NS], d_p[0:NS, i * P:(i + 1) * P], IDENT[0:NS, 0:NS], start=True, stop=True)
                mm.then_inc(sem("dil_turned"), 1)
                pe.wait_ge(sem("dil_pt"), b + 1)
                for h in range(H):
                    j = j0 + h // 2
                    if h % 2 == 0:
                        pe.wait_ge(ring_full[seg.slot(j)], seg.arrived(j, r))
                    V = slot(seg, j)[:, 0:5 * 256].rearrange("p (t h d) -> p t h d", t=5, h=2)
                    out = PS[:, 3, h * TS:(h + 1) * TS]
                    pe.matmul(out, VN[0:NS, h * P:(h + 1) * P], d_pt[0:NS, 5 * NS + h * TS:5 * NS + (h + 1) * TS], start=True, stop=False)
                    for i in range(5):
                        mm = pe.matmul(out, V[:, i, h % 2, :], d_pt[:, i * NS + h * TS:i * NS + (h + 1) * TS], start=False, stop=(i == 4))
                    if h % 2 == 1:
                        mm.then_inc(ring_used, 1)

            def step(b):
                scores(b + 1, ev.dil_seg, b)
                outputs(b, ev.dil_seg, b, 4)
            skewed(pe, NB, lambda: scores(0, ev.dil_first, 0), step, lambda b: outputs(b, ev.dil_last, 0, 0))

        def dil_dve(dve, chain):
            tab = EVT
            chain(dve.memset(d_qb, 0.0))
            dve.memset(d_p[:, 0:NKN], 0.0)
            chain(dve.memset(d_sm[:, 0:NKN], 0.0))

            def queries(b):
                dve.tensor_copy(diag(d_qb, H, TS), BIG[:, DQ:DQ + H, bass.ds(b * TS + TP, TS)]).then_inc(sem("dil_q"), 1)

            def biased(b, scored):
                dve.wait_ge(ring_used, scored)
                dve.tensor_tensor(d_sm[0:NS, 0:512], PS[0:NS, 4, 0:512], tab[0:NS, D_BD:D_BD + 512], ALU.add)
                dve.tensor_tensor(d_sm[0:NS, 512:NKD], PS[0:NS, 5, 0:NKD - 512], tab[0:NS, D_BD + 512:D_BD + NKD], ALU.add)
                chain(dve.tensor_tensor(d_sm[0:NS, NKD:NKD + NS], PS[0:NS, 6, 0:NS], tab[0:NS, bass.ds(b * NS + D_BN, NS)], ALU.add))

            def probabilities(b):
                chain(dve.tensor_reduce(s_mx[:, 0:1], d_sm[0:NS, 0:NKD + NS], AXX, ALU.max))
                dve.tensor_scalar(s_nm[:, 0:1], s_mx[:, 0:1], -1.0, None, ALU.mult).then_inc(sem("dil_nm"), 1)
                dve.wait_ge(sem("dil_exp"), b + 1)
                chain(dve.reciprocal(s_r[:, 0:1], s_l[:, 0:1]))
                dve.tensor_scalar(d_p[0:NS, 0:NKD + NS], d_p[0:NS, 0:NKD + NS], s_r[:, 0:1], None, ALU.mult).then_inc(sem("dil_p"), 1)
                dve.wait_ge(sem("dil_turned"), b + 1)
                dve.tensor_copy(d_pt, PS[:, 7, 0:6 * NS]).then_inc(sem("dil_pt"), 1)

            def output(b, multiplied):
                dve.wait_ge(ring_used, multiplied)
                dve.tensor_copy(HT[:, H:2 * H, bass.ds(b * TS + TP, TS)],
                                PS[:, 3, 0:NS].rearrange("p (h t) -> p h t", h=H)).then_inc(sem("dil_done"), 1)

            def first():
                queries(0)
                biased(0, ev.dil_first.used(3))
                queries(1)
                probabilities(0)

            with_next = ev.dil_seg
            first()
            with dve.Fori(0, NB - 2) as b:
                chain.enter(b, 3)
                biased(b + 1, with_next.used(3, b))
                output(b, with_next.used(7, b))
                queries(b + 2)
                probabilities(b + 1)
            chain.leave(NB - 2)
            biased(NB - 1, with_next.used(3, NB - 2))
            output(NB - 2, with_next.used(7, NB - 2))
            probabilities(NB - 1)
            output(NB - 1, ev.dil_last.used(3))

        MSTEP = SLOTS
        MR = HM * TS
        (m_qb, m_sm, m_p, m_pt) = carve([HM * (MR + TS), NM, NM, 2 * MR])

        def mdec_act(act, st):
            with act.Fori(0, NB) as b:
                act.wait_ge(sem("mdec_nm"), st.at(b))
                act.activation(m_p[0:MR, :], m_sm[0:MR, :], ACT.Exp, bias=s_nm[0:MR, 1:2], accum_out=s_l[0:MR, 1:2]).then_inc(sem("mdec_exp"), 1)

        def mdec_pe(pe, st, seg):
            with pe.Fori(0, NB // MSTEP) as it:
                def scores(j):
                    pe.wait_ge(sem("mdec_q"), it * MSTEP + (st.base + j + 1))
                    pe.wait_ge(ring_full[seg.slot(j)], seg.arrived(j, it))
                    K = slot(seg, j)[:, 0:HM * NM].rearrange("p (h k) -> p h k", h=HM)
                    for h in range(HM):
                        mm = pe.matmul(PS[0:MR, 4, 0:NM], m_qb[:, h * MR:(h + 1) * MR], K[:, h, :], start=(h == 0), stop=(h == HM - 1))
                    mm.then_inc(sem("mdec_sc"), 1)

                def outputs(j):
                    now = it * MSTEP + (st.base + j + 1)
                    V = slot(seg, j)[:, HM * NM:2 * HM * NM].rearrange("p (t h d) -> p t h d", t=2, h=HM)
                    pe.wait_ge(sem("mdec_p"), now)
                    for i in range(2):
                        mm = pe.matmul(PS[:, 5, i * MR:(i + 1) * MR], m_p[0:MR, i * P:(i + 1) * P], IDENT[0:MR, 0:MR], start=True, stop=True)
                    mm.then_inc(sem("mdec_turned"), 1)
                    pe.wait_ge(sem("mdec_pt"), now)
                    for h in range(HM):
                        for i in range(2):
                            mm = pe.matmul(PS[:, 6, h * TS:(h + 1) * TS], V[:, i, h, :], m_pt[:, i * MR + h * TS:i * MR + (h + 1) * TS],
                                           start=(i == 0), stop=(i == 1))
                    mm.then_inc(ring_used, 1)

                scores(0)
                for j in range(MSTEP):
                    if j + 1 < MSTEP:
                        scores(j + 1)
                    outputs(j)

        def mdec_dve(dve, chain, st, seg):
            chain(dve.memset(m_qb, 0.0))
            with dve.Fori(0, NB // MSTEP) as it:
                chain.enter(it, 3 * MSTEP)

                def cols(j):
                    return bass.ds(it * (MSTEP * TS) + (TP + j * TS), TS)

                def queries(j):
                    dve.tensor_copy(diag(m_qb, HM, TS), BIG[:, MQ:MQ + HM, cols(j)]).then_inc(sem("mdec_q"), 1)

                def output(j):
                    dve.wait_ge(ring_used, seg.used(j, it))
                    dve.tensor_copy(HT[:, 0:HM, cols(j)], PS[:, 6, 0:MR].rearrange("p (h t) -> p h t", h=HM)).then_inc(sem("mdec_done"), 1)

                queries(0)
                for j in range(MSTEP):
                    now = it * MSTEP + (st.base + j + 1)
                    dve.wait_ge(sem("mdec_sc"), now)
                    chain(dve.tensor_copy(m_sm[0:MR, :], PS[0:MR, 4, 0:NM]))
                    if j + 1 < MSTEP:
                        queries(j + 1)
                    chain(dve.tensor_reduce(s_mx[0:MR, 1:2], m_sm[0:MR, :], AXX, ALU.max))
                    dve.tensor_scalar(s_nm[0:MR, 1:2], s_mx[0:MR, 1:2], -1.0, None, ALU.mult).then_inc(sem("mdec_nm"), 1)
                    if j:
                        output(j - 1)
                    dve.wait_ge(sem("mdec_exp"), now)
                    chain(dve.reciprocal(s_r[0:MR, 1:2], s_l[0:MR, 1:2]))
                    dve.tensor_scalar(m_p[0:MR, :], m_p[0:MR, :], s_r[0:MR, 1:2], None, ALU.mult).then_inc(sem("mdec_p"), 1)
                    dve.wait_ge(sem("mdec_turned"), now)
                    dve.tensor_copy(m_pt, PS[:, 5, 0:2 * MR]).then_inc(sem("mdec_pt"), 1)
                output(MSTEP - 1)
            chain.leave(NB // MSTEP)

        (l_xin, l_xc, l_wa, l_wi, l_par, l_sp, l_s, l_inv) = carve([LW + 3, LW, P, P, 320, 8 * 8, 8, H * LW])
        L_CONV, L_H0, L_CW, L_CB, L_BA, L_BI, L_LAM = 0, 192, 256, 288, 296, 304, 312
        l_r, l_i = (ODT[:, i * H * LW:(i + 1) * H * LW].rearrange("p (h t) -> p h t", h=H) for i in range(2))
        l_a = A[:, 5888:5888 + H * LW].rearrange("p (h t) -> p h t", h=H)

        def seqs(ap):
            return ap.rearrange("p (b t) -> p b t", t=7)

        def lru_act(act, st):
            lam = l_par[:, L_LAM:L_LAM + 8]
            act.wait_ge(tables_in, table_value["lru"])
            act.activation(l_sp[:, 0:8], lam, ACT.Abs).then_inc(sem("lru_abs"), 1)
            act.wait_ge(sem("lru_abs"), 1)
            act.activation(l_sp[:, 8:16], l_sp[:, 0:8], ACT.Exp, scale=-1.0).then_inc(sem("lru_e"), 1)
            ly = BIG[:, LY:LY + H, :]
            act.activation(ly, ly, ACT.Gelu_apprx_tanh).then_inc(sem("lru_gelu"), 1)
            table(act, ACT.Sigmoid)
            with act.Fori(0, H) as h:
                act.wait_ge(sem("lru_mm"), h + 1)
                act.activation(dyn(l_r, h, 0, LW), PS[:, 4, 0:LW], ACT.Sigmoid, bias=row(l_par, h + L_BA, 1))
                act.activation(dyn(l_i, h, 0, LW), PS[:, 5, 0:LW], ACT.Sigmoid, bias=row(l_par, h + L_BI, 1)).then_inc(sem("lru_sig"), 1)
            act.wait_ge(sem("lru_la"), 1 + H)
            act.activation(l_a[:, :, :], l_r[:, :, :], ACT.Exp).then_inc(sem("lru_exp"), 1)
            act.wait_ge(sem("lru_exp"), 1)
            act.activation(l_r[:, :, :], l_r[:, :, :], ACT.Tanh, scale=-1.0).then_inc(sem("lru_tanh"), 1)
            act.wait_ge(sem("lru_tanh"), 1)
            act.activation(l_inv, l_r[:, :, :].rearrange("p h t -> p (h t)"), ACT.Ln, bias=1.0).then_inc(sem("lru_ln"), 1)
            act.wait_ge(sem("lru_ln"), 1)
            act.activation(l_inv, l_inv, ACT.Exp, scale=-1.0).then_inc(sem("lru_inv"), 1)
            act.wait_ge(sem("lru_b2"), 1)
            act.activation(l_r[:, :, :], l_r[:, :, :], ACT.Sqrt).then_inc(sem("lru_sqrt"), 1)

        def lru_pe(pe, st):
            with pe.Fori(0, H) as h:
                pe.wait_ge(sem("lru_xc"), h + 1)
                pe.matmul(PS[:, 4, 0:LW], l_wa, l_xc, start=True, stop=True)
                pe.matmul(PS[:, 5, 0:LW], l_wi, l_xc, start=True, stop=True).then_inc(sem("lru_mm"), 1)

        def lru_dve(dve, chain, st, seg):
            dve.wait_ge(tables_in, table_value["lru"])
            dve.wait_ge(sem("lru_e"), 1)
            c = [l_sp[:, i * 8:i * 8 + 8] for i in range(8)]
            chain(dve.tensor_scalar(c[2], c[1], 2.0, None, ALU.add))
            chain(dve.reciprocal(c[3], c[2]))
            chain(dve.tensor_tensor(c[4], c[1], c[3], ALU.mult))
            chain(dve.tensor_tensor(c[5], c[4], c[4], ALU.mult))
            chain(dve.tensor_scalar(c[6], c[5], 1.0 / 17, 1.0 / 15, ALU.mult, ALU.add))
            for n in (13, 11, 9, 7, 5, 3, 1):
                chain(dve.tensor_tensor(c[6], c[6], c[5], ALU.mult))
                chain(dve.tensor_scalar(c[6], c[6], 1.0 / n, None, ALU.add))
            chain(dve.tensor_tensor(c[6], c[6], c[4], ALU.mult))
            chain(dve.tensor_scalar(c[7], l_par[:, L_LAM:L_LAM + 8], -1.0, 0.0, ALU.mult, ALU.max))
            chain(dve.scalar_tensor_tensor(out=c[7], in0=c[6], scalar=2.0, in1=c[7], op0=ALU.mult, op1=ALU.add))
            chain(dve.tensor_scalar(l_s, c[7], -8.0, None, ALU.mult))
            chain(dve.memset(l_xin[:, 0:3], 0.0))
            dve.wait_ge(ring_full[seg.slot(0)], seg.arrived(0))
            W = slot(seg, 0)
            with dve.Fori(0, H) as h:
                chain.enter(h, 4)
                dve.wait_ge(sem("lru_la"), h + 1)
                dve.tensor_copy(l_wa, row(W, h * P, P))
                dve.tensor_copy(l_wi, row(W, h * P + H * P, P))
                dve.tensor_copy(l_xin[:, 3:3 + TP], dyn(BIG, h + LX, 0, TP))
                xs = seqs(l_xin[:, 3 + TP:3 + LW])
                dve.tensor_copy(xs[:, :, 0:3], row(l_par, h * 24, 24).rearrange("p (b t) -> p b t", t=3))
                chain(dve.tensor_copy(xs[:, :, 3:7], dyn(BIG, h + LX, TP, T).rearrange("p (b t) -> p b t", t=TS)))
                chain(dve.tensor_scalar(l_xc, l_xin[:, 0:LW], row(l_par, h * 4 + L_CW, 1), row(l_par, h + L_CB, 1), ALU.mult, ALU.add))
                for j in range(1, 4):
                    ins = dve.scalar_tensor_tensor(out=l_xc, in0=l_xin[:, j:j + LW], scalar=row(l_par, h * 4 + (L_CW + j), 1), in1=l_xc,
                                                   op0=ALU.mult, op1=ALU.add)
                    if j < 3:
                        chain(ins)
                ins.then_inc(sem("lru_xc"), 1)
                dve.wait_ge(sem("lru_xc"), h + 1)
                dve.wait_ge(sem("lru_sig"), h + 1)
                dve.tensor_tensor(dyn(l_i, h, 0, LW), dyn(l_i, h, 0, LW), l_xc, ALU.mult)
                dve.tensor_scalar(dyn(l_r, h, 0, LW), dyn(l_r, h, 0, LW), row(l_s, h, 1), None, ALU.mult).then_inc(sem("lru_la"), 1)
            chain.leave(H)
            dve.wait_ge(sem("lru_inv"), 1)
            r = l_r[:, :, :].rearrange("p h t -> p (h t)")
            dve.scalar_tensor_tensor(out=r, in0=r, scalar=2.0, in1=l_inv, op0=ALU.mult, op1=ALU.mult).then_inc(sem("lru_b2"), 1)
            dve.wait_ge(sem("lru_sqrt"), 1)
            dve.wait_ge(sem("lru_gelu"), 1)
            flat = [x[:, :, :].rearrange("p h t -> p (h t)") for x in (l_a, l_i, l_r)]
            chain(dve.tensor_tensor(flat[1], flat[1], flat[2], ALU.mult))
            sa, si, sr = (x[:, :, TP:LW].rearrange("p h (b t) -> p h b t", t=7) for x in (l_a, l_i, l_r))
            dve.memset(l_a[:, :, 0:1], 0.0)
            h0 = l_par[:, L_H0:L_H0 + H * NB].rearrange("p (h b) -> p h b", h=H)
            for t in range(3):
                dve.memset(sa[:, :, :, t], 0.0)
                ins = dve.tensor_copy(si[:, :, :, t], h0)
            chain(ins)
            chain(dve.tensor_tensor_scan(flat[2], flat[0], flat[1], 0.0, ALU.mult, ALU.add))
            dve.tensor_tensor(HT[:, H:2 * H, 0:TP], l_r[:, :, 0:TP], BIG[:, LY:LY + H, 0:TP], ALU.mult)
            for b in range(NB):
                ins = dve.tensor_tensor(HT[:, H:2 * H, TP + b * TS:TP + (b + 1) * TS], sr[:, :, b, 3:7],
                                        BIG[:, LY:LY + H, TP + b * TS:TP + (b + 1) * TS], ALU.mult)
            ins.then_inc(sem("lru_done"), 1)

        N_B, N_CB, N_CM, N_WB, N_NB, N_SEL = 0, 512, 520, 528, 528 + WIN, 528 + WIN + NB * NS
        N_PWT, N_PWV, N_PVT = N_SEL + NPG * NBS, N_SEL + NPG * NBS + P, N_SEL + NPG * NBS + 2 * P
        N_END = N_PVT + BLK
        n_v = ODT[:, N_END:N_END + 4 * 384].rearrange("p (i c) -> p i c", i=4)
        n_kc = ODT[:, N_END + 1536:N_END + 1544]
        n_vt = ODT[:, N_END + 1544:N_END + 1552]
        n_vc = ODT[:, N_END + 1552:N_END + 1552 + 256]
        (n_tmp,) = carve([2 * TP])
        v_tiles = [VSL, VSL + 1, VWN, VWN + 1]

        def gate_pe(pe):
            for i, w in ((0, P), (1, P), (2, NS)):
                mm = pe.matmul(PS[0:w, 4, i * 24:(i + 1) * 24], BIG[0:24, GT, i * P:i * P + w], IDENT[0:24, 0:24], start=True, stop=True)
            mm.then_inc(sem("gate_rows"), 1)
            for i in range(4):
                for c, w in ((0, P), (1, P), (2, NS)):
                    mm = pe.matmul(PS[0:w, i, c * P:(c + 1) * P], BIG[:, v_tiles[i], c * P:c * P + w], IDENT, start=True, stop=True)
            mm.then_inc(sem("nsv_rows"), 1)
            pe.wait_ge(sem("nsc_vt"), 1)
            for g in range(G):
                mm = pe.matmul(PS[0:NBP, 5, g * P:(g + 1) * P], n_vt[:, g * NBP:(g + 1) * NBP], IDENT, start=True, stop=True)
            mm.then_inc(sem("nsc_rows"), 1)

        def gate_act(act):
            act.wait_ge(sem("gate_rows"), 1)
            g = GROW[:, :, :].rearrange("p i c -> p (i c)")
            act.activation(g[:, 0:48], PS[:, 4, 0:48], ACT.Exp, scale=-1.0)
            act.activation(g[0:NS, 48:72], PS[0:NS, 4, 48:72], ACT.Exp, scale=-1.0).then_inc(sem("gate_exp"), 1)
            act.wait_ge(sem("nsv_rows"), 1)
            act.wait_ge(sem("lru_done"), 1)
            act.wait_ge(outs_out, out_value["lru"])
            act.activation(n_v[:, :, 0:256], PS[:, 0:4, 0:256], ACT.Copy)
            act.activation(n_v[0:NS, :, 256:384], PS[0:NS, 0:4, 256:384], ACT.Copy)
            act.wait_ge(sem("nsc_rows"), 1)
            act.activation(n_vc[0:NBP, :], PS[0:NBP, 5, 0:256], ACT.Copy).then_inc(sem("nsc_done"), 1)

        def gate_dve(dve, chain):
            g = GROW[:, :, :].rearrange("p i c -> p (i c)")
            dve.wait_ge(sem("gate_exp"), 1)
            dve.tensor_scalar(g[:, 0:48], g[:, 0:48], 1.0, None, ALU.add)
            chain(dve.tensor_scalar(g[0:NS, 48:72], g[0:NS, 48:72], 1.0, None, ALU.add))
            dve.reciprocal(g[:, 0:48], g[:, 0:48])
            dve.reciprocal(g[0:NS, 48:72], g[0:NS, 48:72]).then_inc(sem("gates"), 1)
            dve.wait_ge(tables_in, table_value["nsa"])
            for n, (tile, pw, out) in enumerate(((KCM, N_PWT, n_kc), (VCM, N_PVT, n_vt))):
                w = ODT[:, pw:pw + BLK].unsqueeze(1).broadcast_to([P, NBP, BLK])
                for g_ in range(G):
                    t = n_tmp[:, g_ * TP:(g_ + 1) * TP].rearrange("p (b r) -> p b r", r=BLK)
                    chain(dve.tensor_tensor(t, BIG[:, tile + g_, 0:TP].rearrange("p (b r) -> p b r", r=BLK), w, ALU.mult))
                    ins = dve.tensor_reduce(out[:, g_ * NBP:(g_ + 1) * NBP], t, AXX, ALU.add)
                    if n == 1 and g_ == 1:
                        ins.then_inc(sem("nsc_vt"), 1)
                    else:
                        chain(ins)

        (n_q, n_sm, n_p, n_pt) = carve([T, 1032, 1032, 1280])
        n_mx, n_nm, n_l, n_r = (PMEM[:, 24 + i * 6:30 + i * 6] for i in range(4))

        def parts(buf):
            return [buf[:, (b * 2 + q) * TP:(b * 2 + q + 1) * TP] for b in range(2) for q in range(2)] + \
                   [buf[:, 1024 + q * NBP:1024 + (q + 1) * NBP] for q in range(2)]

        def nsp_act(act, g):
            h0 = g * (H // G)

            def queries(i):
                act.activation(n_q, dyn(BIG, NQ + h0 + i), ACT.Copy).then_inc(sem("nsp_q"), 1)

            def finish(i):
                act.wait_ge(sem("nsp_nm"), i + (h0 + 1))
                for k, (p, x) in enumerate(zip(parts(n_p), parts(n_sm))):
                    ins = act.activation(p, x, ACT.Exp, bias=n_nm[:, k:k + 1], accum_out=n_l[:, k:k + 1])
                ins.then_inc(sem("nsp_exp"), 1)
                act.wait_ge(sem("nsp_turned"), i + (h0 + 1))
                act.activation(n_pt[:, 0:512], PS[:, 7, 0:512], ACT.Copy)
                act.activation(n_pt[:, 512:1024], PS[:, 3, 0:512], ACT.Copy)
                act.activation(n_pt[0:NBP, 1024:1280], PS[0:NBP, 2, 0:256], ACT.Copy).then_inc(sem("nsp_pt"), 1)

            def step(i):
                act.wait_ge(sem("nsp_sc"), i + (h0 + 1))
                queries(i + 1)
                finish(i)
            act.wait_ge(sem("nsp_done"), h0 + 1)
            skewed(act, H // G, lambda: queries(0), step, finish)

        def nsp_pe(pe, g):
            h0 = g * (H // G)

            def scores(i):
                pe.wait_ge(sem("nsp_q"), i + (h0 + 1))
                for q in range(2):
                    qs = n_q[:, q * P:(q + 1) * P]
                    pe.matmul(PS[:, 4, q * TP:(q + 1) * TP], qs, BIG[:, KSL + g, 0:TP], start=True, stop=True)
                    pe.matmul(PS[:, 5, q * TP:(q + 1) * TP], qs, BIG[:, KWN + g, 0:TP], start=True, stop=True)
                    mm = pe.matmul(PS[:, 6, q * NBP:(q + 1) * NBP], qs, n_kc[:, g * NBP:(g + 1) * NBP], start=True, stop=True)
                mm.then_inc(sem("nsp_sc"), 1)

            def outputs(i):
                pe.wait_ge(sem("nsp_p"), i + (h0 + 1))
                pp = parts(n_p)
                for b, bank in ((0, 7), (1, 3)):
                    for k in range(2):
                        for q in range(2):
                            pe.transpose(PS[:, bank, k * TP + q * P:k * TP + (q + 1) * P], pp[2 * b + q][:, k * P:(k + 1) * P], IDENT)
                for q in range(2):
                    mm = pe.matmul(PS[0:NBP, 2, q * P:(q + 1) * P], pp[4 + q], IDENT, start=True, stop=True)
                mm.then_inc(sem("nsp_turned"), 1)
                pe.wait_ge(sem("nsp_done"), i + (h0 + 1))
                pe.wait_ge(sem("nsp_pt"), i + (h0 + 1))
                for b in range(2):
                    for k in range(2):
                        pe.matmul(PS[:, 1, 0:TP], n_v[:, 2 * b + g, k * P:(k + 1) * P], n_pt[:, b * 512 + k * TP:b * 512 + (k + 1) * TP],
                                  start=(b == 0 and k == 0), stop=False)
                pe.matmul(PS[:, 1, 0:TP], n_vc[0:NBP, g * P:(g + 1) * P], n_pt[0:NBP, 1024:1280], start=False, stop=True).then_inc(sem("nsp_o"), 1)

            def step(i):
                pe.wait_ge(sem("nsp_nm"), i + (h0 + 1))
                scores(i + 1)
                outputs(i)
            skewed(pe, H // G, lambda: scores(0), step, outputs)

        def nsp_dve(dve, chain, g):
            h0 = g * (H // G)

            def probabilities(i):
                dve.wait_ge(sem("nsp_sc"), i + (h0 + 1))
                dve.tensor_tensor(n_sm[:, 0:512], PS[:, 4, 0:512], ODT[:, N_B:N_B + 512], ALU.add)
                dve.tensor_tensor(n_sm[:, 512:1024], PS[:, 5, 0:512], ODT[:, N_B:N_B + 512], ALU.add)
                chain(dve.tensor_tensor(n_sm[:, 1024:1032], PS[:, 6, 0:8], ODT[:, N_CB:N_CB + 8], ALU.add))
                dve.tensor_reduce(n_mx[:, 0:4], n_sm[:, 0:1024].rearrange("p (i k) -> p i k", i=4), AXX, ALU.max)
                chain(dve.tensor_reduce(n_mx[:, 4:6], n_sm[:, 1024:1032].rearrange("p (i k) -> p i k", i=2), AXX, ALU.max))
                dve.tensor_scalar(n_nm, n_mx, -1.0, None, ALU.mult).then_inc(sem("nsp_nm"), 1)
                dve.wait_ge(sem("nsp_exp"), i + (h0 + 1))
                pc = n_p[:, 1024:1032]
                chain(dve.tensor_tensor(pc, pc, ODT[:, N_CM:N_CM + 8], ALU.mult))
                chain(dve.tensor_reduce(n_l[:, 4:6], pc.rearrange("p (q k) -> p q k", q=2), AXX, ALU.add))
                chain(dve.tensor_scalar(n_l, n_l, 1e-30, None, ALU.max))
                chain(dve.reciprocal(n_r, n_l))
                for b, c in ((0, 1), (1, 2), (2, 0)):
                    r2 = n_r[:, 2 * b:2 * b + 2].unsqueeze(2)
                    chain(dve.tensor_tensor(r2, r2, GROW[:, 0:2, bass.ds(i * 3 + (h0 * 3 + c), 1)], ALU.mult))
                for k, p in enumerate(parts(n_p)):
                    ins = dve.tensor_scalar(p, p, n_r[:, k:k + 1], None, ALU.mult)
                    if k == 0:
                        chain(ins)
                ins.then_inc(sem("nsp_p"), 1)

            def output(i):
                dve.wait_ge(sem("nsp_o"), i + (h0 + 1))
                dve.tensor_copy(dyn(HT, h0 + i, 0, TP), PS[:, 1, 0:TP]).then_inc(sem("nsp_done"), 1)

            def step(i):
                chain.enter(i, 10)
                probabilities(i + 1)
                output(i)
            skewed(dve, H // G, lambda: probabilities(0), step, lambda i: (chain.leave(i), output(i)))

        C_SN, C_W, C_WN, C_C, C_END = 1024, 1152, 1664, 1792, 1920
        GR = NS // G
        (e_qb, e_sm, e_p, e_pt, e_kc, e_vc) = carve([G * 3 * GR, C_END, C_END, 15 * NS, G * NBS, 2 * P])
        E_BR = ((0, C_SN + NS), (C_W, C_WN + NS), (C_C, C_C + NBS))

        def nsd_act(act, st):
            with act.Fori(0, NB) as b:
                act.wait_ge(sem("nsd_nm"), b + 1)
                for i, (c0, c1) in enumerate(E_BR):
                    ins = act.activation(e_p[0:NS, c0:c1], e_sm[0:NS, c0:c1], ACT.Exp, bias=s_nm[:, i:i + 1], accum_out=s_l[:, i:i + 1])
                ins.then_inc(sem("nsd_exp"), 1)

        def nsd_pe(pe):
            def scores(b, seg, r):
                pe.wait_ge(sem("nsd_prod"), b + 1)
                pe.sem_inc(ring_used, 1)
                VC = slot(seg, 1).rearrange("p (i c) -> p i c", i=NPG)
                for i in range(NPG):
                    mm = pe.matmul(PS[0:NBS, 3, 0:256], ODT[:, N_SEL + i * NBS:N_SEL + (i + 1) * NBS], VC[:, i, :], start=(i == 0), stop=(i == NPG - 1))
                mm.then_inc(ring_used, 1)
                for half in range(2):
                    pe.wait_ge(ring_full[seg.slot(2 + half)], seg.arrived(2 + half, r))
                    KS = slot(seg, 2 + half)[:, 0:1024].rearrange("p (i g r) -> p g i r", i=4, g=G)
                    for g in range(G):
                        mm = pe.matmul(PS[0:NS, 4 + half, 0:512].rearrange("p (i r) -> p i r", i=4), e_qb[:, g * NS:(g + 1) * NS], KS[:, g],
                                       start=(g == 0), stop=(g == G - 1))
                    mm.then_inc(ring_used, 1)
                pe.wait_ge(ring_full[seg.slot(4)], seg.arrived(4, r))
                KW = slot(seg, 4)[:, 0:1024].rearrange("p (g k) -> p g k", g=G)
                for g in range(G):
                    q = e_qb[:, g * NS:(g + 1) * NS]
                    f, l = g == 0, g == G - 1
                    pe.matmul(PS[0:NS, 7, 0:NS], q, BIG[:, KSL + g, TP:T], start=f, stop=True, skip_group_check=True)
                    pe.matmul(PS[0:NS, 7, NS:2 * NS], q, BIG[:, KWN + g, TP:T], start=False, stop=True, skip_group_check=True)
                    pe.matmul(PS[0:NS, 7, 2 * NS:2 * NS + NBS], q, e_kc[:, g * NBS:(g + 1) * NBS], start=False, stop=True, skip_group_check=True)
                    mm = pe.matmul(PS[0:NS, 6, 0:512], q, KW[:, g, :], start=f, stop=l)
                mm.then_inc(ring_used, 1)

            def outputs(b, seg, r, j0):
                pe.wait_ge(sem("nsd_p"), b + 1)
                for i in range(15):
                    mm = pe.matmul(PS[:, 2, i * NS:(i + 1) * NS], e_p[0:NS, i * P:(i + 1) * P], IDENT[0:NS, 0:NS], start=True, stop=True)
                mm.then_inc(sem("nsd_turned"), 1)
                pe.wait_ge(sem("nsd_pt"), b + 1)

                def out(g):
                    return PS[:, 1, g * GR:(g + 1) * GR]

                def pt(i, g, n=P):
                    return e_pt[0:n, i * NS + g * GR:i * NS + (g + 1) * GR]
                for half in range(2):
                    j = j0 + half
                    pe.wait_ge(ring_full[seg.slot(j)], seg.arrived(j, r))
                    VS = slot(seg, j)[:, 0:1024].rearrange("p (i g d) -> p i g d", i=4, g=G)
                    for g in range(G):
                        for i in range(4):
                            mm = pe.matmul(out(g), VS[:, i, g, :], pt(4 * half + i, g), start=(half == 0 and g == 0 and i == 0), stop=True,
                                           skip_group_check=True)
                    mm.then_inc(ring_used, 1)
                j = j0 + 2
                pe.wait_ge(ring_full[seg.slot(j)], seg.arrived(j, r))
                VW_ = slot(seg, j)[:, 0:1024].rearrange("p (i g d) -> p i g d", i=4, g=G)
                for g in range(G):
                    pe.matmul(out(g), n_v[0:NS, g, 256:384], pt(8, g, NS), start=False, stop=True, skip_group_check=True)
                    pe.matmul(out(g), n_v[0:NS, 2 + g, 256:384], pt(13, g, NS), start=False, stop=True, skip_group_check=True)
                    pe.matmul(out(g), e_vc[0:NBS, g * P:(g + 1) * P], pt(14, g, NBS), start=False, stop=True, skip_group_check=True)
                    for i in range(4):
                        mm = pe.matmul(out(g), VW_[:, i, g, :], pt(9 + i, g), start=False, stop=True, skip_group_check=True)
                mm.then_inc(ring_used, 1)

            def step(b):
                scores(b + 1, od.nsd_seg, b)
                outputs(b, od.nsd_seg, b, 5)
            skewed(pe, NB, lambda: scores(0, od.nsd_first, 0), step, lambda b: outputs(b, od.nsd_last, 0, 0))

        def nsd_dve(dve, chain):
            first, seg, last = od.nsd_first, od.nsd_seg, od.nsd_last
            chain(dve.memset(e_qb, 0.0))
            dve.memset(e_p, 0.0)
            chain(dve.memset(e_sm, 0.0))

            def compress(b, seg, r):
                dve.tensor_copy(diag(e_qb, G, GR).rearrange("p g (h t) -> p g h t", t=TS),
                                BIG[:, NQ:NQ + H, bass.ds(b * TS + TP, TS)].rearrange("p (g h) t -> p g h t", g=G))
                dve.wait_ge(ring_full[seg.slot(0)], seg.arrived(0, r))
                S = slot(seg, 0)
                KC = S.rearrange("p (i r) -> p i r", r=P)
                chain(dve.tensor_tensor(KC, KC, ODT[:, N_PWT:N_PWT + P].unsqueeze(1).broadcast_to([P, 16, P]), ALU.mult))
                for g in range(G):
                    chain(dve.tensor_reduce(e_kc[:, g * NBS:(g + 1) * NBS].rearrange("p (i x) -> p i x", x=2),
                                            S.rearrange("p (i g x r) -> p g i x r", i=NPG, g=G, r=BLK)[:, g], AXX, ALU.add))
                dve.wait_ge(ring_full[seg.slot(1)], seg.arrived(1, r))
                VC = slot(seg, 1).rearrange("p (i r) -> p i r", r=P)
                return dve.tensor_tensor(VC, VC, ODT[:, N_PWV:N_PWV + P].unsqueeze(1).broadcast_to([P, 16, P]), ALU.mult)

            def biased(b, scored):
                dve.wait_ge(ring_used, scored)
                dve.tensor_copy(e_sm[0:NS, 0:1024], PS[0:NS, 4:6, :].rearrange("p a c -> p (a c)"))
                dve.tensor_tensor(e_sm[0:NS, C_W:C_W + WIN], PS[0:NS, 6, 0:WIN], ODT[0:NS, N_WB:N_WB + WIN], ALU.add)
                nb = ODT[0:NS, bass.ds(b * NS + N_NB, NS)]
                dve.tensor_tensor(e_sm[0:NS, C_SN:C_SN + NS], PS[0:NS, 7, 0:NS], nb, ALU.add)
                dve.tensor_tensor(e_sm[0:NS, C_WN:C_WN + NS], PS[0:NS, 7, NS:2 * NS], nb, ALU.add)
                chain(dve.tensor_copy(e_sm[0:NS, C_C:C_C + NBS], PS[0:NS, 7, 2 * NS:2 * NS + NBS]))

            def values():
                return dve.tensor_copy(e_vc[0:NBS, :], PS[0:NBS, 3, 0:256])

            def probabilities(b):
                for i, (c0, c1) in enumerate(E_BR):
                    ins = dve.tensor_reduce(s_mx[:, i:i + 1], e_sm[0:NS, c0:c1], AXX, ALU.max)
                chain(ins)
                dve.tensor_scalar(s_nm[:, 0:3], s_mx[:, 0:3], -1.0, None, ALU.mult).then_inc(sem("nsd_nm"), 1)
                dve.wait_ge(sem("nsd_exp"), b + 1)
                chain(dve.reciprocal(s_r[:, 0:3], s_l[:, 0:3]))
                chain(dve.tensor_tensor(s_r[:, 0:2], s_r[:, 0:2], GDEC[:, bass.ds(b * 3 + 1, 2)], ALU.mult))
                chain(dve.tensor_tensor(s_r[:, 2:3], s_r[:, 2:3], GDEC[:, bass.ds(b * 3, 1)], ALU.mult))
                for i, (c0, c1) in enumerate(E_BR):
                    ins = dve.tensor_scalar(e_p[0:NS, c0:c1], e_p[0:NS, c0:c1], s_r[:, i:i + 1], None, ALU.mult)
                ins.then_inc(sem("nsd_p"), 1)
                dve.wait_ge(sem("nsd_turned"), b + 1)
                dve.tensor_copy(e_pt, PS[:, 2, 0:15 * NS]).then_inc(sem("nsd_pt"), 1)

            def output(b, multiplied):
                dve.wait_ge(ring_used, multiplied)
                dve.tensor_copy(HT[:, 0:H, bass.ds(b * TS + TP, TS)],
                                PS[:, 1, 0:NS].rearrange("p (h t) -> p h t", h=H)).then_inc(sem("nsd_done"), 1)

            compress(0, first, 0).then_inc(sem("nsd_prod"), 1)
            biased(0, first.used(4))
            compress(1, seg, 0)
            values().then_inc(sem("nsd_prod"), 1)
            probabilities(0)
            with dve.Fori(0, NB - 2) as b:
                chain.enter(b, 8)
                biased(b + 1, seg.used(4, b))
                compress(b + 2, seg, b + 1)
                output(b, seg.used(7, b))
                values().then_inc(sem("nsd_prod"), 1)
                probabilities(b + 1)
            chain.leave(NB - 2)
            biased(NB - 1, seg.used(4, NB - 2))
            output(NB - 2, seg.used(7, NB - 2))
            values()
            probabilities(NB - 1)
            output(NB - 1, last.used(2))

        def after_ret(eng):
            eng.wait_ge(sem("ret_done"), 1 + H)
            eng.wait_ge(sem("ret_saved"), 32 + 32 * H)

        def after_nsp(eng):
            eng.wait_ge(sem("nsp_done"), 1 + H)

        block = ctx.enter_context(nc.Block())

        @block.sync
        def _(sp):
            for dst, name in ((X[:, :, :], "x"), (CORE[:, :], "core"), (GAIN[:, :], "gain"), (SCL[:, :], "scl"), (PT[:, :], "pages")):
                sp.dma_start(dst, a[name]).then_inc(consts_in, 16)

            def fill(seg, loads):
                def unit(j, it):
                    copies = loads(j, it)
                    sp.wait_ge(ring_used, seg.may_fill(j, it))
                    for dst, src in copies:
                        sp.dma_start(dst, src).then_inc(ring_full[seg.slot(j)], 16)
                whole = seg.units // seg.round
                if whole > 1:
                    with sp.Fori(0, whole) as it:
                        for j in range(seg.round):
                            unit(j, it)
                for j in range(seg.round * whole if whole > 1 else 0, seg.units):
                    unit(j, 0)

            def one(ap, i):
                return ap[bass.ds(i, 1)].rearrange("o p n -> (o p) n")

            def weights(w, name):
                n = w.kt * P
                fill(w.seg, lambda j, it: [(slot(w.seg, j)[:, 0:n], a[name][j] if isinstance(it, int) else one(a[name], it * SLOTS + j))])

            for s in layers:
                layer = layers.index(s)
                if layer == 0:
                    weights(s.w_in, "ev_w_in")

                    def dil_loads(seg, j, k, b):
                        n, src, x = (2 * NKD, "dil_k", k) if b is None or (k is not None and j < 4) else (5 * 256, "dil_v", b)
                        return [(slot(seg, j)[:, 0:n], one(a[src], x * 4 + j % 4))]
                    fill(s.dil_first, lambda j, it: dil_loads(s.dil_first, j, 0, None))
                    fill(s.dil_seg, lambda j, b: dil_loads(s.dil_seg, j, b + 1, b))
                    fill(s.dil_last, lambda j, it: dil_loads(s.dil_last, j, None, NB - 1))
                else:
                    weights(s.w_in, "od_w_in")
                    fill(s.lru_seg, lambda j, it: [(slot(s.lru_seg, 0), a["lru_w"])])
                    sp.wait_ge(consts_in, 80)
                    pages = []

                    def nsd_loads(seg, j, kind, b):
                        S = slot(seg, j)
                        if kind in (4, 7):
                            return [(S[:, 0:1024], one(a["win_k" if kind == 4 else "win_v"], b))]
                        if kind in (0, 5):
                            pages[:] = [sp.value_load(PT[0:1, bass.ds(b * NPG + i, 1)], min_val=0, max_val=a["cmp_k"].shape[0] - 1)
                                        for i in range(NPG)]
                        name, mine = {0: ("cmp_k", pages), 1: ("cmp_v", pages), 2: ("slc_k", pages[:4]), 3: ("slc_k", pages[4:]),
                                      5: ("slc_v", pages[:4]), 6: ("slc_v", pages[4:])}[kind]
                        return [(S[:, i * 256:(i + 1) * 256], one(a[name], page)) for i, page in enumerate(mine)]
                    fill(s.nsd_first, lambda j, it: nsd_loads(s.nsd_first, j, j, 0))
                    fill(s.nsd_seg, lambda j, b: nsd_loads(s.nsd_seg, j, j, b + 1 if j < 5 else b))
                    fill(s.nsd_last, lambda j, it: nsd_loads(s.nsd_last, j, 5 + j, NB - 1))
                weights(s.w_out, f"w_out{layer}")
                weights(s.w_kv, f"mem_w_kv{layer}")
                weights(s.w_q, f"mem_w_q{layer}")
                mseg = s.mdec_seg

                def mem_loads(j, it):
                    b = it * MSTEP + (layer * NB + j)
                    return [(slot(mseg, j)[:, 0:1024], one(a["mem_k"], b)), (slot(mseg, j)[:, 1024:2048], one(a["mem_v"], b))]
                fill(mseg, mem_loads)
                weights(s.w_o, f"mem_w_o{layer}")
                weights(s.mlp, f"mlp{layer}")

        @block.gpsimd
        def _(pool):
            after_tiles(pool, ev.w_in)
            pool.dma_start(EVT[:, 0:R_END], a["ret_tab"]).then_inc(tables_in, 16)
            pool.wait_ge(sem("gn_done"), 1)
            pool.dma_start(EVT[:, 0:D_BN + NB * NS], a["dil_tab"]).then_inc(tables_in, 16)
            pool.dma_start(MX, a["mem_x"]).then_inc(mem_in, 16)
            after_prep(pool, ev.prep[-1][0])
            pool.dma_start(o["dil_kv"], BIG[:, DK:DK + 2 * H, :]).then_inc(outs_out, 16)
            after_prep(pool, ev.prep_k[0])
            pool.dma_start(o["mem_kv0"], BIG[:, 0:2 * HM, 0:NM]).then_inc(outs_out, 16)
            after_tiles(pool, od.w_in)
            pool.dma_start(l_par, a["lru_par"]).then_inc(tables_in, 16)
            pool.dma_start(o["lx"], BIG[:, LX:LX + H, :]).then_inc(outs_out, 16)
            pool.wait_ge(sem("lru_done"), 1)
            pool.dma_start(o["lru_h"], l_r[:, :, :]).then_inc(outs_out, 16)
            pool.wait_ge(outs_out, out_value["lru"])
            pool.dma_start(ODT[:, 0:N_PWT], a["nsa_tab"]).then_inc(tables_in, 16)
            pool.dma_start(ODT[:, N_PWT:N_END], a["pw"]).then_inc(tables_in, 16)
            pool.wait_ge(sem("gates"), 1)
            pool.dma_start(scratch, GROW[0:NS, 2, :]).then_inc(sem("gates_out"), 16)
            pool.wait_ge(sem("gates_out"), 16)
            for h in range(H):
                pool.dma_start(GDEC[h * TS:(h + 1) * TS, :].rearrange("t (b j) -> t b j", j=3),
                               scratch.rearrange("(b t) c -> t b c", t=TS)[:, :, 3 * h:3 * h + 3]).then_inc(sem("gates_in"), 16)
            after_prep(pool, od.prep[-1][0])
            pool.dma_start(o["nsa_kv"], BIG[:, KCM:KCM + 12, :]).then_inc(outs_out, 16)
            pool.wait_ge(sem("nsd_done"), NB)
            pool.wait_ge(outs_out, out_value["nsa"])
            pool.dma_start(MX, a["mem_x"]).then_inc(mem_in, 16)
            after_prep(pool, od.prep_k[0])
            pool.dma_start(o["mem_kv1"], BIG[:, 0:2 * HM, 0:NM]).then_inc(outs_out, 16)
            after_tiles(pool, od.mlp)
            pool.dma_start(o["y"], X[:, :, :]).then_inc(outs_out, 16)
            pool.wait_ge(outs_out, 112)

        @block.tensor
        def _(pe):
            for name in ("ring_used", "w_used", "tile_free"):
                pe.sem_inc(sem(name), 4)
            pe.sem_inc(hid_hi, 2)
            pe.sem_inc(sq_in, 1)
            pe.sem_inc(acc_in, 4)
            pe.sem_inc(sem("ret_saved"), 32)
            pe.wait_ge(consts_in, 80)
            groups = Groups()
            for s in layers:
                layer = layers.index(s)
                norm_pe(pe, s.n_mix, T)
                lin_pe(pe, s.w_in, groups(4))
                after_tiles(pe, s.w_in)
                if layer == 0:
                    ret_pe(pe, s.ret)
                    after_ret(pe)
                    gn_pe(pe)
                    pe.wait_ge(sem("gn_done"), 1)
                    prep_pe(pe, s.prep, T, True)
                    after_prep(pe, s.prep[-1][0])
                    att_pe(pe, s.att, DK, True)
                    after_att(pe, s.att)
                    dil_pe(pe)
                    pe.wait_ge(sem("dil_done"), NB)
                else:
                    lru_pe(pe, s.lru)
                    pe.wait_ge(sem("lru_done"), 1)
                    pe.sem_inc(ring_used, 1)
                    prep_pe(pe, s.prep, T, True)
                    after_prep(pe, s.prep[-1][0])
                    gate_pe(pe)
                    pe.wait_ge(sem("nsc_done"), 1)
                    for g in range(G):
                        nsp_pe(pe, g)
                    after_nsp(pe)
                    nsd_pe(pe)
                    pe.wait_ge(sem("nsd_done"), NB)
                lin_pe(pe, s.w_out, groups(4))
                norm_pe(pe, s.n_kv, NM)
                lin_pe(pe, s.w_kv, groups(4), NM)
                after_tiles(pe, s.w_kv)
                prep_pe(pe, [s.prep_k], NM, False)
                after_prep(pe, s.prep_k[0])
                norm_pe(pe, s.n_mem, T)
                lin_pe(pe, s.w_q, groups(4))
                after_tiles(pe, s.w_q)
                prep_pe(pe, [s.prep_q], T, False)
                after_prep(pe, s.prep_q[0])
                att_pe(pe, s.matt, MK, False)
                after_att(pe, s.matt)
                mdec_pe(pe, s.mdec, s.mdec_seg)
                pe.wait_ge(sem("mdec_done"), s.mdec.end)
                lin_pe(pe, s.w_o, groups(1))
                norm_pe(pe, s.n_mlp, T)
                mlp_pe(pe, s.mlp, layer, groups(4))

        @block.scalar
        def _(act):
            act.wait_ge(consts_in, 80)
            groups = Groups()
            for s in layers:
                layer = layers.index(s)
                norm_act(act, s.n_mix, X, T, groups(4), s.w_in)
                lin_act(act, s.w_in)
                after_tiles(act, s.w_in)
                if layer == 0:
                    ret_act(act, s.ret)
                    after_ret(act)
                    gn_act(act)
                    act.wait_ge(sem("gn_done"), 1)
                    prep_act(act, s.prep, T)
                    after_prep(act, s.prep[-1][0])
                    att_act(act, s.att, DQ, DV, True)
                    after_att(act, s.att)
                    dil_act(act, s.dil)
                    act.wait_ge(sem("dil_done"), NB)
                else:
                    lru_act(act, s.lru)
                    act.wait_ge(sem("lru_done"), 1)
                    prep_act(act, s.prep, T)
                    after_prep(act, s.prep[-1][0])
                    gate_act(act)
                    for g in range(G):
                        nsp_act(act, g)
                    after_nsp(act)
                    nsd_act(act, s.nsd)
                    act.wait_ge(sem("nsd_done"), NB)
                split_act(act, groups(4), T)
                weights_ahead(act, s.w_out, weights_act)
                act.wait_ge(outs_out, out_value["nsa" if layer else "dil"])
                lin_act(act, s.w_out, s.n_mem)
                after_tiles(act, s.w_out)
                act.wait_ge(mem_in, 16 * (layer + 1))
                norm_act(act, s.n_kv, MX, NM, groups(4), s.w_kv)
                lin_act(act, s.w_kv)
                after_tiles(act, s.w_kv)
                prep_act(act, [s.prep_k], NM)
                after_prep(act, s.prep_k[0])
                norm_act(act, s.n_mem, X, T, groups(4), s.w_q)
                lin_act(act, s.w_q)
                after_tiles(act, s.w_q)
                prep_act(act, [s.prep_q], T)
                after_prep(act, s.prep_q[0])
                att_act(act, s.matt, MQ, MV, False)
                after_att(act, s.matt)
                mdec_act(act, s.mdec)
                act.wait_ge(sem("mdec_done"), s.mdec.end)
                split_act(act, groups(1), T)
                weights_ahead(act, s.w_o, weights_act)
                lin_act(act, s.w_o, s.n_mlp)
                after_tiles(act, s.w_o)
                norm_act(act, s.n_mlp, X, T, groups(4), s.mlp)
                act.wait_ge(outs_out, out_value[f"mem{layer}"])
                mlp_act(act, s.mlp, layer, None if layer else od.n_mix)
                after_tiles(act, s.mlp)

        @block.vector
        def _(dve):
            chain = Chain(dve, sem("dve_chain"))
            for name in ("ret_done", "att_done", "nsp_done", "lru_la"):
                dve.sem_inc(sem(name), 1)
            dve.wait_ge(consts_in, 80)
            gains = GAIN[:, G_EV:G_EV + S_END]
            chain(dve.tensor_tensor(gains, gains, SCL[:, 0:S_END], ALU.mult))
            groups = Groups()
            for s in layers:
                layer = layers.index(s)
                norm_dve(dve, s.n_mix, X, GN_MIX + KT * layer, T, groups(4), s.w_in)
                lin_dve(dve, s.w_in, s.n_mix)
                after_tiles(dve, s.w_in)
                if layer == 0:
                    ret_dve(dve, chain, s.ret)
                    after_ret(dve)
                    gn_dve(dve, chain)
                    dve.wait_ge(sem("gn_done"), 1)
                    prep_dve(dve, chain, s.prep, 3 * layer, T, True)
                    after_prep(dve, s.prep[-1][0])
                    dve.wait_ge(tables_in, table_value["dil"])
                    att_dve(dve, chain, s.att, EVT[:, D_B:D_B + 512], H)
                    after_att(dve, s.att)
                    dil_dve(dve, chain)
                else:
                    lru_dve(dve, chain, s.lru, s.lru_seg)
                    dve.wait_ge(sem("lru_done"), 1)
                    prep_dve(dve, chain, s.prep, 3 * layer, T, True)
                    after_prep(dve, s.prep[-1][0])
                    gate_dve(dve, chain)
                    dve.wait_ge(sem("nsc_done"), 1)
                    for g in range(G):
                        nsp_dve(dve, chain, g)
                    after_nsp(dve)
                    dve.wait_ge(sem("gates_in"), 16 * H)
                    nsd_dve(dve, chain)
                split_dve(dve, groups(4), T)
                weights_ahead(dve, s.w_out, weights_dve)
                dve.wait_ge(outs_out, out_value["nsa" if layer else "dil"])
                lin_dve(dve, s.w_out, gather=s.n_mem)
                dve.wait_ge(mem_in, 16 * (layer + 1))
                norm_dve(dve, s.n_kv, MX, GN_KV + KT * layer, NM, groups(4), s.w_kv)
                lin_dve(dve, s.w_kv, s.n_kv, 0, NM)
                after_tiles(dve, s.w_kv)
                prep_dve(dve, chain, [s.prep_k], 3 * layer + 1, NM, False)
                norm_dve(dve, s.n_mem, X, GN_MEM + KT * layer, T, groups(4), s.w_q)
                lin_dve(dve, s.w_q, s.n_mem, MQ)
                after_tiles(dve, s.w_q)
                prep_dve(dve, chain, [s.prep_q], 3 * layer + 2, T, False)
                after_prep(dve, s.prep_q[0])
                att_dve(dve, chain, s.matt, None, 0)
                after_att(dve, s.matt)
                mdec_dve(dve, chain, s.mdec, s.mdec_seg)
                split_dve(dve, groups(1), T)
                weights_ahead(dve, s.w_o, weights_dve)
                lin_dve(dve, s.w_o, gather=s.n_mlp)
                norm_dve(dve, s.n_mlp, X, GN_MLP + KT * layer, T, groups(4), s.mlp)
                dve.wait_ge(outs_out, out_value[f"mem{layer}"])
                mlp_dve(dve, s.mlp, layer, s.n_mlp, None if layer else od.n_mix)


def tiles(w):
    k, n = w.shape
    return w.reshape(k // P, P, n // P, P).transpose(2, 1, 0, 3).reshape(n // P, P, -1)


def columns(v):
    return v.reshape(-1, P).T


def layout(i):
    xs = np.concatenate([i["x_prompt"][0], i["x_sample"].reshape(NS, D)], 0)
    w_od = i["od_w_in"][0]
    nq = H * HD + 6 * G * HD
    rows = dilated_rows()
    kd = i["cache_dil_k"][0][:, rows].reshape(NB, NKD, 4, 2, HD).transpose(0, 2, 4, 3, 1)
    vd = i["cache_dil_v"][0][:, rows].reshape(NB, NKD // P, P, 4, 2, HD).transpose(0, 3, 2, 1, 4, 5)
    pool_k = lambda c: c[0].transpose(0, 3, 2, 1).reshape(-1, P, G * PAGE)
    pool_v = lambda c: c[0].reshape(-1, P, G * HD)
    gains = [columns(g) for name in ("norm_mix_g", "norm_mem_g", "norm_mlp_g", "mem_norm_g") for g in i[name]]
    rep = lambda v, n: np.repeat(v.reshape(P, 1), n, 1)
    kg = i["nsa_k_norm_g"][0]
    gains += [rep(i["dil_q_norm_g"][0], H), rep(i["dil_k_norm_g"][0], H), rep(i["nsa_q_norm_g"][0], H), rep(kg[0], G), rep(kg[1], G),
              rep(kg[2], G), rep(i["mem_q_norm_g"][0], HM), rep(i["mem_q_norm_g"][1], HM), rep(i["mem_k_norm_g"][0], HM),
              rep(i["mem_k_norm_g"][1], HM), columns(i["ret_gn_g"][0].reshape(-1))]
    pwk, pwv = i["nsa_pw_k"][0], i["nsa_pw_v"][0]
    par = [i["state_lru_conv"][0].reshape(NB, 3, H, P).transpose(3, 2, 0, 1).reshape(P, -1),
           i["state_lru_h"][0].reshape(NB, H, P).transpose(2, 1, 0).reshape(P, -1),
           i["lru_conv_w"][0].reshape(4, H, P).transpose(2, 1, 0).reshape(P, -1)]
    par += [columns(i[n][0]) for n in ("lru_conv_b", "lru_b_a", "lru_b_i", "lru_lambda")]
    out = {
        "x": xs.reshape(T, KT, P).transpose(2, 1, 0),
        "core": core_table(), "scl": scales_table(), "gain": np.concatenate(gains, 1),
        "pages": i["page_table"].reshape(1, -1),
        "ret_tab": retention_table(), "dil_tab": dilated_table(), "nsa_tab": sparse_table(),
        "pw": np.concatenate([pwk.T, pwk.T, np.concatenate([pwv, pwv], 0), pwv.T], 1),
        "lru_par": np.concatenate(par, 1),
        "lru_w": np.concatenate([i[n][0].transpose(1, 0, 2).reshape(P, -1) for n in ("lru_w_a", "lru_w_i")], 1),
        "state_ret": i["state_ret"][0].transpose(1, 2, 0, 3).reshape(H, P, -1),
        "dil_k": kd.reshape(4 * NB, P, -1), "dil_v": vd.reshape(4 * NB, P, -1),
        "cmp_k": pool_k(i["cache_nsa_cmp_k"]), "cmp_v": pool_v(i["cache_nsa_cmp_v"]),
        "slc_k": pool_k(i["cache_nsa_slc_k"]), "slc_v": pool_v(i["cache_nsa_slc_v"]),
        "win_k": i["cache_nsa_win_k"][0].transpose(0, 3, 2, 1).reshape(NB, P, -1),
        "win_v": i["cache_nsa_win_v"][0].reshape(NB, 4, P, G * HD).transpose(0, 2, 1, 3).reshape(NB, P, -1),
        "mem_k": i["cache_mem_k"].transpose(0, 1, 4, 3, 2).reshape(2 * NB, P, -1),
        "mem_v": i["cache_mem_v"].reshape(2 * NB, 2, P, HM * HD).transpose(0, 2, 1, 3).reshape(2 * NB, P, -1),
        "mem_x": i["mem_prompt"][0].reshape(NM, KT, P).transpose(2, 1, 0),
        "ev_w_in": tiles(i["ev_w_in"][0]),
        "od_w_in": tiles(np.pad(np.concatenate([w_od[:, :nq], w_od[:, nq + 3 * H:], w_od[:, nq:nq + 3 * H]], 1), ((0, 0), (0, P - 3 * H)))),
        "w_out0": tiles(i["ev_w_out"][0]), "w_out1": tiles(i["od_w_out"][0]),
    }
    for l in range(2):
        out[f"mem_w_kv{l}"] = np.concatenate([tiles(i["mem_w_k"][l]), tiles(i["mem_w_v"][l])], 0)
        out[f"mem_w_q{l}"] = tiles(i["mem_w_q"][l])
        out[f"mem_w_o{l}"] = tiles(i["mem_w_o"][l])
        w1 = tiles(i["mlp_w1"][l]).reshape(4, KT, P, SLOT)
        w2 = np.stack([tiles(q) for q in np.split(i["mlp_w2"][l], 4, 0)])
        out[f"mlp{l}"] = np.concatenate([w1, w2], 1).reshape(-1, P, SLOT)
    return {n: np.ascontiguousarray(v) for n, v in out.items()}


_OUTS = {"y": (P, KT, T), "ret_s": (H, P, NB * P), "ret_p": (H, P, P), "dil_kv": (P, 2 * H, T), "nsa_kv": (P, 12, T), "lx": (P, H, T),
         "lru_h": (P, H, LW), "mem_kv0": (P, 2 * HM, NM), "mem_kv1": (P, 2 * HM, NM)}


def kernel(**inputs):
    import concourse.bacc as bacc
    from concourse.bass_utils import run_bass_kernel_spmd

    nc = bacc.Bacc("TRN2", target_bir_lowering=False, num_devices=1)
    arrays = {f"in_{n}": v for n, v in layout({k: np.asarray(v) for k, v in inputs.items()}).items()}
    a = {n[3:]: nc.dram_tensor(n, v.shape, mybir.dt.from_np(v.dtype), kind="ExternalInput").ap() for n, v in arrays.items()}
    o = {n: nc.dram_tensor(f"out_{n}", s, F32, kind="ExternalOutput").ap() for n, s in _OUTS.items()}
    scratch = nc.dram_tensor("gate_scratch", (NS, 3 * H), F32).ap()
    build(nc, a, o, scratch)
    r = run_bass_kernel_spmd(nc, [arrays], core_ids=[0]).results[0]
    r = {n: np.asarray(r[f"out_{n}"]) for n in _OUTS}

    def heads(x, first, n, cols, lead):
        return np.ascontiguousarray(x[:, first:first + n, cols].transpose(2, 1, 0)).reshape(lead + (n, P))

    prompt, sample = slice(0, TP), slice(TP, T)
    y = r["y"].transpose(2, 1, 0).reshape(T, D)
    out = [y[:TP].reshape(1, TP, D), y[TP:].reshape(NB, TS, D),
           r["ret_p"].reshape(1, 1, H, P, P), r["ret_s"].reshape(H, P, NB, P).transpose(2, 0, 1, 3)[None]]
    for cols, lead in ((prompt, (1, 1, TP)), (sample, (1, NB, TS))):
        out += [heads(r["dil_kv"], 0, H, cols, lead), heads(r["dil_kv"], H, H, cols, lead)]
    for first in (0, 4, 8):
        for cols, lead in ((prompt, (1, 1, TP)), (sample, (1, NB, TS))):
            out += [heads(r["nsa_kv"], first, G, cols, lead), heads(r["nsa_kv"], first + G, G, cols, lead)]
    h = r["lru_h"]
    out += [h[:, :, TP - 1].T.reshape(1, 1, -1), h[:, :, TP:].reshape(P, H, NB, 7)[..., 6].transpose(2, 1, 0).reshape(1, NB, -1)]
    lx = r["lx"]
    out += [lx[:, :, TP - 3:TP].transpose(2, 1, 0).reshape(1, 1, 3, -1),
            lx[:, :, TP:].reshape(P, H, NB, TS)[..., 1:].transpose(2, 3, 1, 0).reshape(1, NB, 3, -1)]
    mem = [r["mem_kv0"], r["mem_kv1"]]
    out += [np.stack([heads(m, f, HM, slice(0, NM), (1, NM)) for m in mem]) for f in (0, HM)]
    return tuple(np.ascontiguousarray(v) for v in out)
```
